# Optimizing a Trainium2 kernel written in Bass

```python
import math
import jax, jax.numpy as jnp
from jax import lax
import numpy as np

D_MODEL = 1024
BATCH = 1
SEQ = 128
DEPTH = 1
DEC_BATCH = 1
DEC_SEQ = 256
PAST_LEN = 128

GRID_W = 64
N_HEADS = 8
Q_LORA = 512
KV_LORA = 256
QK_NOPE = 64
QK_ROPE = 32
V_HEAD = 64
QK_HEAD = QK_NOPE + QK_ROPE
ATTN_SCALE = QK_HEAD ** -0.5
ROPE_BASE = 10000.0
Q_BLOCK = 128
FN_GROUPS = 4
FN_GROUP_W = 128
FN_WIDTH = FN_GROUPS * FN_GROUP_W
N_GROUPS = 4
EXPERTS_PER_GROUP = 4
N_EXPERTS = N_GROUPS * EXPERTS_PER_GROUP
TOP_K_EXPERTS = 2
D_EXPERT = 512
EPS = 1e-6
IN_WIDTH = Q_LORA + KV_LORA + QK_ROPE + FN_WIDTH + 2 * D_MODEL
IN_OFFSETS = (Q_LORA, Q_LORA + KV_LORA, Q_LORA + KV_LORA + QK_ROPE, Q_LORA + KV_LORA + QK_ROPE + FN_WIDTH, Q_LORA + KV_LORA + QK_ROPE + FN_WIDTH + D_MODEL)

kernel_name = "hybrid_mla_fnet_hmoe_diffusion_step"

def rmsnorm(x, g):
    xf = x.astype(jnp.float32)
    y = xf * lax.rsqrt(jnp.mean(xf * xf, axis=-1, keepdims=True) + EPS)
    return (y * g).astype(x.dtype)

def adaln(cond, w_mod, b_mod):
    m = jax.nn.silu(cond) @ w_mod + b_mod
    return jnp.split(m[:, None, :], 6, axis=-1)

def modulate(x, g, shift, scale):
    return rmsnorm(x, g) * (1 + scale) + shift

def rope_axis(x, pos):
    half = x.shape[-1] // 2
    freqs = ROPE_BASE ** (-jnp.arange(half, dtype=jnp.float32) / half)
    ang = pos.astype(jnp.float32)[:, None] * freqs[None, :]
    cos = jnp.cos(ang)[None, :, None, :]
    sin = jnp.sin(ang)[None, :, None, :]
    x1 = x[..., :half].astype(jnp.float32)
    x2 = x[..., half:].astype(jnp.float32)
    return jnp.concatenate([x1 * cos - x2 * sin, x1 * sin + x2 * cos], axis=-1).astype(x.dtype)

def rope_2d(x):
    n = x.shape[1]
    rows = n // GRID_W
    row = jnp.repeat(jnp.arange(rows), GRID_W)
    col = jnp.tile(jnp.arange(GRID_W), rows)
    half = QK_ROPE // 2
    x_nope = x[..., :QK_NOPE]
    x_row = x[..., QK_NOPE:QK_NOPE + half]
    x_col = x[..., QK_NOPE + half:]
    return jnp.concatenate([x_nope, rope_axis(x_row, row), rope_axis(x_col, col)], axis=-1)

def mixer_inputs(x, shift, scale, norm_g, w_in):
    h = modulate(x, norm_g, shift, scale)
    return jnp.split(h @ w_in, list(IN_OFFSETS), axis=-1)

def mla_query(q_a, q_a_g, w_q_b, q_norm_g):
    b, s, _ = q_a.shape
    q = (rmsnorm(q_a, q_a_g) @ w_q_b).reshape(b, s, N_HEADS, QK_HEAD)
    return rmsnorm(q, q_norm_g)

def mla_kv(ckv, kpe, w_kv_b, k_norm_g):
    b, l, _ = ckv.shape
    kv = (ckv @ w_kv_b).reshape(b, l, N_HEADS, QK_NOPE + V_HEAD)
    k_nope, v = kv[..., :QK_NOPE], kv[..., QK_NOPE:]
    k_pe = jnp.broadcast_to(kpe[:, :, None, :], (b, l, N_HEADS, QK_ROPE))
    k = rmsnorm(jnp.concatenate([k_nope, k_pe], axis=-1), k_norm_g)
    return k, v

def attend(q, k, v):
    b, sq, h, dq = q.shape
    nb = sq // Q_BLOCK
    qb = q.reshape(b, nb, Q_BLOCK, h, dq).transpose(1, 0, 2, 3, 4)

    def one_block(qi):
        s = jnp.einsum('bqhd,bkhd->bhqk', qi, k).astype(jnp.float32) * ATTN_SCALE
        p = jax.nn.softmax(s, axis=-1)
        return jnp.einsum('bhqk,bkhd->bqhd', p.astype(v.dtype), v)

    o = lax.map(one_block, qb)
    return o.transpose(1, 0, 2, 3, 4).reshape(b, sq, h * V_HEAD)

def fourier_mix(f):
    b, s, _ = f.shape
    fg = f.reshape(b, s, FN_GROUPS, FN_GROUP_W).astype(jnp.float32)
    y = jnp.fft.fft2(fg, axes=(1, 3), norm='ortho').real
    return y.reshape(b, s, FN_WIDTH).astype(f.dtype)

def merge_branches(attn, fn, gate_a, gate_f, w_attn_o, w_fnet, w_out):
    u = jax.nn.sigmoid(gate_a) * (attn @ w_attn_o) + jax.nn.sigmoid(gate_f) * (fourier_mix(fn) @ w_fnet)
    return u @ w_out

def hier_moe(h, w_rg, b_rg, w_re, b_re, w_gate, w_up, w_down):
    b, s, d = h.shape
    n = b * s
    t = h.reshape(n, d)
    g_prob = jax.nn.softmax((t @ w_rg).astype(jnp.float32) + b_rg, axis=-1)
    g_top_p, g_top_i = lax.top_k(g_prob, 1)
    e_logit = ((t @ w_re).astype(jnp.float32) + b_re).reshape(n, N_GROUPS, EXPERTS_PER_GROUP)
    e_sel = e_logit[jnp.arange(n), g_top_i[:, 0]]
    e_top_l, e_top_i = lax.top_k(e_sel, TOP_K_EXPERTS)
    e_w = jax.nn.softmax(e_top_l, axis=-1) * g_top_p
    expert_idx = g_top_i * EXPERTS_PER_GROUP + e_top_i
    combine = jnp.sum(jax.nn.one_hot(expert_idx, N_EXPERTS, dtype=jnp.float32) * e_w[..., None], axis=1)
    a = jnp.einsum('nd,edf->nef', t, w_gate)
    u = jnp.einsum('nd,edf->nef', t, w_up)
    act = jax.nn.silu(a) * u * combine.astype(t.dtype)[..., None]
    y = jnp.einsum('nef,efd->nd', act, w_down)
    return y.reshape(b, s, d)

def setup_inputs(seed: int = 0) -> dict:
    key = jax.random.key(seed)
    ks = jax.random.split(key, 32)

    def nrm(k, shape, scale):
        return jax.random.normal(k, shape, jnp.float32) * scale

    def gain(k, shape):
        return 1.0 + 0.02 * jax.random.normal(k, shape, jnp.float32)

    L = DEPTH
    return {
        'x_prompt': nrm(ks[0], (BATCH, SEQ, D_MODEL), 1.0),
        'x_sample': nrm(ks[1], (DEC_BATCH, DEC_SEQ, D_MODEL), 1.0),
        'cache_ckv': nrm(ks[2], (DEC_BATCH, DEPTH, PAST_LEN, KV_LORA), 1.0),
        'cache_kpe': nrm(ks[3], (DEC_BATCH, DEPTH, PAST_LEN, QK_ROPE), 1.0),
        'c': nrm(ks[4], (DEC_BATCH, D_MODEL), 1.0),
        'c_ctx': nrm(ks[5], (D_MODEL,), 1.0),
        'w_mod': nrm(ks[6], (L, D_MODEL, 6 * D_MODEL), D_MODEL ** -0.5),
        'b_mod': nrm(ks[7], (L, 6 * D_MODEL), 0.02),
        'norm1_g': gain(ks[8], (L, D_MODEL)),
        'w_in': nrm(ks[9], (L, D_MODEL, IN_WIDTH), D_MODEL ** -0.5),
        'q_a_norm_g': gain(ks[10], (L, Q_LORA)),
        'w_q_b': nrm(ks[11], (L, Q_LORA, N_HEADS * QK_HEAD), Q_LORA ** -0.5),
        'kv_a_norm_g': gain(ks[12], (L, KV_LORA)),
        'w_kv_b': nrm(ks[13], (L, KV_LORA, N_HEADS * (QK_NOPE + V_HEAD)), KV_LORA ** -0.5),
        'q_norm_g': gain(ks[14], (L, QK_HEAD)),
        'k_norm_g': gain(ks[15], (L, QK_HEAD)),
        'w_attn_o': nrm(ks[16], (L, N_HEADS * V_HEAD, D_MODEL), (N_HEADS * V_HEAD) ** -0.5),
        'w_fnet': nrm(ks[17], (L, FN_WIDTH, D_MODEL), FN_WIDTH ** -0.5),
        'w_out': nrm(ks[18], (L, D_MODEL, D_MODEL), D_MODEL ** -0.5),
        'norm2_g': gain(ks[19], (L, D_MODEL)),
        'w_router_group': nrm(ks[20], (L, D_MODEL, N_GROUPS), D_MODEL ** -0.5),
        'b_router_group': nrm(ks[21], (L, N_GROUPS), 0.01),
        'w_router_expert': nrm(ks[22], (L, D_MODEL, N_EXPERTS), D_MODEL ** -0.5),
        'b_router_expert': nrm(ks[23], (L, N_EXPERTS), 0.01),
        'w_exp_gate': nrm(ks[24], (L, N_EXPERTS, D_MODEL, D_EXPERT), D_MODEL ** -0.5),
        'w_exp_up': nrm(ks[25], (L, N_EXPERTS, D_MODEL, D_EXPERT), D_MODEL ** -0.5),
        'w_exp_down': nrm(ks[26], (L, N_EXPERTS, D_EXPERT, D_MODEL), D_EXPERT ** -0.5),
    }

def reference(x_prompt, x_sample, cache_ckv, cache_kpe, c, c_ctx, w_mod, b_mod, norm1_g, w_in, q_a_norm_g, w_q_b,
              kv_a_norm_g, w_kv_b, q_norm_g, k_norm_g, w_attn_o, w_fnet, w_out, norm2_g, w_router_group,
              b_router_group, w_router_expert, b_router_expert, w_exp_gate, w_exp_up, w_exp_down):
    xp = x_prompt
    xs = x_sample
    ckv_layers = []
    kpe_layers = []
    for l in range(DEPTH):
        mod_ctx = adaln(c_ctx[None, :], w_mod[l], b_mod[l])
        mod_lat = adaln(c, w_mod[l], b_mod[l])
        moe_args = (w_router_group[l], b_router_group[l], w_router_expert[l], b_router_expert[l],
                    w_exp_gate[l], w_exp_up[l], w_exp_down[l])

        q_a, kv_a, kpe, fn, ga, gf = mixer_inputs(xp, mod_ctx[0], mod_ctx[1], norm1_g[l], w_in[l])
        ckv = rmsnorm(kv_a, kv_a_norm_g[l])
        q = mla_query(q_a, q_a_norm_g[l], w_q_b[l], q_norm_g[l])
        k, v = mla_kv(ckv, kpe, w_kv_b[l], k_norm_g[l])
        attn = attend(q, k, v)
        xp = xp + mod_ctx[2] * merge_branches(attn, fn, ga, gf, w_attn_o[l], w_fnet[l], w_out[l])
        xp = xp + mod_ctx[5] * hier_moe(modulate(xp, norm2_g[l], mod_ctx[3], mod_ctx[4]), *moe_args)
        ckv_layers.append(ckv)
        kpe_layers.append(kpe)

        q_a, kv_a, kpe_s, fn, ga, gf = mixer_inputs(xs, mod_lat[0], mod_lat[1], norm1_g[l], w_in[l])
        ckv_s = rmsnorm(kv_a, kv_a_norm_g[l])
        q = rope_2d(mla_query(q_a, q_a_norm_g[l], w_q_b[l], q_norm_g[l]))
        k_lat, v_lat = mla_kv(ckv_s, kpe_s, w_kv_b[l], k_norm_g[l])
        k_lat = rope_2d(k_lat)
        k_ctx, v_ctx = mla_kv(cache_ckv[:, l], cache_kpe[:, l], w_kv_b[l], k_norm_g[l])
        attn = attend(q, jnp.concatenate([k_ctx, k_lat], axis=1), jnp.concatenate([v_ctx, v_lat], axis=1))
        xs = xs + mod_lat[2] * merge_branches(attn, fn, ga, gf, w_attn_o[l], w_fnet[l], w_out[l])
        xs = xs + mod_lat[5] * hier_moe(modulate(xs, norm2_g[l], mod_lat[3], mod_lat[4]), *moe_args)

    new_ckv = jnp.stack(ckv_layers, axis=1)
    new_kpe = jnp.stack(kpe_layers, axis=1)
    return (xp, xs, new_ckv, new_kpe)


_drawn_inputs = setup_inputs


def setup_inputs(seed=0):
    import zlib

    import numpy as np

    out = dict(_drawn_inputs(seed))
    spreads = {}
    factors = {'q_a_norm_g': 8.0,
     'kv_a_norm_g': 3.019,
     'q_norm_g': 8.0,
     'k_norm_g': 5.455,
     'b_router_group': 9.626,
     'b_router_expert': 32.332}
    for name, (base, spread) in spreads.items():
        noise = np.random.default_rng([zlib.crc32(name.encode()), seed]).standard_normal(out[name].shape)
        drawn = base * np.exp(spread * noise) if base else spread * noise
        out[name] = __import__('jax').numpy.asarray(drawn.astype(out[name].dtype))
    for name, factor in factors.items():
        out[name] = (out[name] * factor).astype(out[name].dtype)
    return out
```

```python
from contextlib import ExitStack

import numpy as np
import concourse.bass as bass
from concourse import mybir

F32 = mybir.dt.float32
I32 = mybir.dt.int32
ALU = mybir.AluOpType
ACT = mybir.ActivationFunctionType
AX = mybir.AxisListType

P = 128
D = 1024
KC = D // P
NT = 3
NTOK = NT * P
Q_LORA, KV_LORA, ROPE, NOPE, VH, H = 512, 256, 32, 64, 64, 8
QKH = NOPE + ROPE
FNW, FG = 512, 4
TOKW = Q_LORA + KV_LORA + ROPE + FNW
GATE0 = TOKW
GRID_W = 64
NG, EPG = 4, 4
NE = NG * EPG
DE = 512
EPS = 1e-6
SCALE = QKH ** -0.5
SLOTS = 64
MAX_TILES = NTOK // SLOTS
ALL_TILES = NE + 2 * NTOK // SLOTS
PIECE = 4096
RING1 = 4
ESLOTS = 3

C_ID, C_ONE, C_TRI, C_IOTA, C_FC, C_FS = 0, 128, 256, 384, 512, 640
C_SL, C_SC, C_RC, C_RS, C_DESC = 768, 1792, 2048, 2080, 2112
NCON = 2128


def constants():
    t = np.zeros((P, NCON), np.float64)
    i = np.arange(P)
    t[:, C_ID:C_ID + P] = np.eye(P)
    t[:, C_ONE:C_ONE + P] = 1.0
    t[:, C_TRI:C_TRI + P] = i[:, None] < i[None, :]
    t[:, C_IOTA:C_IOTA + P] = (i % SLOTS)[None, :]
    ang = 2 * np.pi * np.outer(i, i) / P
    t[:, C_FC:C_FC + P] = np.cos(ang) / np.sqrt(P)
    t[:, C_FS:C_FS + P] = -np.sin(ang) / np.sqrt(P)
    s = 2 * P
    for ch in range(2):
        a = 2 * np.pi * (np.outer(i + ch * P, np.arange(s)) % s) / s
        t[:, C_SL + ch * 512:C_SL + ch * 512 + 256] = np.cos(a) / np.sqrt(s)
        t[:, C_SL + ch * 512 + 256:C_SL + ch * 512 + 512] = np.sin(a) / np.sqrt(s)
    t[:, C_SC:C_SC + P] = np.cos(ang) / np.sqrt(P)
    t[:, C_SC + P:C_SC + 2 * P] = np.sin(ang) / np.sqrt(P)
    freqs = np.float32(10000.0) ** (-np.arange(8, dtype=np.float32) / np.float32(8))
    for tt in range(2):
        pos = i + tt * P
        for ax, q in enumerate((pos // GRID_W, pos % GRID_W)):
            a = (q.astype(np.float32)[:, None] * freqs[None, :]).astype(np.float32).astype(np.float64)
            t[:, C_RC + tt * 16 + ax * 8:C_RC + tt * 16 + ax * 8 + 8] = np.cos(a)
            t[:, C_RS + tt * 16 + ax * 8:C_RS + tt * 16 + ax * 8 + 8] = np.sin(a)
    t[:, C_DESC:C_DESC + 16] = np.tile(np.arange(4, 0, -1), 4)[None, :]
    return t.astype(np.float32)


class Steps:

    def __init__(self, sem, names):
        self.sem, self.names, self.count = sem, names, 0
        self.value = {n: i + 1 for i, n in enumerate(names)}
        assert len(self.value) == len(names)

    def at(self, name):
        return self.sem, self.value[name]

    def mark(self, name):
        assert self.names[self.count] == name, (name, self.names[self.count])
        self.count += 1
        return self.sem, 1


FILLERS = [("g", 0), ("g", 1), ("g", 2), ("g", 3), ("mod", 1), ("g", 8), ("g", 9), ("g", 10), ("g", 11), ("mod", 2),
           ("g", 4), ("g", 5), ("g", 6), ("g", 7), ("g", 12), ("g", 13), ("g", 14), ("g", 15)]
UNITS = [(h, t) for h in range(H) for t in range(NT)]
MIDDLE = [("tok", 0), ("T", "c"), ("tok", 1), ("T", 0), ("tok", 2), ("KV", "c"), ("T", 1), ("FA", 0), ("FA", 1),
          ("KV", 0), ("XK", "c"), ("QB", 0), ("T", 2), ("FA", 2), ("XK", 0), ("KV", 1), ("FA", 3), ("XQ", 0),
          ("QB", 1), ("XK", 1), ("KV", 2), ("FB", 0), ("XQ", 1), ("QB", 2), ("XK", 2), ("FB", 1), ("XQ", 2)]
ROW = {"c": 3, 0: 0, 1: 1, 2: 2}
KSLOT = {"c": 0, 1: 1, 2: 2, 0: 3}


DVE_MIDDLE = [("tok", 0), ("T", "c"), ("tok", 1), ("T", 0), ("tok", 2), ("kh", "c"), ("T", 1), ("kn", "c"),
              ("kh", 0), ("kn", 0), ("T", 2), ("qn", 0), ("kh", 1), ("kn", 1), ("qn", 1), ("kh", 2), ("kn", 2), ("qn", 2)]
ACT_MIDDLE = [("tok", 0), ("tok", 1), ("tok", 2), ("vv", "c"), ("rk", "c"), ("fA", 0), ("fA", 1), ("vv", 0), ("rk", 0),
              ("kT", "c"), ("qh", 0), ("rq", 0), ("fA", 2), ("kT", 0), ("vv", 1), ("rk", 1), ("fA", 3), ("qT", 0),
              ("qh", 1), ("rq", 1), ("kT", 1), ("vv", 2), ("rk", 2), ("yT", 0), ("qT", 1), ("qh", 2), ("rq", 2),
              ("kT", 2), ("yT", 1), ("qT", 2)]


def pe_steps():
    s = ["vecT"] + [f"xT{t}" for t in range(NT)] + ["mod0", "modT"]
    s += [f"{k} {i}" for k, i in MIDDLE]
    s += ["S 0"]
    for u in range(len(UNITS)):
        if u + 1 < len(UNITS):
            s.append(f"S {u + 1}")
        if u < len(FILLERS):
            s.append("fill %s %d" % FILLERS[u])
        s.append(f"PT {u}")
        if u:
            s.append(f"PV {u - 1}")
    s += [f"PV {len(UNITS) - 1}"]
    s += [f"AF {c}" for c in range(KC)] + [f"out {t}" for t in range(NT)]
    s += [f"h2T {t}" for t in range(NT)] + ["router", "rank", "xg", "xeT"]
    return s


def dve_order():
    s = ["silu c", "vec out"] + [f"xn {t}" for t in range(NT)] + ["modrow 0", "mod cols"]
    s += [f"hT {t}" for t in range(NT)]
    for what, i in DVE_MIDDLE:
        s += [n % i for n in {"tok": ["nr %s", "ckv %s"], "T": ["Tev %s"], "kh": ["kh %s"], "kn": ["rk %s", "kn %s"],
                              "qn": ["rq %s", "qn %s"]}[what]]
    s += ["mx 0"]
    for u in range(len(UNITS)):
        s.append(f"pn {u}")
        if u + 1 < len(UNITS):
            s.append(f"mx {u + 1}")
        if 1 <= u <= len(FILLERS) and FILLERS[u - 1][0] == "mod":
            s.append("modrow %d" % FILLERS[u - 1][1])
        if u and u % 6 == 0:
            s.append(f"oT {u // 6 - 1}")
    s += ["oT 3"] + [f"u {c}" for c in range(KC)]
    for t in range(NT):
        s += [f"x1 {t}", f"h2 {t}"]
    return s + ["gmax", "top2", "masks", "tab"]


def act_order():
    s = ["exp c", "rsx", *(f"hT {t}" for t in range(NT))]
    for what, i in ACT_MIDDLE:
        s += [n % i for n in {"tok": ["rs %s", "kpe %s", "fn %s", "qan %s"], "vv": ["vv %s"], "rk": ["rk %s"],
                              "qh": ["qh %s"], "rq": ["rq %s"], "kT": ["kT %s"], "qT": ["qT %s"], "fA": ["fA %s"],
                              "yT": ["yT %s"]}[what]]
    s += ["p 0"]
    for u in range(len(UNITS)):
        if u + 1 < len(UNITS):
            s.append(f"p {u + 1}")
        if u < len(FILLERS) and FILLERS[u][0] == "g":
            s.append("ge %d" % FILLERS[u][1])
        s.append(f"pT {u}")
    for t in range(NT):
        s += [f"rs2 {t}"]
        if t:
            s.append(f"h2T {t - 1}")
    return s + ["h2T 2", "gexp", "dexp"]


def program(nc, a):
    ctx = ExitStack()
    with ctx:
        def sb(name, shape, dt=F32):
            return ctx.enter_context(nc.sbuf_tensor(name, shape, dt))

        def sem(name):
            return ctx.enter_context(nc.semaphore(name))

        con = sb("con", [P, NCON])
        x_sb = sb("x_sb", [P, NT, D])
        hT = sb("hT", [P, KC, NTOK])
        work = sb("work", [P, 5632])
        yTt = sb("yTt", [P, 1536])
        big = sb("big", [P, 9 * PIECE])
        small = sb("small", [P, 840])
        tab = sb("tab", [1, 40], I32)

        ident, ones = con[:, C_ID:C_ID + P], con[:, C_ONE:C_ONE + P]
        tri, iota = con[:, C_TRI:C_TRI + P], con[:, C_IOTA:C_IOTA + P]
        dft_c, dft_s = con[:, C_FC:C_FC + P], con[:, C_FS:C_FS + P]

        def piece(n):
            return big[:, n * PIECE:(n + 1) * PIECE]

        wqb = x_sb[:, :, :].rearrange("p a b -> p (a b)").rearrange("p (k n) -> p k n", k=4)
        vv = work[:, 0:2048].rearrange("p (s n) -> p s n", s=4)
        qaT = work[:, 2048:3584].rearrange("p (k n) -> p k n", k=4)
        ckvT = work[:, 3584:4608].rearrange("p (k r n) -> p k r n", k=2, r=4)
        ckv = work[:, 4608:5632].rearrange("p (r n) -> p r n", r=4)
        yT = yTt[:, :].rearrange("p (g n) -> p g n", g=4)
        misc = piece(4)
        wkvb = misc[:, 0:2048].rearrange("p (k n) -> p k n", k=2)
        bmod = misc[:, 2048:3584].rearrange("p (j n) -> p j n", j=3)
        modrow = misc[:, 3584:4096]
        A0 = 5 * PIECE
        gates = big[:, A0:A0 + 6144].rearrange("p (c n) -> p c n", c=16)
        qan = big[:, A0:A0 + 1024].rearrange("p (b n) -> p b n", b=2)
        fn = big[:, A0 + 1024:A0 + 2560].rearrange("p (t n) -> p t n", t=NT)
        qh = big[:, A0 + 2560:A0 + 3328].rearrange("p (h n) -> p h n", h=H)
        kh = big[:, A0 + 3328:A0 + 4096].rearrange("p (h n) -> p h n", h=H)
        sq = big[:, A0 + 4096:A0 + 4864]
        sqa = big[:, A0 + 4864:A0 + 5888]
        qT = big[:, A0 + 6144:A0 + 9216].rearrange("p (h n) -> p h n", h=H)
        uT = qT
        kT = big[:, A0 + 9216:A0 + 13312].rearrange("p (h n) -> p h n", h=H)
        fA = big[:, A0 + 13312:A0 + 16384].rearrange("p (g n) -> p g n", g=4)
        c32 = big[:, A0 + 13312:A0 + 13568].rearrange("p (k m) -> p k m", k=KC)
        c32_late = bmod[:, 0, 0:256].rearrange("p (k m) -> p k m", k=KC)
        vrow = big[:, A0 + 13568:A0 + 13696]
        srow = big[:, A0 + 13696:A0 + 13824]
        erow = big[:, A0 + 13824:A0 + 13952]
        probs = big[:, A0 + 13312:A0 + 14080].rearrange("p (b n) -> p b n", b=2)
        pT = big[:, A0 + 14080:A0 + 14848].rearrange("p (b n) -> p b n", b=2)
        oT = big[:, A0 + 14848:A0 + 16384].rearrange("p (c n) -> p c n", c=4)
        bc = big[:, A0:A0 + 6144].rearrange("p (v r n) -> p v r n", v=3, r=2)
        g2b = big[:, A0 + 9216:A0 + 10240]
        otmp = big[:, A0 + 10240:A0 + 11264]
        junk = big[:, A0 + 11424:A0 + 12448]
        g5 = piece(3)[:, 0:2048].rearrange("p (r n) -> p r n", r=2)
        wr = big[:, A0 + 11264:A0 + 11424].rearrange("p (k n) -> p k n", k=KC)
        h2T = big[:, A0 + 13312:A0 + 16384].rearrange("p (k n) -> p k n", k=KC)
        h2 = hT[:, :, :].rearrange("p a b -> p (a b)").rearrange("p (t n) -> p t n", t=NT)
        acc = work[:, 0:3072].rearrange("p (t n) -> p t n", t=NT)
        xg = work[:, 3072:3584]
        xeT = work[:, 3584:4096].rearrange("p (i g s) -> p i g s", i=4, g=2)
        eg = work[:, 4096:4352]
        actv = work[:, 4352:4608]
        actT = work[:, 4608:4864].rearrange("p (j g s) -> p j g s", j=2, g=2)
        ye = work[:, 4864:5376]
        P2 = yTt[:, 0:384].rearrange("p (t n) -> p t n", t=NT)
        Pw = yTt[:, 384:768].rearrange("p (t n) -> p t n", t=NT)
        PwT = yTt[:, 768:1152].rearrange("p (t n) -> p t n", t=NT)
        ptmp = yTt[:, 1152:1536].rearrange("p (t n) -> p t n", t=NT)

        off = [0]

        def take(n):
            v = small[:, off[0]:off[0] + n]
            off[0] += n
            return v
        kvg, qng, kng, rb = take(256), take(96), take(96), take(20)
        g1T, qgT, shT, a1T = take(8), take(4), take(16), take(16)
        kpe = take(128).rearrange("p (r n) -> p r n", r=4)
        ssx, msx, rsx, nwx = take(3), take(3), take(3), take(3)
        ss, ms, rs, nw = take(10), take(10), take(10), take(10)
        mx, sm, ri = take(4), take(4), take(4)
        epsc = take(1)
        fsl = take(6).rearrange("p (t c) -> p t c", t=NT)
        wsl = take(6).rearrange("p (t c) -> p t c", t=NT)
        shT = shT.rearrange("p (r k) -> p r k", r=2)
        a1T = a1T.rearrange("p (r k) -> p r k", r=2)
        ro = [3072]

        def rtake(n, pat=None, **kw):
            v = work[:, ro[0]:ro[0] + n]
            ro[0] += n
            return v.rearrange(pat, **kw) if pat else v
        lg = rtake(60, "p (t n) -> p t n", t=NT)
        rm, rsum, gp, rm1, rm2, rd, rr = (rtake(3) for _ in range(7))
        t4, ohg, esel, oh1, oh2, e2 = (rtake(12, "p (t n) -> p t n", t=NT) for _ in range(6))
        prod = rtake(48, "p (t g e) -> p t g e", t=NT, g=4)
        M1, M2, MM, slot, tmp48 = (rtake(48, "p (t n) -> p t n", t=NT) for _ in range(5))
        cnt, ntf, cA, cB, base = rtake(16), rtake(16), rtake(17), rtake(17), rtake(16)

        B = [ctx.enter_context(nc.psum_tensor(f"bank{i}", [P, 512], F32)) for i in range(8)]
        modd = nc.dram_tensor("mod_rows", (2, 4096), F32, kind="Internal").ap()

        pe_done, v_done, a_done = sem("pe_done"), sem("dve_done"), sem("act_done")
        PE = Steps(pe_done, pe_steps())
        V = Steps(v_done, dve_order())
        A = Steps(a_done, act_order())
        zero_done = sem("zero_done")
        d_vec, d_con, d_small, d_cache, d_kvb, d_qb, d_bmod = map(sem, ("d_vec", "d_con", "d_small", "d_cache", "d_kvb", "d_qb", "d_bmod"))
        d_x = [sem(f"d_x{t}") for t in range(NT)]
        d_xre, d_mod1, d_mod2, d_bc, d_g5, d_out, d_outc = map(sem, ("d_xre", "d_mod1", "d_mod2", "d_bc", "d_g5", "d_out", "d_outc"))
        d_ring = [sem(f"d_ring{i}") for i in range(RING1)]
        d_gu = [sem(f"d_gu{s}") for s in range(ESLOTS)]
        d_dn = [sem(f"d_dn{s}") for s in range(ESLOTS)]
        t_p2, t_h, t_xg, t_xgs, t_xeTp, t_xeTs = map(sem, ("t_onehot", "t_gate_up", "t_gathered", "t_xg_sbuf", "t_xeT_psum", "t_xeT_sbuf"))
        t_exp, t_act, t_aTp, t_aTs, t_y, t_ye = map(sem, ("t_exp", "t_act", "t_actT_psum", "t_actT_sbuf", "t_down", "t_y_sbuf"))
        t_pw, t_pwp, t_pws, t_comb, t_add, t_acc = map(sem, ("t_weighted", "t_pwT_psum", "t_pwT_sbuf", "t_combined", "t_added", "t_acc"))
        fin = sem("y_ready")

        win = a["w_in"][0].rearrange("(k p) n -> p k n", p=P)
        wmod = a["w_mod"][0].rearrange("(k p) n -> p k n", p=P)
        TOKK = [(0, 3), (3, 6), (6, 8)]
        ring, n = {}, 0
        order = [("mod0", q) for q in range(4)] + [("tokw", q) for q in range(3)] + [("gate", 0)]
        order += [("mod1", q) for q in range(4)] + [("gate", 1)] + [("mod2", q) for q in range(4)]
        order += [("gate", 2), ("gate", 3), ("attn_o", 0), ("fnet", 0), ("out", 0), ("out", 1)]
        for n, key in enumerate(order):
            ring[key] = (n % RING1, n // RING1 + 1)

        def arrived(eng, key):
            s, k = ring[key]
            eng.wait_ge(d_ring[s], 16 * k)

        def rpiece(key, width):
            s = ring[key][0]
            return big[:, s * PIECE:s * PIECE + (PIECE // width) * width].rearrange("p (k n) -> p k n", n=width)

        used = {("mod0", q): "mod0" for q in range(4)}
        used |= {("tokw", q): "tok 2" for q in range(3)}
        used |= {("mod1", q): "fill mod 1" for q in range(4)} | {("mod2", q): "fill mod 2" for q in range(4)}
        GCH = {0: [0, 1, 2, 3], 1: [8, 9, 10, 11], 2: [4, 5, 6, 7], 3: [12, 13, 14, 15]}
        used |= {("gate", q): "fill g %d" % GCH[q][-1] for q in range(4)}

        block = ctx.enter_context(nc.Block())

        @block.sync
        def _(sp):
            sp.dma_start(vrow[0:8, :], a["c_ctx"].rearrange("(k n) -> k n", n=P)).then_inc(d_vec, 16)
            sp.dma_start(vrow[8:16, :], a["c"].rearrange("b (k n) -> (b k) n", n=P)).then_inc(d_vec, 16)
            sp.dma_start(vrow[16:24, :], a["norm1_g"].rearrange("b (k n) -> (b k) n", n=P)).then_inc(d_vec, 16)
            sp.dma_start(vrow[24:28, :], a["q_a_norm_g"].rearrange("b (k n) -> (b k) n", n=P)).then_inc(d_vec, 16)
            sp.dma_start(con[:, :], a["const_table"]).then_inc(d_con, 16)
            sp.dma_start(x_sb[:, 0, :], a["x_prompt"][0]).then_inc(d_x[0], 16)
            for q in range(4):
                if q < 2:
                    sp.dma_start(x_sb[:, 1 + q, :], a["x_sample"][0, q * P:(q + 1) * P, :]).then_inc(d_x[1 + q], 16)
                sp.dma_start(rpiece(("mod0", q), 2048), wmod[:, 2 * q:2 * q + 2, 0:2048]).then_inc(d_ring[q], 16)
            sp.wait_ge(zero_done, 2)
            for r in range(2):
                sp.dma_start(bmod[r:r + 97:32, :, :], a["b_mod"][0].rearrange("(j g n) -> g j n", j=3, g=4)).then_inc(d_bmod, 16)
            sp.dma_start(kvg, a["kv_a_norm_g"].to_broadcast([P, KV_LORA])).then_inc(d_small, 16)
            sp.dma_start(qng, a["q_norm_g"].to_broadcast([P, QKH])).then_inc(d_small, 16)
            sp.dma_start(kng, a["k_norm_g"].to_broadcast([P, QKH])).then_inc(d_small, 16)
            sp.dma_start(rb[:, 0:4], a["b_router_group"].to_broadcast([P, NG])).then_inc(d_small, 16)
            sp.dma_start(rb[:, 4:20], a["b_router_expert"].to_broadcast([P, NE])).then_inc(d_small, 16)
            sp.dma_start(ckv[:, 3, :], a["cache_ckv"][0, 0]).then_inc(d_cache, 16)
            sp.dma_start(kpe[:, 3, :], a["cache_kpe"][0, 0]).then_inc(d_cache, 16)
            sp.dma_start(wkvb, a["w_kv_b"][0].rearrange("(k p) n -> p k n", p=P)).then_inc(d_kvb, 16)

            def load(key):
                n = order.index(key)
                if n >= RING1:
                    sp.wait_ge(*PE.at(used[order[n - RING1]]))
                kind, q = key
                s = ring[key][0]
                if kind.startswith("mod"):
                    j = int(kind[3])
                    dst, src = rpiece(key, 2048), wmod[:, 2 * q:2 * q + 2, 2048 * j:2048 * j + 2048]
                elif kind == "tokw":
                    k0, k1 = TOKK[q]
                    dst, src = rpiece(key, TOKW)[:, 0:k1 - k0, :], win[:, k0:k1, 0:TOKW]
                elif kind == "gate":
                    dst = rpiece(key, 512)
                    c0 = GATE0 + GCH[q][0] * P
                    src = win[:, :, c0:c0 + 512]
                elif kind == "out":
                    dst, src = rpiece(key, D), a["w_out"][0].rearrange("(k p) n -> p k n", p=P)[:, 4 * q:4 * q + 4, :]
                else:
                    w = a["w_attn_o"] if kind == "attn_o" else a["w_fnet"]
                    dst, src = rpiece(key, D), w[0].rearrange("(k p) n -> p k n", p=P)
                sp.dma_start(dst, src).then_inc(d_ring[s], 16)

            for q in range(3):
                load(("tokw", q))
            load(("gate", 0))
            sp.wait_ge(*PE.at("xT2"))
            sp.dma_start(wqb, a["w_q_b"][0].rearrange("(k p) n -> p k n", p=P)).then_inc(d_qb, 16)
            sp.wait_ge(*V.at("ckv 0"))
            sp.wait_ge(*A.at("kpe 0"))
            sp.dma_start(a["new_ckv"][0, 0], ckv[:, 0, :]).then_inc(d_outc, 16)
            sp.dma_start(a["new_kpe"][0, 0], kpe[:, 0, :]).then_inc(d_outc, 16)
            for key in order[8:17]:
                load(key)
            sp.wait_ge(*V.at("modrow 1"))
            for r in range(2):
                sp.dma_start(modd[r, 0:2048].rearrange("(g n) -> g n", g=4), modrow[r:r + 97:32, :]).then_inc(d_mod1, 16)
            for key in order[17:19]:
                load(key)
            sp.wait_ge(*V.at("modrow 2"))
            for r in range(2):
                sp.dma_start(modd[r, 2048:4096].rearrange("(g n) -> g n", g=4), modrow[r:r + 97:32, :]).then_inc(d_mod2, 16)
            sp.wait_ge(*PE.at("QB 2"))
            sp.dma_start(x_sb[:, 0, :], a["x_prompt"][0]).then_inc(d_xre, 16)
            sp.dma_start(x_sb[:, 1:3, :], a["x_sample"][0].rearrange("(t p) n -> p t n", p=P)).then_inc(d_xre, 16)
            for key in order[19:23]:
                load(key)
            sp.wait_ge(*V.at("u 7"))
            sp.wait_ge(d_mod1, 32)
            sp.wait_ge(d_mod2, 32)
            for v in range(3):
                for r in range(2):
                    sp.dma_start(bc[:, v, r, :], modd[r:r + 1, v * D:(v + 1) * D].to_broadcast([P, D])).then_inc(d_bc, 16)
            sp.dma_start(g2b, a["norm2_g"].to_broadcast([P, D])).then_inc(d_bc, 16)
            sp.dma_start(wr[:, :, 0:NG], a["w_router_group"][0].rearrange("(k p) n -> p k n", p=P)).then_inc(d_bc, 16)
            sp.dma_start(wr[:, :, NG:NG + NE], a["w_router_expert"][0].rearrange("(k p) n -> p k n", p=P)).then_inc(d_bc, 16)

            wg = a["w_exp_gate"][0].rearrange("e (k p) n -> p e k n", p=P)
            wu = a["w_exp_up"][0].rearrange("e (k p) n -> p e k n", p=P)
            wd = a["w_exp_down"][0].rearrange("e (k p) n -> p e k n", p=P)

            def load_gate(e, s):
                sp.dma_start(piece(3 * s).rearrange("p (k n) -> p k n", n=DE), wg[:, e]).then_inc(d_gu[s], 16)

            def load_up(e, s):
                sp.dma_start(piece(3 * s + 1).rearrange("p (k n) -> p k n", n=DE), wu[:, e]).then_inc(d_gu[s], 16)

            def load_down(e, s):
                sp.dma_start(piece(3 * s + 2).rearrange("p (k n) -> p k n", n=D), wd[:, e]).then_inc(d_dn[s], 16)

            sp.wait_ge(*PE.at("AF 7"))
            load_gate(0, 0)
            load_gate(1, 1)
            load_up(1, 1)
            sp.wait_ge(*PE.at("out 2"))
            load_up(0, 0)
            load_down(0, 0)
            sp.wait_ge(*V.at("h2 2"))
            load_down(1, 1)
            sp.wait_ge(*PE.at("router"))
            load_gate(2, 2)
            load_up(2, 2)
            load_down(2, 2)
            sp.wait_ge(*V.at("tab"))

            def next_expert(e, s):
                done = sp.value_load(tab[0:1, bass.ds(16 + e - 2, 1)], min_val=1, max_val=ALL_TILES)
                sp.wait_ge(t_y, done)
                load_gate(e, s)
                load_up(e, s)
                load_down(e, s)

            with sp.Fori(1, NE // ESLOTS) as g:
                for s in range(ESLOTS):
                    next_expert(g * ESLOTS + s, s)
            next_expert(NE - 1, (NE - 1) % ESLOTS)
            done = sp.value_load(tab[0:1, 16 + 14:16 + 15], min_val=1, max_val=ALL_TILES)
            sp.wait_ge(t_y, done)
            for r in range(2):
                sp.dma_start(g5[:, r, :], modd[r:r + 1, 3 * D:4 * D].to_broadcast([P, D])).then_inc(d_g5, 16)
            for t in range(NT):
                sp.wait_ge(fin, t + 1)
                dst = a["y_prompt"][0] if t == 0 else a["y_sample"][0, (t - 1) * P:t * P, :]
                sp.dma_start(dst, acc[:, t, :]).then_inc(d_out, 16)
            sp.wait_ge(d_out, 16 * NT)
            sp.wait_ge(d_outc, 32)

        @block.gpsimd
        def _(pool):
            nc.gpsimd.memset(c32, 0.0).then_inc(zero_done, 1)
            nc.gpsimd.memset(bmod, 0.0).then_inc(zero_done, 1)
            nc.gpsimd.memset(epsc, EPS).then_inc(zero_done, 1)

        @block.tensor
        def _(pe):
            mm, tr = nc.tensor.matmul, nc.tensor.transpose
            pe.wait_ge(d_con, 16)
            pe.wait_ge(d_vec, 64)
            tr(B[0][:, 0:28], vrow[0:28, :], ident[0:28, 0:28])
            pe.wait_ge(*V.at("silu c"))
            tr(B[0][:, 32:48], srow[0:16, :], ident[0:16, 0:16]).then_inc(*PE.mark("vecT"))
            for t in range(NT):
                pe.wait_ge(*V.at(f"xn {t}"))
                for k in range(KC):
                    i = tr(B[1 + 2 * t + k // 4][:, (k % 4) * P:(k % 4 + 1) * P], x_sb[:, t, k * P:(k + 1) * P], ident)
                i.then_inc(*PE.mark(f"xT{t}"))

            def modulation(j, bank):
                for k in range(KC):
                    key = (f"mod{j}", k // 2)
                    if k % 2 == 0:
                        arrived(pe, key)
                    for g in range(4):
                        i = mm(bank[32 * g:32 * g + 32, :], (c32_late if j else c32)[:, k, :], rpiece(key, 2048)[:, k % 2, 512 * g:512 * g + 512],
                               start=(k == 0), stop=(k == KC - 1))
                return i

            pe.wait_ge(*V.at("vec out"))
            modulation(0, B[7]).then_inc(*PE.mark("mod0"))
            pe.wait_ge(*V.at("modrow 0"))
            for i4 in range(4):
                i = tr(B[0][:, i4 * P:(i4 + 1) * P], modrow[:, i4 * P:(i4 + 1) * P], ident)
            i.then_inc(*PE.mark("modT"))

            def tok(t):
                b = 1 if t % 2 == 0 else 4
                if t == 2:
                    pe.wait_ge(*A.at("qan 0"))
                    pe.wait_ge(*V.at("ckv 0"))
                else:
                    for x in range(NT):
                        pe.wait_ge(*V.at(f"hT {x}"))
                        pe.wait_ge(*A.at(f"hT {x}"))
                for k in range(KC):
                    key = ("tokw", [0, 0, 0, 1, 1, 1, 2, 2][k])
                    arrived(pe, key)
                    w = rpiece(key, TOKW)[:, k - TOKK[key[1]][0], :]
                    lhs = hT[:, k, t * P:(t + 1) * P]
                    mm(B[b][:, :], lhs, w[:, 0:512], start=(k == 0), stop=(k == KC - 1))
                    mm(B[b + 1][:, 0:288], lhs, w[:, 512:800], start=(k == 0), stop=(k == KC - 1))
                    i = mm(B[b + 2][:, :], lhs, w[:, 800:1312], start=(k == 0), stop=(k == KC - 1))
                i.then_inc(*PE.mark(f"tok {t}"))

            def lora_T(r):
                if r == "c":
                    pe.wait_ge(d_cache, 32)
                    pe.wait_ge(*V.at("mod cols"))
                else:
                    pe.wait_ge(*V.at(f"ckv {r}"))
                    pe.wait_ge(*A.at(f"qan {r}"))
                    pe.wait_ge(*V.at("Tev %s" % {0: "c", 1: 0, 2: 1}[r]))
                    if r == 0:
                        pe.wait_ge(*V.at("modrow 0"))
                    for k in range(4):
                        tr(B[7][:, k * P:(k + 1) * P], qan[:, r % 2, k * P:(k + 1) * P], ident)
                for k in range(2):
                    i = tr(B[0][:, k * P:(k + 1) * P], ckv[:, ROW[r], k * P:(k + 1) * P], ident)
                i.then_inc(*PE.mark(f"T {r}"))

            def kv_b(r):
                pe.wait_ge(*V.at(f"Tev {r}"))
                if r == "c":
                    pe.wait_ge(d_kvb, 16)
                    pe.wait_ge(*A.at("fn 2"))
                    pe.wait_ge(*A.at("qan 1"))
                else:
                    prev = {0: "c", 1: 0, 2: 1}[r]
                    pe.wait_ge(*V.at(f"kh {prev}"))
                    pe.wait_ge(*A.at(f"vv {prev}"))
                for half in range(2):
                    for k in range(2):
                        i = mm(B[3 + half][:, :], ckvT[:, k, ROW[r], :], wkvb[:, k, half * 512:(half + 1) * 512],
                               start=(k == 0), stop=(k == 1))
                i.then_inc(*PE.mark(f"KV {r}"))

            def q_b(t):
                pe.wait_ge(*V.at(f"Tev {t}"))
                if t == 0:
                    pe.wait_ge(d_qb, 16)
                    pe.wait_ge(*A.at("qan 2"))
                    pe.wait_ge(*V.at("ckv 2"))
                else:
                    pe.wait_ge(*A.at(f"qh {t - 1}"))
                for half in range(2):
                    for k in range(4):
                        i = mm(B[1 + half][:, 0:384], qaT[:, k, t * P:(t + 1) * P], wqb[:, k, half * 384:(half + 1) * 384],
                               start=(k == 0), stop=(k == 3))
                i.then_inc(*PE.mark(f"QB {t}"))

            def heads_T(src, step):
                for h in range(H):
                    i = tr(B[5 + h // 4][0:QKH, (h % 4) * P:(h % 4 + 1) * P], src[:, h, :], ident)
                i.then_inc(*PE.mark(step))

            last_x = []

            def xk(r):
                pe.wait_ge(*V.at(f"kn {r}"))
                pe.wait_ge(*A.at(last_x[-1] if last_x else "fA 1"))
                heads_T(kh, f"XK {r}")
                last_x.append(f"kT {r}")

            def xq(t):
                pe.wait_ge(*V.at(f"qn {t}"))
                pe.wait_ge(*A.at(last_x[-1]))
                heads_T(qh, f"XQ {t}")
                last_x.append(f"qT {t}")

            def fourier_seq(g):
                bl, bx = (B[5], B[6]) if g < 2 else (B[7], B[0])
                if g == 0:
                    pe.wait_ge(*A.at("fn 2"))
                    pe.wait_ge(*A.at("qan 1"))
                elif g == 2:
                    pe.wait_ge(*V.at("Tev 2"))
                else:
                    pe.wait_ge(*A.at(f"fA {g - 1}"))
                for s in range(2):
                    mm(bl[:, :], fn[:, 1 + s, g * P:(g + 1) * P], con[:, C_SL + s * 512:C_SL + (s + 1) * 512],
                       start=(s == 0), stop=(s == 1))
                mm(bx[:, 0:256], fn[:, 0, g * P:(g + 1) * P], con[:, C_SC:C_SC + 256], start=True,
                   stop=True).then_inc(*PE.mark(f"FA {g}"))

            def fourier_ch(part):
                if part == 0:
                    pe.wait_ge(*A.at("fA 3"))
                    for pair in range(2):
                        b = (B[7], B[0])[pair]
                        mm(b[:, :], dft_c, fA[:, 2 * pair:2 * pair + 2, 0:256], start=True, stop=False)
                        i = mm(b[:, :], dft_s, fA[:, 2 * pair:2 * pair + 2, 256:512], start=False, stop=True)
                else:
                    pe.wait_ge(*A.at("yT 0"))
                    mm(B[7][:, :], dft_c, fA[:, :, 512:640], start=True, stop=False)
                    i = mm(B[7][:, :], dft_s, fA[:, :, 640:768], start=False, stop=True)
                i.then_inc(*PE.mark(f"FB {part}"))

            does = {"tok": tok, "T": lora_T, "KV": kv_b, "QB": q_b, "XK": xk, "XQ": xq, "FA": fourier_seq, "FB": fourier_ch}
            for what, i in MIDDLE:
                does[what](i)

            def scores(u):
                h, t = UNITS[u]
                if u >= 2:
                    pe.wait_ge(*A.at(f"p {u - 2}"))
                else:
                    pe.wait_ge(*A.at("qT 2"))
                k0, kn = (384, P) if t == 0 else (0, 384)
                mm(B[1 + u % 2][:, 0:kn], qT[0:QKH, h, t * P:(t + 1) * P], kT[0:QKH, h, k0:k0 + kn], start=True,
                   stop=True).then_inc(*PE.mark(f"S {u}"))

            def fill(n):
                kind, c = FILLERS[n]
                bank = B[7] if n % 2 == 0 else B[0]
                if n >= 2:
                    pk, pc = FILLERS[n - 2]
                    pe.wait_ge(*(A.at(f"ge {pc}") if pk == "g" else V.at(f"modrow {pc}")))
                else:
                    pe.wait_ge(*A.at("yT 1"))
                if kind == "mod":
                    modulation(c, bank).then_inc(*PE.mark(f"fill mod {c}"))
                    return
                q = [q for q in GCH if c in GCH[q]][0]
                arrived(pe, ("gate", q))
                w = rpiece(("gate", q), 512)
                c0 = (c - GCH[q][0]) * P
                for k in range(KC):
                    i = mm(bank[:, 0:NTOK], w[:, k, c0:c0 + P], hT[:, k, :], start=(k == 0), stop=(k == KC - 1))
                i.then_inc(*PE.mark(f"fill g {c}"))

            def probs_T(u):
                h, t = UNITS[u]
                pe.wait_ge(*V.at(f"pn {u}"))
                if u >= 2:
                    pe.wait_ge(*A.at(f"pT {u - 2}"))
                for kt in range(1 if t == 0 else 3):
                    i = tr(B[3 + u % 2][:, kt * P:(kt + 1) * P], probs[:, u % 2, kt * P:(kt + 1) * P], ident)
                i.then_inc(*PE.mark(f"PT {u}"))

            def pv(u):
                h, t = UNITS[u]
                pair = h // 2
                pe.wait_ge(*A.at(f"pT {u}"))
                if u % 6 == 0 and pair >= 2:
                    pe.wait_ge(*V.at(f"oT {pair - 2}"))
                slots = [3] if t == 0 else [0, 1, 2]
                o = B[5 + pair % 2][VH * (h % 2):VH * (h % 2) + VH, t * P:(t + 1) * P]
                for n, s in enumerate(slots):
                    i = mm(o, vv[:, s, h * VH:(h + 1) * VH], pT[:, u % 2, n * P:(n + 1) * P], start=(n == 0), stop=(n == len(slots) - 1))
                i.then_inc(*PE.mark(f"PV {u}"))

            scores(0)
            for u in range(len(UNITS)):
                if u + 1 < len(UNITS):
                    scores(u + 1)
                if u < len(FILLERS):
                    fill(u)
                probs_T(u)
                if u:
                    pv(u - 1)
            pv(len(UNITS) - 1)

            pe.wait_ge(*V.at("oT 3"))
            arrived(pe, ("attn_o", 0))
            arrived(pe, ("fnet", 0))
            wa, wf = rpiece(("attn_o", 0), D), rpiece(("fnet", 0), D)
            for c in range(KC):
                if c >= 2:
                    pe.wait_ge(*V.at(f"u {c - 2}"))
                for k in range(4):
                    mm(B[1 + c % 2][:, 0:NTOK], wa[:, k, c * P:(c + 1) * P], oT[:, k, :], start=(k == 0), stop=(k == 3))
                for k in range(4):
                    i = mm(B[3 + c % 2][:, 0:NTOK], wf[:, k, c * P:(c + 1) * P], yT[:, k, :], start=(k == 0), stop=(k == 3))
                i.then_inc(*PE.mark(f"AF {c}"))

            OB = [(5, 6), (7, 0), (5, 6)]
            pe.wait_ge(*V.at("u 7"))
            arrived(pe, ("out", 0))
            arrived(pe, ("out", 1))
            for t in range(NT):
                if t == 2:
                    pe.wait_ge(*V.at("x1 0"))
                for half in range(2):
                    for k in range(KC):
                        w = rpiece(("out", k // 4), D)[:, k % 4, half * 512:(half + 1) * 512]
                        i = mm(B[OB[t][half]][:, :], uT[:, k, t * P:(t + 1) * P], w, start=(k == 0), stop=(k == KC - 1))
                i.then_inc(*PE.mark(f"out {t}"))
            for t in range(NT):
                pe.wait_ge(*V.at(f"h2 {t}"))
                if t == 2:
                    pe.wait_ge(*A.at("h2T 0"))
                b = 1 if t % 2 == 0 else 3
                for k in range(KC):
                    i = tr(B[b + k // 4][:, (k % 4) * P:(k % 4 + 1) * P], h2[:, t, k * P:(k + 1) * P], ident)
                i.then_inc(*PE.mark(f"h2T {t}"))
            pe.wait_ge(*A.at("h2T 2"))
            pe.wait_ge(d_bc, 9 * 16)
            for t in range(NT):
                for k in range(KC):
                    i = mm(B[7][:, t * 32:t * 32 + 20], h2T[:, k, t * P:(t + 1) * P], wr[:, k, :], start=(k == 0), stop=(k == KC - 1))
            i.then_inc(*PE.mark("router"))
            pe.wait_ge(*V.at("masks"))
            for t in range(NT):
                for x in range(t + 1):
                    mm(B[0][:, t * 16:(t + 1) * 16], ones if x < t else tri, MM[:, x, :], start=(x == 0), stop=(x == t))
            for x in range(NT):
                i = mm(B[0][:, 48:64], ones, MM[:, x, :], start=(x == 0), stop=(x == NT - 1))
            i.then_inc(*PE.mark("rank"))

            def gather():
                for t in range(NT):
                    for g in range(2):
                        i = mm(B[1][SLOTS * g:SLOTS * (g + 1), :], P2[:, t, 0:SLOTS], h2[:, t, g * 512:(g + 1) * 512],
                               start=(t == 0), stop=(t == NT - 1))
                return i

            def gathered_T():
                for q in range(4):
                    i = tr(B[2][:, q * P:(q + 1) * P], xg[:, q * P:(q + 1) * P], ident)
                return i

            pe.wait_ge(t_p2, 1)
            gather().then_inc(t_xg, 1)
            pe.wait_ge(t_xgs, 1)
            gathered_T().then_inc(t_xeTp, 1)
            pe.wait_ge(*V.at("tab"))

            def expert(e, s, n):
                first = pe.value_load(tab[0:1, bass.ds(16 + e, 1)], min_val=0, max_val=ALL_TILES)
                tiles = pe.value_load(tab[0:1, bass.ds(e, 1)], min_val=1, max_val=MAX_TILES)
                wgu = big[:, 3 * s * PIECE:(3 * s + 2) * PIECE].rearrange("p (w k n) -> p w k n", w=2, k=KC)
                wdn = piece(3 * s + 2).rearrange("p (k n) -> p k n", n=D)
                n_gu, n_dn = (pe.snap(n * 32), pe.snap(n * 16)) if not isinstance(n, int) else (n * 32, n * 16)
                with pe.Fori(0, tiles) as j:
                    T1, T2 = pe.snap(first + j + 1), pe.snap(first + j + 2)
                    add0, add2 = pe.snap((first + j) * 3 + 3), pe.snap((first + j) * 3 + 4)
                    pe.wait_ge(t_xeTs, T1)
                    pe.wait_ge(d_gu[s], n_gu)
                    for k in range(KC):
                        for g in range(2):
                            i = mm(B[0][SLOTS * g:SLOTS * (g + 1), :], xeT[:, k % 4, k // 4, :], wgu[:, :, k, g * 256:(g + 1) * 256],
                                   start=(k == 0), stop=(k == KC - 1))
                    i.then_inc(t_h, 1)
                    pe.wait_ge(t_p2, T2)
                    gather().then_inc(t_xg, 1)
                    pe.wait_ge(t_act, T1)
                    for q in range(2):
                        i = tr(B[3][:, q * P:(q + 1) * P], actv[:, q * P:(q + 1) * P], ident)
                    i.then_inc(t_aTp, 1)
                    pe.wait_ge(t_xgs, T2)
                    gathered_T().then_inc(t_xeTp, 1)
                    pe.wait_ge(t_aTs, T1)
                    pe.wait_ge(d_dn[s], n_dn)
                    for f in range(4):
                        for g in range(2):
                            i = mm(B[1][SLOTS * g:SLOTS * (g + 1), :], actT[:, f % 2, f // 2, :], wdn[:, f, g * 512:(g + 1) * 512],
                                   start=(f == 0), stop=(f == 3))
                    i.then_inc(t_y, 1)
                    pe.wait_ge(t_pw, T1)
                    for t in range(NT):
                        i = tr(B[3][:, t * P:(t + 1) * P], Pw[:, t, :], ident)
                    i.then_inc(t_pwp, 1)
                    pe.wait_ge(t_ye, T1)
                    pe.wait_ge(t_pws, T1)
                    for t in range(NT):
                        if t != 1:
                            pe.wait_ge(t_add, add0 if t == 0 else add2)
                        for g in range(2):
                            i = mm(B[(4, 6, 4)[t] + g][:, :], PwT[SLOTS * g:SLOTS * (g + 1), t, :], ye[SLOTS * g:SLOTS * (g + 1), :],
                                   start=True, stop=True)
                        i.then_inc(t_comb, 1)

            with pe.Fori(0, NE // ESLOTS) as g:
                for s in range(ESLOTS):
                    expert(g * ESLOTS + s, s, g + 1)
            expert(NE - 1, (NE - 1) % ESLOTS, NE // ESLOTS + 1)

        @block.vector
        def _(v):
            ts, tt, cp, stt = nc.vector.tensor_scalar, nc.vector.tensor_tensor, nc.vector.tensor_copy, nc.vector.scalar_tensor_tensor

            def order(eng=v):
                eng.drain()

            def rsqrt(r, m, w):
                tt(w, r, r, ALU.mult)
                order()
                tt(w, w, m, ALU.mult)
                order()
                ts(w, w, -0.5, 1.5, ALU.mult, ALU.add)
                order()
                return tt(r, r, w, ALU.mult)

            v.wait_ge(*A.at("exp c"))
            ts(erow[0:16, :], erow[0:16, :], 1.0, None, ALU.add)
            order()
            nc.vector.reciprocal(erow[0:16, :], erow[0:16, :])
            order()
            tt(srow[0:16, :], vrow[0:16, :], erow[0:16, :], ALU.mult).then_inc(*V.mark("silu c"))
            v.wait_ge(*PE.at("vecT"))
            cp(g1T, B[0][:, 16:24])
            cp(qgT, B[0][:, 24:28])
            v.wait_ge(zero_done, 3)
            cp(c32[:, :, 0:2], B[0][:, 32:48].rearrange("p (r k) -> p k r", r=2)).then_inc(*V.mark("vec out"))
            v.wait_ge(*A.at("rsx"))
            ts(msx, ssx, EPS, None, ALU.add)
            order()
            rsqrt(rsx, msx, nwx)
            order()
            for t in range(NT):
                ts(x_sb[:, t, :], x_sb[:, t, :], rsx[:, t:t + 1], None, ALU.mult).then_inc(*V.mark(f"xn {t}"))
            v.wait_ge(*PE.at("mod0"))
            v.wait_ge(d_bmod, 32)
            tt(modrow, B[7][:, :], bmod[:, 0, :], ALU.add).then_inc(*V.mark("modrow 0"))
            v.wait_ge(*PE.at("modT"))
            mv = B[0][:, :].rearrange("p (i g x) -> p g i x", i=4, g=4)
            for r in range(2):
                cp(shT[:, r, :].rearrange("p (g i) -> p g i", g=2), mv[:, 0:2, :, r])
                i = stt(out=a1T[:, r, :].rearrange("p (g i) -> p g i", g=2), in0=mv[:, 2:4, :, r], scalar=1.0,
                        in1=g1T.rearrange("p (g i) -> p g i", g=2), op0=ALU.add, op1=ALU.mult)
            i.then_inc(*V.mark("mod cols"))
            order()
            cp(c32_late, c32)
            for t in range(NT):
                r = min(t, 1)
                for k in range(KC // 2):
                    i = ts(hT[:, k, t * P:(t + 1) * P], B[1 + 2 * t + k // 4][:, (k % 4) * P:(k % 4 + 1) * P],
                           a1T[:, r, k:k + 1], shT[:, r, k:k + 1], ALU.mult, ALU.add)
                i.then_inc(*V.mark(f"hT {t}"))

            def tok(t):
                b = 1 if t % 2 == 0 else 4
                v.wait_ge(*A.at(f"rs {t}"))
                if t == 0:
                    v.wait_ge(d_small, 80)
                ts(ms[:, 8:10], ss[:, 8:10], EPS, None, ALU.add)
                order()
                rsqrt(rs[:, 8:10], ms[:, 8:10], nw[:, 8:10]).then_inc(*V.mark(f"nr {t}"))
                order()
                v.wait_ge(*A.at(f"kpe {t}"))
                stt(out=ckv[:, t, :], in0=B[b + 1][:, 0:256], scalar=rs[:, 9:10], in1=kvg, op0=ALU.mult,
                    op1=ALU.mult).then_inc(*V.mark(f"ckv {t}"))

            def lora(r):
                v.wait_ge(*PE.at(f"T {r}"))
                if r != "c":
                    for k in range(4):
                        ts(qaT[:, k, r * P:(r + 1) * P], B[7][:, k * P:(k + 1) * P], qgT[:, k:k + 1], None, ALU.mult)
                cp(ckvT[:, :, ROW[r], :], B[0][:, 0:256].rearrange("p (k n) -> p k n", k=2)).then_inc(*V.mark(f"Tev {r}"))

            def k_in(r):
                v.wait_ge(*A.at(f"vv {r}"))
                if r != "c":
                    v.wait_ge(*PE.at("XK %s" % {0: "c", 1: 0, 2: 1}[r]))
                for half in range(2):
                    cp(kh[:, 4 * half:4 * half + 4, 0:NOPE], B[3 + half][:, :].rearrange("p (h n) -> p h n", h=4)[:, :, 0:NOPE])
                if r == "c":
                    v.wait_ge(d_cache, 32)
                else:
                    v.wait_ge(*A.at(f"kpe {r}"))
                cp(kh[:, :, NOPE:QKH], kpe[:, ROW[r], :].unsqueeze(1).to_broadcast([P, H, ROPE])).then_inc(*V.mark(f"kh {r}"))

            def head_norm(x, gain, t, rs_step, step):
                order()
                sqv = sq.rearrange("p (h n) -> p h n", h=H)
                tt(sqv, x, x, ALU.mult)
                order()
                nc.vector.tensor_reduce(ss[:, 0:8], sqv, AX.X, ALU.add)
                order()
                ts(ms[:, 0:8], ss[:, 0:8], 1.0 / QKH, EPS, ALU.mult, ALU.add).then_inc(*V.mark(rs_step))
                v.wait_ge(*A.at(rs_step))
                rsqrt(rs[:, 0:8], ms[:, 0:8], nw[:, 0:8])
                order()
                tt(x, x, rs[:, 0:8].unsqueeze(2).to_broadcast([P, H, QKH]), ALU.mult)
                order()
                i = tt(x, x, gain.unsqueeze(1).to_broadcast([P, H, QKH]), ALU.mult)
                if t in (1, 2):
                    order()
                    pe4 = x[:, :, NOPE:QKH].rearrange("p h (a b f) -> p h a b f", a=2, b=2)
                    x1, x2 = pe4[:, :, :, 0, :], pe4[:, :, :, 1, :]
                    c0 = (t - 1) * 16
                    cos = con[:, C_RC + c0:C_RC + c0 + 16].rearrange("p (a f) -> p a f", a=2).unsqueeze(1).to_broadcast([P, H, 2, 8])
                    sin = con[:, C_RS + c0:C_RS + c0 + 16].rearrange("p (a f) -> p a f", a=2).unsqueeze(1).to_broadcast([P, H, 2, 8])
                    r1, r2, r3, r4 = (sq[:, 128 * q:128 * q + 128].rearrange("p (h a f) -> p h a f", h=H, a=2) for q in range(4))
                    tt(r1, x1, cos, ALU.mult)
                    tt(r2, x2, sin, ALU.mult)
                    tt(r3, x1, sin, ALU.mult)
                    tt(r4, x2, cos, ALU.mult)
                    order()
                    tt(x1, r1, r2, ALU.subtract)
                    i = tt(x2, r3, r4, ALU.add)
                i.then_inc(*V.mark(step))

            def kn(r):
                head_norm(kh, kng, r, f"rk {r}", f"kn {r}")

            def qn(t):
                v.wait_ge(*A.at(f"qh {t}"))
                head_norm(qh, qng, t, f"rq {t}", f"qn {t}")

            does = {"tok": tok, "T": lora, "kh": k_in, "kn": kn, "qn": qn}
            for what, i in DVE_MIDDLE:
                does[what](i)

            def row_max(u):
                h, t = UNITS[u]
                v.wait_ge(*PE.at(f"S {u}"))
                nc.vector.tensor_reduce(mx[:, u % 2:u % 2 + 1], B[1 + u % 2][:, 0:P if t == 0 else 384], AX.X, ALU.max)
                order()
                ts(mx[:, 2 + u % 2:3 + u % 2], mx[:, u % 2:u % 2 + 1], -SCALE, None, ALU.mult).then_inc(*V.mark(f"mx {u}"))

            def normalise(u):
                h, t = UNITS[u]
                v.wait_ge(*A.at(f"p {u}"))
                nc.vector.reciprocal(ri[:, u % 2:u % 2 + 1], sm[:, u % 2:u % 2 + 1])
                order()
                pr = probs[:, u % 2, 0:P if t == 0 else 384]
                ts(pr, pr, ri[:, u % 2:u % 2 + 1], None, ALU.mult).then_inc(*V.mark(f"pn {u}"))

            def filled(n):
                kind, c = FILLERS[n]
                if kind == "mod":
                    v.wait_ge(*PE.at(f"fill mod {c}"))
                    if c == 2:
                        v.wait_ge(d_mod1, 32)
                    tt(modrow, B[7 if n % 2 == 0 else 0][:, :], bmod[:, c, :], ALU.add).then_inc(*V.mark(f"modrow {c}"))
                else:
                    v.wait_ge(*A.at(f"ge {c}"))
                    ts(gates[:, c, :], gates[:, c, :], 1.0, None, ALU.add)
                    order()
                    nc.vector.reciprocal(gates[:, c, :], gates[:, c, :])

            def pair_out(pair):
                v.wait_ge(*PE.at(f"PV {6 * pair + 5}"))
                cp(oT[:, pair, :], B[5 + pair % 2][:, 0:NTOK]).then_inc(*V.mark(f"oT {pair}"))

            row_max(0)
            for u in range(len(UNITS)):
                normalise(u)
                if u + 1 < len(UNITS):
                    row_max(u + 1)
                if 1 <= u <= len(FILLERS):
                    filled(u - 1)
                if u and u % 6 == 0:
                    pair_out(u // 6 - 1)
            pair_out(3)
            for c in range(KC):
                v.wait_ge(*PE.at(f"AF {c}"))
                order()
                tt(uT[:, c, :], B[1 + c % 2][:, 0:NTOK], gates[:, c, :], ALU.mult)
                tt(otmp[:, 0:NTOK], B[3 + c % 2][:, 0:NTOK], gates[:, 8 + c, :], ALU.mult)
                order()
                tt(uT[:, c, :], uT[:, c, :], otmp[:, 0:NTOK], ALU.add).then_inc(*V.mark(f"u {c}"))
            v.wait_ge(d_bc, 9 * 16)
            for r in range(2):
                stt(out=bc[:, 2, r, :], in0=bc[:, 2, r, :], scalar=1.0, in1=g2b, op0=ALU.add, op1=ALU.mult)
            v.wait_ge(d_xre, 32)
            for t in range(NT):
                r = min(t, 1)
                v.wait_ge(*PE.at(f"out {t}"))
                order()
                for half in range(2):
                    o = slice(half * 512, half * 512 + 512)
                    tt(otmp[:, o], B[((5, 6), (7, 0), (5, 6))[t][half]][:, :], bc[:, 0, r, o], ALU.mult)
                order()
                tt(x_sb[:, t, :], x_sb[:, t, :], otmp[:, :], ALU.add).then_inc(*V.mark(f"x1 {t}"))
                v.wait_ge(*A.at(f"rs2 {t}"))
                c = slice(t, t + 1)
                ts(msx[:, c], ssx[:, c], EPS, None, ALU.add)
                order()
                rsqrt(rsx[:, c], msx[:, c], nwx[:, c])
                order()
                stt(out=h2[:, t, :], in0=x_sb[:, t, :], scalar=rsx[:, c], in1=bc[:, 2, r, :], op0=ALU.mult, op1=ALU.mult)
                order()
                tt(h2[:, t, :], h2[:, t, :], bc[:, 1, r, :], ALU.add).then_inc(*V.mark(f"h2 {t}"))

            def b4(x):
                return x.unsqueeze(2).to_broadcast([P, NT, 4])
            desc = con[:, C_DESC:C_DESC + 4].unsqueeze(1).to_broadcast([P, NT, 4])

            def first_max(out, x, m):
                nc.vector.tensor_reduce(m, x, AX.X, ALU.max)
                order()
                tt(t4, x, b4(m), ALU.is_ge)
                order()
                tt(t4, t4, desc, ALU.mult)
                order()
                nc.vector.tensor_reduce(rr, t4, AX.X, ALU.max)
                order()
                tt(out, t4, b4(rr), ALU.is_equal)
                order()

            v.wait_ge(*PE.at("router"))
            nc.vector.memset(work[:, 0:3072], 0.0).then_inc(t_add, 3)
            tt(lg, B[7][:, 0:96].rearrange("p (t n) -> p t n", t=NT)[:, :, 0:20], rb.unsqueeze(1).to_broadcast([P, NT, 20]), ALU.add)
            order()
            first_max(ohg, lg[:, :, 0:4], rm)
            tt(e2, lg[:, :, 0:4], b4(rm), ALU.subtract).then_inc(*V.mark("gmax"))
            tt(prod, lg[:, :, 4:20].rearrange("p t (g e) -> p t g e", g=4), ohg.unsqueeze(3).to_broadcast([P, NT, 4, 4]), ALU.mult)
            order()
            nc.vector.tensor_reduce(esel, prod.rearrange("p t g e -> p t e g"), AX.X, ALU.add)
            order()
            first_max(oh1, esel, rm1)
            v.wait_ge(*A.at("gexp"))
            nc.vector.tensor_reduce(rsum, e2, AX.X, ALU.add)
            order()
            nc.vector.reciprocal(gp, rsum)
            stt(out=e2, in0=oh1, scalar=-1e38, in1=esel, op0=ALU.mult, op1=ALU.add)
            order()
            first_max(oh2, e2, rm2)
            tt(rd, rm2, rm1, ALU.subtract).then_inc(*V.mark("top2"))
            for m, oh in ((M1, oh1), (M2, oh2)):
                tt(m.rearrange("p t (g e) -> p t g e", g=4), ohg.unsqueeze(3).to_broadcast([P, NT, 4, 4]),
                   oh.unsqueeze(2).to_broadcast([P, NT, 4, 4]), ALU.mult)
            order()
            tt(MM, M1, M2, ALU.add).then_inc(*V.mark("masks"))
            v.wait_ge(*A.at("dexp"))
            ts(rr, rd, 1.0, None, ALU.add)
            order()
            nc.vector.reciprocal(rr, rr)
            order()
            tt(wsl[:, :, 0], rr, gp, ALU.mult)
            order()
            tt(wsl[:, :, 1], wsl[:, :, 0], rd, ALU.mult)
            v.wait_ge(*PE.at("rank"))
            cp(cnt, B[0][:, 48:64])
            nc.vector.memset(ntf, 1.0)
            order()
            for k in range(1, MAX_TILES):
                stt(out=ntf, in0=cnt, scalar=float(SLOTS * k), in1=ntf, op0=ALU.is_gt, op1=ALU.add)
                order()
            nc.vector.memset(cA[:, 0:1], 0.0)
            cp(cA[:, 1:17], ntf)
            nc.vector.memset(cB[:, 0:1], 0.0)
            order()
            src, dst = cA, cB
            for sh in (1, 2, 4, 8):
                cp(dst[:, 1:1 + sh], src[:, 1:1 + sh])
                tt(dst[:, 1 + sh:17], src[:, 1 + sh:17], src[:, 1:17 - sh], ALU.add)
                order()
                src, dst = dst, src
            cp(tab[0:1, 0:16], ntf[0:1, :])
            cp(tab[0:1, 16:33], src[0:1, :]).then_inc(*V.mark("tab"))
            stt(out=slot, in0=src[:, 0:16].unsqueeze(1).to_broadcast([P, NT, 16]), scalar=float(SLOTS),
                in1=B[0][:, 0:48].rearrange("p (t n) -> p t n", t=NT), op0=ALU.mult, op1=ALU.add)
            order()
            for c, m in enumerate((M1, M2)):
                tt(tmp48, slot, m, ALU.mult)
                order()
                nc.vector.tensor_reduce(fsl[:, :, c], tmp48, AX.X, ALU.add)
                order()

            def onehot():
                for t in range(NT):
                    ts(P2[:, t, 0:SLOTS], iota[:, 0:SLOTS], fsl[:, t, 0:1], None, ALU.is_equal)
                order()
                for t in range(NT):
                    i = stt(out=P2[:, t, 0:SLOTS], in0=iota[:, 0:SLOTS], scalar=fsl[:, t, 1:2], in1=P2[:, t, 0:SLOTS],
                            op0=ALU.is_equal, op1=ALU.add)
                return i

            onehot().then_inc(t_p2, 1)

            def expert(e, s, n):
                first = v.value_load(tab[0:1, bass.ds(16 + e, 1)], min_val=0, max_val=ALL_TILES)
                tiles = v.value_load(tab[0:1, bass.ds(e, 1)], min_val=1, max_val=MAX_TILES)
                with v.Fori(0, tiles) as j:
                    T1 = v.snap(first + j + 1)
                    C = [v.snap((first + j) * 3 + (t + 1)) for t in range(NT)]
                    for t in range(NT):
                        ts(Pw[:, t, :], iota, fsl[:, t, 0:1], wsl[:, t, 0:1], ALU.is_equal, ALU.mult)
                        ts(ptmp[:, t, :], iota, fsl[:, t, 1:2], wsl[:, t, 1:2], ALU.is_equal, ALU.mult)
                    order()
                    tt(Pw, Pw, ptmp, ALU.add).then_inc(t_pw, 1)
                    ts(fsl, fsl, -float(SLOTS), None, ALU.add)
                    order()
                    v.wait_ge(t_xg, T1)
                    onehot().then_inc(t_p2, 1)
                    v.wait_ge(t_exp, T1)
                    ts(eg, eg, 1.0, None, ALU.add)
                    order()
                    nc.vector.reciprocal(eg, eg)
                    order()
                    tt(eg, eg, B[0][:, 0:256], ALU.mult)
                    order()
                    tt(actv, eg, B[0][:, 256:512], ALU.mult).then_inc(t_act, 1)
                    v.wait_ge(t_y, T1)
                    cp(ye, B[1][:, :]).then_inc(t_ye, 1)
                    for t in range(NT):
                        v.wait_ge(t_comb, C[t])
                        for g in range(2):
                            i = tt(acc[:, t, g * 512:(g + 1) * 512], acc[:, t, g * 512:(g + 1) * 512],
                                   B[(4, 6, 4)[t] + g][:, :], ALU.add)
                        i.then_inc(t_add, 1)
                    order()

            with v.Fori(0, NE // ESLOTS) as g:
                for s in range(ESLOTS):
                    expert(g * ESLOTS + s, s, g + 1)
            expert(NE - 1, (NE - 1) % ESLOTS, NE // ESLOTS + 1)
            v.wait_ge(d_g5, 32)
            for t in range(NT):
                tt(acc[:, t, :], acc[:, t, :], g5[:, min(t, 1), :], ALU.mult)
                order()
                tt(acc[:, t, :], acc[:, t, :], x_sb[:, t, :], ALU.add).then_inc(fin, 1)

        @block.scalar
        def _(act):
            av = nc.scalar.activation

            def rsqrt0(out, mean, bias=0.0):
                av(out, mean, ACT.Ln, bias=bias)
                act.drain()
                return av(out, out, ACT.Exp, scale=-0.5)

            nc.scalar.preload_act_table_set("natural_log_exp_and_others")
            act.wait_ge(d_vec, 64)
            av(erow[0:16, :], vrow[0:16, :], ACT.Exp, scale=-1.0).then_inc(*A.mark("exp c"))
            act.wait_ge(zero_done, 3)
            for t in range(NT):
                act.wait_ge(d_x[t], 16)
                av(sqa, x_sb[:, t, :], ACT.Square, scale=D ** -0.5, accum_out=ssx[:, t:t + 1])
                act.drain()
            rsqrt0(rsx, ssx, epsc).then_inc(*A.mark("rsx"))
            act.wait_ge(*V.at("mod cols"))
            for t in range(NT):
                act.wait_ge(*PE.at(f"xT{t}"))
                r = min(t, 1)
                for k in range(KC // 2, KC):
                    i = av(hT[:, k, t * P:(t + 1) * P], B[1 + 2 * t + k // 4][:, (k % 4) * P:(k % 4 + 1) * P], ACT.Identity,
                           scale=a1T[:, r, k:k + 1], bias=shT[:, r, k:k + 1])
                i.then_inc(*A.mark(f"hT {t}"))

            def tok(t):
                b = 1 if t % 2 == 0 else 4
                act.wait_ge(*PE.at(f"tok {t}"))
                if t:
                    act.wait_ge(*V.at(f"ckv {t - 1}"))
                av(sqa[:, 0:512], B[b][:, :], ACT.Square, scale=Q_LORA ** -0.5, accum_out=ss[:, 8:9])
                av(sqa[:, 512:768], B[b + 1][:, 0:256], ACT.Square, scale=KV_LORA ** -0.5, accum_out=ss[:, 9:10])
                act.drain()
                rsqrt0(rs[:, 8:10], ss[:, 8:10], epsc).then_inc(*A.mark(f"rs {t}"))
                av(kpe[:, t, :], B[b + 1][:, 256:288], ACT.Copy).then_inc(*A.mark(f"kpe {t}"))
                av(fn[:, t, :], B[b + 2][:, :], ACT.Copy).then_inc(*A.mark(f"fn {t}"))
                act.wait_ge(*V.at(f"nr {t}"))
                if t == 2:
                    act.wait_ge(*PE.at("T 0"))
                av(qan[:, t % 2, :], B[b][:, :], ACT.Copy, scale=rs[:, 8:9]).then_inc(*A.mark(f"qan {t}"))

            def values(r):
                act.wait_ge(*PE.at(f"KV {r}"))
                for half in range(2):
                    i = av(vv[:, KSLOT[r], half * 256:(half + 1) * 256].rearrange("p (h n) -> p h n", h=4),
                           B[3 + half][:, :].rearrange("p (h n) -> p h n", h=4)[:, :, NOPE:128], ACT.Copy)
                i.then_inc(*A.mark(f"vv {r}"))

            def rstart(name):
                act.wait_ge(*V.at(name))
                rsqrt0(rs[:, 0:8], ms[:, 0:8]).then_inc(*A.mark(name))

            def q_in(t):
                act.wait_ge(*PE.at(f"QB {t}"))
                if t:
                    act.wait_ge(*PE.at(f"XQ {t - 1}"))
                for half in range(2):
                    i = av(qh[:, 4 * half:4 * half + 4, :], B[1 + half][:, 0:384].rearrange("p (h n) -> p h n", h=4), ACT.Copy)
                i.then_inc(*A.mark(f"qh {t}"))

            def heads_out(dst, lo, pstep, step):
                act.wait_ge(*PE.at(pstep))
                for half in range(2):
                    i = av(dst[0:QKH, 4 * half:4 * half + 4, lo:lo + P], B[5 + half][0:QKH, :].rearrange("p (h n) -> p h n", h=4), ACT.Copy)
                i.then_inc(*A.mark(step))

            def fourier_seq(g):
                bl, bx = (B[5], B[6]) if g < 2 else (B[7], B[0])
                act.wait_ge(*PE.at(f"FA {g}"))
                av(fA[:, g, 0:512], bl[:, :], ACT.Copy)
                av(fA[:, g, 512:768], bx[:, 0:256], ACT.Copy).then_inc(*A.mark(f"fA {g}"))

            def fourier_ch(part):
                act.wait_ge(*PE.at(f"FB {part}"))
                if part == 0:
                    for pair in range(2):
                        i = av(yT[:, 2 * pair:2 * pair + 2, P:NTOK], (B[7], B[0])[pair][:, :].rearrange("p (g n) -> p g n", g=2), ACT.Copy)
                else:
                    i = av(yT[:, :, 0:P], B[7][:, :].rearrange("p (g n) -> p g n", g=4), ACT.Copy)
                i.then_inc(*A.mark(f"yT {part}"))

            does = {"tok": tok, "vv": values, "rk": lambda r: rstart(f"rk {r}"), "rq": lambda t: rstart(f"rq {t}"), "qh": q_in,
                    "kT": lambda r: heads_out(kT, KSLOT[r] * P, f"XK {r}", f"kT {r}"),
                    "qT": lambda t: heads_out(qT, t * P, f"XQ {t}", f"qT {t}"), "fA": fourier_seq, "yT": fourier_ch}
            for what, i in ACT_MIDDLE:
                does[what](i)

            def exps(u):
                h, t = UNITS[u]
                act.wait_ge(*V.at(f"mx {u}"))
                if u >= 2:
                    act.wait_ge(*PE.at(f"PT {u - 2}"))
                n = P if t == 0 else 384
                av(probs[:, u % 2, 0:n], B[1 + u % 2][:, 0:n], ACT.Exp, scale=SCALE, bias=mx[:, 2 + u % 2:3 + u % 2],
                   accum_out=sm[:, u % 2:u % 2 + 1])
                act.drain().then_inc(*A.mark(f"p {u}"))

            exps(0)
            for u in range(len(UNITS)):
                if u + 1 < len(UNITS):
                    exps(u + 1)
                if u < len(FILLERS) and FILLERS[u][0] == "g":
                    c = FILLERS[u][1]
                    act.wait_ge(*PE.at(f"fill g {c}"))
                    av(gates[:, c, :], B[7 if u % 2 == 0 else 0][:, 0:NTOK], ACT.Exp, scale=-1.0).then_inc(*A.mark(f"ge {c}"))
                act.wait_ge(*PE.at(f"PT {u}"))
                if u >= 2:
                    act.wait_ge(*PE.at(f"PV {u - 2}"))
                n = P if UNITS[u][1] == 0 else 384
                av(pT[:, u % 2, 0:n], B[3 + u % 2][:, 0:n], ACT.Copy).then_inc(*A.mark(f"pT {u}"))

            def h2T_out(t):
                act.wait_ge(*PE.at(f"h2T {t}"))
                b = 1 if t % 2 == 0 else 3
                for half in range(2):
                    i = av(h2T[:, 4 * half:4 * half + 4, t * P:(t + 1) * P], B[b + half][:, :].rearrange("p (k n) -> p k n", k=4), ACT.Copy)
                i.then_inc(*A.mark(f"h2T {t}"))

            for t in range(NT):
                act.wait_ge(*V.at(f"x1 {t}"))
                av(junk, x_sb[:, t, :], ACT.Square, scale=D ** -0.5, accum_out=ssx[:, t:t + 1])
                act.drain()
                rsqrt0(rsx[:, t:t + 1], ssx[:, t:t + 1], epsc).then_inc(*A.mark(f"rs2 {t}"))
                if t:
                    h2T_out(t - 1)
            h2T_out(2)
            act.wait_ge(*V.at("gmax"))
            av(e2, e2, ACT.Exp).then_inc(*A.mark("gexp"))
            act.wait_ge(*V.at("top2"))
            av(rd, rd, ACT.Exp).then_inc(*A.mark("dexp"))

            def gathered():
                return av(xg, B[1][:, :], ACT.Copy)

            def gathered_T():
                return av(xeT, B[2][:, :].rearrange("p (i g s) -> p i g s", i=4, g=2), ACT.Copy)

            act.wait_ge(t_xg, 1)
            gathered().then_inc(t_xgs, 1)
            act.wait_ge(t_xeTp, 1)
            gathered_T().then_inc(t_xeTs, 1)
            act.wait_ge(*V.at("tab"))

            def expert(e, s, n):
                first = act.value_load(tab[0:1, bass.ds(16 + e, 1)], min_val=0, max_val=ALL_TILES)
                tiles = act.value_load(tab[0:1, bass.ds(e, 1)], min_val=1, max_val=MAX_TILES)
                with act.Fori(0, tiles) as j:
                    T1, T2 = act.snap(first + j + 1), act.snap(first + j + 2)
                    act.wait_ge(t_h, T1)
                    av(eg, B[0][:, 0:256], ACT.Exp, scale=-1.0).then_inc(t_exp, 1)
                    act.wait_ge(t_xg, T2)
                    gathered().then_inc(t_xgs, 1)
                    act.wait_ge(t_aTp, T1)
                    av(actT, B[3][:, 0:256].rearrange("p (j g s) -> p j g s", j=2, g=2), ACT.Copy).then_inc(t_aTs, 1)
                    act.wait_ge(t_xeTp, T2)
                    gathered_T().then_inc(t_xeTs, 1)
                    act.wait_ge(t_pwp, T1)
                    av(PwT, B[3][:, 0:384].rearrange("p (t n) -> p t n", t=NT), ACT.Copy).then_inc(t_pws, 1)

            with act.Fori(0, NE // ESLOTS) as g:
                for s in range(ESLOTS):
                    expert(g * ESLOTS + s, s, g + 1)
            expert(NE - 1, (NE - 1) % ESLOTS, NE // ESLOTS + 1)


INS = ["x_prompt", "x_sample", "cache_ckv", "cache_kpe", "c", "c_ctx", "w_mod", "b_mod", "norm1_g", "w_in", "q_a_norm_g", "w_q_b",
       "kv_a_norm_g", "w_kv_b", "q_norm_g", "k_norm_g", "w_attn_o", "w_fnet", "w_out", "norm2_g", "w_router_group",
       "b_router_group", "w_router_expert", "b_router_expert", "w_exp_gate", "w_exp_up", "w_exp_down"]
OUTS = [("y_prompt", (1, P, D)), ("y_sample", (1, 2 * P, D)), ("new_ckv", (1, 1, P, KV_LORA)), ("new_kpe", (1, 1, P, ROPE))]


def kernel(**inputs):
    import concourse.bacc as bacc
    from concourse.bass_utils import run_bass_kernel_spmd

    nc = bacc.Bacc("TRN2", target_bir_lowering=False, num_devices=1)
    arrays, aps = {}, {}
    for name in INS:
        x = np.ascontiguousarray(inputs[name])
        arrays[f"in_{name}"] = x
        aps[name] = nc.dram_tensor(f"in_{name}", x.shape, mybir.dt.from_np(x.dtype), kind="ExternalInput").ap()
    arrays["in_const_table"] = constants()
    aps["const_table"] = nc.dram_tensor("in_const_table", (P, NCON), F32, kind="ExternalInput").ap()
    for name, shape in OUTS:
        aps[name] = nc.dram_tensor(f"out_{name}", shape, F32, kind="ExternalOutput").ap()
    program(nc, aps)
    r = run_bass_kernel_spmd(nc, [arrays], core_ids=[0])
    return tuple(r.results[0][f"out_{name}"] for name, _ in OUTS)
```

```python
from contextlib import ExitStack

import numpy as np
import concourse.bass as bass
from concourse import mybir

F32 = mybir.dt.float32
I32 = mybir.dt.int32
ALU = mybir.AluOpType
ACT = mybir.ActivationFunctionType
AX = mybir.AxisListType

P = 128
D = 1024
KC = D // P
NT = 3
NTOK = NT * P
Q_LORA, KV_LORA, ROPE, NOPE, VH, H = 512, 256, 32, 64, 64, 8
QKH = NOPE + ROPE
FNW, FG = 512, 4
TOKW = Q_LORA + KV_LORA + ROPE + FNW
GATE0 = TOKW
GRID_W = 64
NG, EPG = 4, 4
NE = NG * EPG
DE = 512
EPS = 1e-6
SCALE = QKH ** -0.5
SLOTS = 64
MAX_TILES = NTOK // SLOTS
ALL_TILES = NE + 2 * NTOK // SLOTS
SLOT_ROWS = -(-(ALL_TILES + 1) * SLOTS // P) * P
PIECE = 4096
RING1 = 4
ESLOTS = 3

C_ID, C_ONE, C_TRI, C_IOTA, C_FC, C_FS = 0, 128, 256, 384, 512, 640
C_SL, C_SC, C_RC, C_RS, C_DESC = 768, 1792, 2048, 2080, 2112
NCON = 2128


def constants():
    t = np.zeros((P, NCON), np.float64)
    i = np.arange(P)
    t[:, C_ID:C_ID + P] = np.eye(P)
    t[:, C_ONE:C_ONE + P] = 1.0
    t[:, C_TRI:C_TRI + P] = i[:, None] < i[None, :]
    t[:, C_IOTA:C_IOTA + P] = (i % SLOTS)[None, :]
    ang = 2 * np.pi * np.outer(i, i) / P
    t[:, C_FC:C_FC + P] = np.cos(ang) / np.sqrt(P)
    t[:, C_FS:C_FS + P] = -np.sin(ang) / np.sqrt(P)
    s = 2 * P
    for ch in range(2):
        a = 2 * np.pi * (np.outer(i + ch * P, np.arange(s)) % s) / s
        t[:, C_SL + ch * 512:C_SL + ch * 512 + 256] = np.cos(a) / np.sqrt(s)
        t[:, C_SL + ch * 512 + 256:C_SL + ch * 512 + 512] = np.sin(a) / np.sqrt(s)
    t[:, C_SC:C_SC + P] = np.cos(ang) / np.sqrt(P)
    t[:, C_SC + P:C_SC + 2 * P] = np.sin(ang) / np.sqrt(P)
    freqs = np.float32(10000.0) ** (-np.arange(8, dtype=np.float32) / np.float32(8))
    for tt in range(2):
        pos = i + tt * P
        for ax, q in enumerate((pos // GRID_W, pos % GRID_W)):
            a = (q.astype(np.float32)[:, None] * freqs[None, :]).astype(np.float32).astype(np.float64)
            t[:, C_RC + tt * 16 + ax * 8:C_RC + tt * 16 + ax * 8 + 8] = np.cos(a)
            t[:, C_RS + tt * 16 + ax * 8:C_RS + tt * 16 + ax * 8 + 8] = np.sin(a)
    t[:, C_DESC:C_DESC + 16] = np.tile(np.arange(4, 0, -1), 4)[None, :]
    return t.astype(np.float32)


class Steps:

    def __init__(self, sem, names):
        self.sem, self.names, self.count = sem, names, 0
        self.value = {n: i + 1 for i, n in enumerate(names)}
        assert len(self.value) == len(names)

    def at(self, name):
        return self.sem, self.value[name]

    def mark(self, name):
        assert self.names[self.count] == name, (name, self.names[self.count])
        self.count += 1
        return self.sem, 1


FILLERS = [("g", 0), ("g", 1), ("g", 2), ("g", 3), ("mod", 1), ("g", 8), ("g", 9), ("g", 10), ("g", 11), ("mod", 2),
           ("g", 4), ("g", 5), ("g", 6), ("g", 7), ("g", 12), ("g", 13), ("g", 14), ("g", 15)]
UNITS = [(h, t) for h in range(H) for t in range(NT)]
MIDDLE = [("tok", 0), ("T", "c"), ("tok", 1), ("T", 0), ("tok", 2), ("KV", "c"), ("T", 1), ("FA", 0), ("FA", 1),
          ("KV", 0), ("XK", "c"), ("QB", 0), ("T", 2), ("FA", 2), ("XK", 0), ("KV", 1), ("FA", 3), ("XQ", 0),
          ("QB", 1), ("XK", 1), ("KV", 2), ("FB", 0), ("XQ", 1), ("QB", 2), ("XK", 2), ("FB", 1), ("XQ", 2)]
ROW = {"c": 3, 0: 0, 1: 1, 2: 2}
KSLOT = {"c": 0, 1: 1, 2: 2, 0: 3}


DVE_MIDDLE = [("tok", 0), ("T", "c"), ("tok", 1), ("T", 0), ("tok", 2), ("kh", "c"), ("T", 1), ("kn", "c"),
              ("kh", 0), ("kn", 0), ("T", 2), ("qn", 0), ("kh", 1), ("kn", 1), ("qn", 1), ("kh", 2), ("kn", 2), ("qn", 2)]
ACT_MIDDLE = [("tok", 0), ("tok", 1), ("tok", 2), ("vv", "c"), ("rk", "c"), ("fA", 0), ("fA", 1), ("vv", 0), ("rk", 0),
              ("kT", "c"), ("qh", 0), ("rq", 0), ("fA", 2), ("kT", 0), ("vv", 1), ("rk", 1), ("fA", 3), ("qT", 0),
              ("qh", 1), ("rq", 1), ("kT", 1), ("vv", 2), ("rk", 2), ("yT", 0), ("qT", 1), ("qh", 2), ("rq", 2),
              ("kT", 2), ("yT", 1), ("qT", 2)]


def pe_steps():
    s = ["vecT"] + [f"xT{t}" for t in range(NT)] + ["mod0", "modT"]
    s += [f"{k} {i}" for k, i in MIDDLE]
    s += ["S 0"]
    for u in range(len(UNITS)):
        if u + 1 < len(UNITS):
            s.append(f"S {u + 1}")
        if u < len(FILLERS):
            s.append("fill %s %d" % FILLERS[u])
        s.append(f"PT {u}")
        if u:
            s.append(f"PV {u - 1}")
    s += [f"PV {len(UNITS) - 1}"]
    s += [f"AF {c}" for c in range(KC)] + [f"out {t}" for t in range(NT)]
    s += [f"h2T {t}" for t in range(NT)] + ["router", "rank"]
    return s


def dve_order():
    s = ["silu c", "vec out"] + [f"xn {t}" for t in range(NT)] + ["modrow 0", "mod cols"]
    s += [f"hT {t}" for t in range(NT)]
    for what, i in DVE_MIDDLE:
        s += [n % i for n in {"tok": ["nr %s", "ckv %s"], "T": ["Tev %s"], "kh": ["kh %s"], "kn": ["rk %s", "kn %s"],
                              "qn": ["rq %s", "qn %s"]}[what]]
    s += ["mx 0"]
    for u in range(len(UNITS)):
        s.append(f"pn {u}")
        if u + 1 < len(UNITS):
            s.append(f"mx {u + 1}")
        if 1 <= u <= len(FILLERS) and FILLERS[u - 1][0] == "mod":
            s.append("modrow %d" % FILLERS[u - 1][1])
        if u and u % 6 == 0:
            s.append(f"oT {u // 6 - 1}")
    s += ["oT 3"] + [f"u {c}" for c in range(KC)]
    for t in range(NT):
        s += [f"x1 {t}", f"h2 {t}"]
    return s + ["gmax", "top2", "masks", "tab", "slots"]


def act_order():
    s = ["exp c", "rsx", *(f"hT {t}" for t in range(NT))]
    for what, i in ACT_MIDDLE:
        s += [n % i for n in {"tok": ["rs %s", "kpe %s", "fn %s", "qan %s"], "vv": ["vv %s"], "rk": ["rk %s"],
                              "qh": ["qh %s"], "rq": ["rq %s"], "kT": ["kT %s"], "qT": ["qT %s"], "fA": ["fA %s"],
                              "yT": ["yT %s"]}[what]]
    s += ["p 0"]
    for u in range(len(UNITS)):
        if u + 1 < len(UNITS):
            s.append(f"p {u + 1}")
        if u < len(FILLERS) and FILLERS[u][0] == "g":
            s.append("ge %d" % FILLERS[u][1])
        s.append(f"pT {u}")
    for t in range(NT):
        s += [f"rs2 {t}"]
        if t:
            s.append(f"h2T {t - 1}")
    return s + ["h2T 2", "gexp", "dexp"]


def program(nc, a):
    ctx = ExitStack()
    with ctx:
        def sb(name, shape, dt=F32):
            return ctx.enter_context(nc.sbuf_tensor(name, shape, dt))

        def sem(name):
            return ctx.enter_context(nc.semaphore(name))

        con = sb("con", [P, NCON])
        x_sb = sb("x_sb", [P, NT, D])
        hT = sb("hT", [P, KC, NTOK])
        work = sb("work", [P, 5632])
        yTt = sb("yTt", [P, 1536])
        big = sb("big", [P, 9 * PIECE])
        small = sb("small", [P, 720])
        tab = sb("tab", [1, 67], I32)
        sidx = sb("sidx", [P, 6], I32)

        ident, ones = con[:, C_ID:C_ID + P], con[:, C_ONE:C_ONE + P]
        tri, iota = con[:, C_TRI:C_TRI + P], con[:, C_IOTA:C_IOTA + P]
        dft_c, dft_s = con[:, C_FC:C_FC + P], con[:, C_FS:C_FS + P]

        def piece(n):
            return big[:, n * PIECE:(n + 1) * PIECE]

        wqb = x_sb[:, :, :].rearrange("p a b -> p (a b)").rearrange("p (k n) -> p k n", k=4)
        vv = work[:, 0:2048].rearrange("p (s n) -> p s n", s=4)
        qaT = work[:, 2048:3584].rearrange("p (k n) -> p k n", k=4)
        ckvT = work[:, 3584:4608].rearrange("p (k r n) -> p k r n", k=2, r=4)
        ckv = work[:, 4608:5632].rearrange("p (r n) -> p r n", r=4)
        yT = yTt[:, :].rearrange("p (g n) -> p g n", g=4)
        misc = piece(4)
        wkvb = misc[:, 0:2048].rearrange("p (k n) -> p k n", k=2)
        bmod = misc[:, 2048:3584].rearrange("p (j n) -> p j n", j=3)
        modrow = misc[:, 3584:4096]
        A0 = 5 * PIECE
        gates = big[:, A0:A0 + 6144].rearrange("p (c n) -> p c n", c=16)
        qan = big[:, A0:A0 + 1024].rearrange("p (b n) -> p b n", b=2)
        fn = big[:, A0 + 1024:A0 + 2560].rearrange("p (t n) -> p t n", t=NT)
        qh = big[:, A0 + 2560:A0 + 3328].rearrange("p (h n) -> p h n", h=H)
        kh = big[:, A0 + 3328:A0 + 4096].rearrange("p (h n) -> p h n", h=H)
        sq = big[:, A0 + 4096:A0 + 4864]
        sqa = big[:, A0 + 4864:A0 + 5888]
        qT = big[:, A0 + 6144:A0 + 9216].rearrange("p (h n) -> p h n", h=H)
        uT = qT
        kT = big[:, A0 + 9216:A0 + 13312].rearrange("p (h n) -> p h n", h=H)
        fA = big[:, A0 + 13312:A0 + 16384].rearrange("p (g n) -> p g n", g=4)
        c32 = big[:, A0 + 13312:A0 + 13568].rearrange("p (k m) -> p k m", k=KC)
        c32_late = bmod[:, 0, 0:256].rearrange("p (k m) -> p k m", k=KC)
        vrow = big[:, A0 + 13568:A0 + 13696]
        srow = big[:, A0 + 13696:A0 + 13824]
        erow = big[:, A0 + 13824:A0 + 13952]
        probs = big[:, A0 + 13312:A0 + 14080].rearrange("p (b n) -> p b n", b=2)
        pT = big[:, A0 + 14080:A0 + 14848].rearrange("p (b n) -> p b n", b=2)
        oT = big[:, A0 + 14848:A0 + 16384].rearrange("p (c n) -> p c n", c=4)
        bc = big[:, A0:A0 + 6144].rearrange("p (v r n) -> p v r n", v=3, r=2)
        g2b = big[:, A0 + 9216:A0 + 10240]
        otmp = big[:, A0 + 10240:A0 + 11264]
        junk = big[:, A0 + 11424:A0 + 12448]
        g5 = piece(5)[:, 0:2048].rearrange("p (r n) -> p r n", r=2)
        wr = big[:, A0 + 11264:A0 + 11424].rearrange("p (k n) -> p k n", k=KC)
        h2T = big[:, A0 + 13312:A0 + 16384].rearrange("p (k n) -> p k n", k=KC)
        h2 = hT[:, :, :].rearrange("p a b -> p (a b)").rearrange("p (t n) -> p t n", t=NT)
        ybuf = big[:, 3 * PIECE:3 * PIECE + 6144].rearrange("p (t c n) -> p t c n", t=NT, c=2)
        xg = work[:, 0:3072].rearrange("p (s j n) -> p s j n", s=ESLOTS, j=2)
        xeT = work[:, 3072:3584].rearrange("p (i g s) -> p i g s", i=4, g=2)
        eg = work[:, 3584:3840]
        actv = work[:, 3840:4096]
        actT = work[:, 4096:4352].rearrange("p (j g s) -> p j g s", j=2, g=2)
        ye = hT[:, :, :].rearrange("p a b -> p (a b)").rearrange("p (s n) -> p s n", n=512)

        off = [0]

        def take(n):
            v = small[:, off[0]:off[0] + n]
            off[0] += n
            return v
        kvg, qng, kng, rb = take(256), take(96), take(96), take(20)
        g1T, qgT, shT, a1T = take(8), take(4), take(16), take(16)
        kpe = take(128).rearrange("p (r n) -> p r n", r=4)
        ssx, msx, rsx, nwx = take(3), take(3), take(3), take(3)
        ss, ms, rs, nw = take(10), take(10), take(10), take(10)
        mx, sm, ri = take(4), take(4), take(4)
        epsc = take(1)
        fsl = take(6).rearrange("p (t c) -> p t c", t=NT)
        wsl = take(6).rearrange("p (t c) -> p t c", t=NT)
        shT = shT.rearrange("p (r k) -> p r k", r=2)
        a1T = a1T.rearrange("p (r k) -> p r k", r=2)
        ro = [4352]

        def rtake(n, pat=None, **kw):
            v = work[:, ro[0]:ro[0] + n]
            ro[0] += n
            return v.rearrange(pat, **kw) if pat else v
        lg = rtake(60, "p (t n) -> p t n", t=NT)
        rm, rsum, gp, rm1, rm2, rd, rr = (rtake(3) for _ in range(7))
        t4, ohg, esel, oh1, oh2, e2 = (rtake(12, "p (t n) -> p t n", t=NT) for _ in range(6))
        prod = rtake(48, "p (t g e) -> p t g e", t=NT, g=4)
        M1, M2, MM, slot, tmp48 = (rtake(48, "p (t n) -> p t n", t=NT) for _ in range(5))
        cnt, nt2 = rtake(16), rtake(48, "p (v n) -> p v n", v=3)
        cA, cB = (rtake(51, "p (v n) -> p v n", v=3) for _ in range(2))

        B = [ctx.enter_context(nc.psum_tensor(f"bank{i}", [P, 512], F32)) for i in range(8)]
        modd = nc.dram_tensor("mod_rows", (2, 4096), F32, kind="Internal").ap()
        slots = nc.dram_tensor("slots", (SLOT_ROWS, D), F32, kind="Internal").ap()

        pe_done, v_done, a_done = sem("pe_done"), sem("dve_done"), sem("act_done")
        PE = Steps(pe_done, pe_steps())
        V = Steps(v_done, dve_order())
        A = Steps(a_done, act_order())
        zero_done = sem("zero_done")
        d_vec, d_con, d_small, d_cache, d_kvb, d_qb, d_bmod = map(sem, ("d_vec", "d_con", "d_small", "d_cache", "d_kvb", "d_qb", "d_bmod"))
        d_x = [sem(f"d_x{t}") for t in range(NT)]
        d_xre, d_mod1, d_mod2, d_bc, d_g5, d_out, d_outc = map(sem, ("d_xre", "d_mod1", "d_mod2", "d_bc", "d_g5", "d_out", "d_outc"))
        d_ring = [sem(f"d_ring{i}") for i in range(RING1)]
        d_gu = [sem(f"d_gu{s}") for s in range(ESLOTS)]
        d_dn = [sem(f"d_dn{s}") for s in range(ESLOTS)]
        d_scat, d_xmore, d_ymore = map(sem, ("d_scatter", "d_xg_more", "d_y_more"))
        d_xg = [sem(f"d_xg{s}") for s in range(ESLOTS)]
        d_y0 = [sem(f"d_y_slot{s}") for s in range(ESLOTS)]
        d_gath = [sem(f"d_gather{t}") for t in range(NT)]
        all_stored = sem("all_stored")
        t_g, t_u, t_xeTp, t_xeTs = map(sem, ("t_gate", "t_up", "t_xeT_psum", "t_xeT_sbuf"))
        t_exp, t_act, t_aTp, t_aTs, t_y, t_ye = map(sem, ("t_exp", "t_act", "t_actT_psum", "t_actT_sbuf", "t_down", "t_y_sbuf"))
        fin = sem("y_ready")

        win = a["w_in"][0].rearrange("(k p) n -> p k n", p=P)
        wmod = a["w_mod"][0].rearrange("(k p) n -> p k n", p=P)
        TOKK = [(0, 3), (3, 6), (6, 8)]
        ring, n = {}, 0
        order = [("mod0", q) for q in range(4)] + [("tokw", q) for q in range(3)] + [("gate", 0)]
        order += [("mod1", q) for q in range(4)] + [("gate", 1)] + [("mod2", q) for q in range(4)]
        order += [("gate", 2), ("gate", 3), ("attn_o", 0), ("fnet", 0), ("out", 0), ("out", 1)]
        for n, key in enumerate(order):
            ring[key] = (n % RING1, n // RING1 + 1)

        def arrived(eng, key):
            s, k = ring[key]
            eng.wait_ge(d_ring[s], 16 * k)

        def rpiece(key, width):
            s = ring[key][0]
            return big[:, s * PIECE:s * PIECE + (PIECE // width) * width].rearrange("p (k n) -> p k n", n=width)

        used = {("mod0", q): "mod0" for q in range(4)}
        used |= {("tokw", q): "tok 2" for q in range(3)}
        used |= {("mod1", q): "fill mod 1" for q in range(4)} | {("mod2", q): "fill mod 2" for q in range(4)}
        GCH = {0: [0, 1, 2, 3], 1: [8, 9, 10, 11], 2: [4, 5, 6, 7], 3: [12, 13, 14, 15]}
        used |= {("gate", q): "fill g %d" % GCH[q][-1] for q in range(4)}

        def routed(eng, e):
            return (eng.value_load(tab[0:1, bass.ds(16 + e, 1)], min_val=0, max_val=ALL_TILES),
                    eng.value_load(tab[0:1, bass.ds(e, 1)], min_val=1, max_val=MAX_TILES))

        block = ctx.enter_context(nc.Block())

        @block.sync
        def _(sp):
            sp.dma_start(vrow[0:8, :], a["c_ctx"].rearrange("(k n) -> k n", n=P)).then_inc(d_vec, 16)
            sp.dma_start(vrow[8:16, :], a["c"].rearrange("b (k n) -> (b k) n", n=P)).then_inc(d_vec, 16)
            sp.dma_start(vrow[16:24, :], a["norm1_g"].rearrange("b (k n) -> (b k) n", n=P)).then_inc(d_vec, 16)
            sp.dma_start(vrow[24:28, :], a["q_a_norm_g"].rearrange("b (k n) -> (b k) n", n=P)).then_inc(d_vec, 16)
            sp.dma_start(con[:, :], a["const_table"]).then_inc(d_con, 16)
            sp.dma_start(x_sb[:, 0, :], a["x_prompt"][0]).then_inc(d_x[0], 16)
            for q in range(4):
                if q < 2:
                    sp.dma_start(x_sb[:, 1 + q, :], a["x_sample"][0, q * P:(q + 1) * P, :]).then_inc(d_x[1 + q], 16)
                sp.dma_start(rpiece(("mod0", q), 2048), wmod[:, 2 * q:2 * q + 2, 0:2048]).then_inc(d_ring[q], 16)
            sp.wait_ge(zero_done, 2)
            for r in range(2):
                sp.dma_start(bmod[r:r + 97:32, :, :], a["b_mod"][0].rearrange("(j g n) -> g j n", j=3, g=4)).then_inc(d_bmod, 16)
            sp.dma_start(kvg, a["kv_a_norm_g"].to_broadcast([P, KV_LORA])).then_inc(d_small, 16)
            sp.dma_start(qng, a["q_norm_g"].to_broadcast([P, QKH])).then_inc(d_small, 16)
            sp.dma_start(kng, a["k_norm_g"].to_broadcast([P, QKH])).then_inc(d_small, 16)
            sp.dma_start(rb[:, 0:4], a["b_router_group"].to_broadcast([P, NG])).then_inc(d_small, 16)
            sp.dma_start(rb[:, 4:20], a["b_router_expert"].to_broadcast([P, NE])).then_inc(d_small, 16)
            sp.dma_start(ckv[:, 3, :], a["cache_ckv"][0, 0]).then_inc(d_cache, 16)
            sp.dma_start(kpe[:, 3, :], a["cache_kpe"][0, 0]).then_inc(d_cache, 16)
            sp.dma_start(wkvb, a["w_kv_b"][0].rearrange("(k p) n -> p k n", p=P)).then_inc(d_kvb, 16)

            def load(key):
                n = order.index(key)
                if n >= RING1:
                    sp.wait_ge(*PE.at(used[order[n - RING1]]))
                kind, q = key
                s = ring[key][0]
                if kind.startswith("mod"):
                    j = int(kind[3])
                    dst, src = rpiece(key, 2048), wmod[:, 2 * q:2 * q + 2, 2048 * j:2048 * j + 2048]
                elif kind == "tokw":
                    k0, k1 = TOKK[q]
                    dst, src = rpiece(key, TOKW)[:, 0:k1 - k0, :], win[:, k0:k1, 0:TOKW]
                elif kind == "gate":
                    dst = rpiece(key, 512)
                    c0 = GATE0 + GCH[q][0] * P
                    src = win[:, :, c0:c0 + 512]
                elif kind == "out":
                    dst, src = rpiece(key, D), a["w_out"][0].rearrange("(k p) n -> p k n", p=P)[:, 4 * q:4 * q + 4, :]
                else:
                    w = a["w_attn_o"] if kind == "attn_o" else a["w_fnet"]
                    dst, src = rpiece(key, D), w[0].rearrange("(k p) n -> p k n", p=P)
                sp.dma_start(dst, src).then_inc(d_ring[s], 16)

            for q in range(3):
                load(("tokw", q))
            load(("gate", 0))
            sp.wait_ge(*PE.at("xT2"))
            sp.dma_start(wqb, a["w_q_b"][0].rearrange("(k p) n -> p k n", p=P)).then_inc(d_qb, 16)
            sp.wait_ge(*V.at("ckv 0"))
            sp.wait_ge(*A.at("kpe 0"))
            sp.dma_start(a["new_ckv"][0, 0], ckv[:, 0, :]).then_inc(d_outc, 16)
            sp.dma_start(a["new_kpe"][0, 0], kpe[:, 0, :]).then_inc(d_outc, 16)
            for key in order[8:17]:
                load(key)
            sp.wait_ge(*V.at("modrow 1"))
            for r in range(2):
                sp.dma_start(modd[r, 0:2048].rearrange("(g n) -> g n", g=4), modrow[r:r + 97:32, :]).then_inc(d_mod1, 16)
            for key in order[17:19]:
                load(key)
            sp.wait_ge(*V.at("modrow 2"))
            for r in range(2):
                sp.dma_start(modd[r, 2048:4096].rearrange("(g n) -> g n", g=4), modrow[r:r + 97:32, :]).then_inc(d_mod2, 16)
            sp.wait_ge(*PE.at("QB 2"))
            sp.dma_start(x_sb[:, 0, :], a["x_prompt"][0]).then_inc(d_xre, 16)
            sp.dma_start(x_sb[:, 1:3, :], a["x_sample"][0].rearrange("(t p) n -> p t n", p=P)).then_inc(d_xre, 16)
            for key in order[19:23]:
                load(key)
            sp.wait_ge(*V.at("u 7"))
            sp.wait_ge(d_mod1, 32)
            sp.wait_ge(d_mod2, 32)
            for v in range(3):
                for r in range(2):
                    sp.dma_start(bc[:, v, r, :], modd[r:r + 1, v * D:(v + 1) * D].to_broadcast([P, D])).then_inc(d_bc, 16)
            sp.dma_start(g2b, a["norm2_g"].to_broadcast([P, D])).then_inc(d_bc, 16)
            sp.dma_start(wr[:, :, 0:NG], a["w_router_group"][0].rearrange("(k p) n -> p k n", p=P)).then_inc(d_bc, 16)
            sp.dma_start(wr[:, :, NG:NG + NE], a["w_router_expert"][0].rearrange("(k p) n -> p k n", p=P)).then_inc(d_bc, 16)

            wg = a["w_exp_gate"][0].rearrange("e (k p) n -> p e k n", p=P)
            wu = a["w_exp_up"][0].rearrange("e (k p) n -> p e k n", p=P)
            wd = a["w_exp_down"][0].rearrange("e (k p) n -> p e k n", p=P)

            def load_gate(e, s):
                sp.dma_start(piece(3 * s).rearrange("p (k n) -> p k n", n=DE), wg[:, e]).then_inc(d_gu[s], 16)

            def load_up(e, s):
                sp.dma_start(piece(3 * s + 1).rearrange("p (k n) -> p k n", n=DE), wu[:, e]).then_inc(d_gu[s], 16)

            def load_down(e, s):
                sp.dma_start(piece(3 * s + 2).rearrange("p (k n) -> p k n", n=D), wd[:, e]).then_inc(d_dn[s], 16)

            sp.wait_ge(*PE.at("AF 7"))
            load_gate(0, 0)
            load_gate(1, 1)
            load_up(1, 1)
            sp.wait_ge(*PE.at("out 2"))
            load_up(0, 0)
            load_down(0, 0)
            sp.wait_ge(*V.at("h2 2"))
            load_down(1, 1)
            sp.wait_ge(*PE.at("router"))
            load_gate(2, 2)
            load_up(2, 2)
            load_down(2, 2)
            sp.wait_ge(*V.at("tab"))

            def load_rows(e, s):
                first = sp.value_load(tab[0:1, bass.ds(16 + e, 1)], min_val=0, max_val=ALL_TILES - 1)
                row = sp.snap(first * SLOTS)
                for g in range(2):
                    sp.dma_start(xg[SLOTS * g:SLOTS * (g + 1), s], slots[bass.ds(row, 2 * SLOTS), g * 512:(g + 1) * 512].rearrange(
                        "(j p) n -> p j n", j=2)).then_inc(d_xg[s], 16)

            sp.wait_ge(d_scat, 6 * 16)
            for s in range(ESLOTS):
                load_rows(s, s)

            def store(T2, tile, buf, done):
                row = sp.snap(tile * SLOTS)
                sp.wait_ge(t_ye, T2)
                for g in range(2):
                    sp.dma_start(slots[bass.ds(row, SLOTS), g * 512:(g + 1) * 512], ye[SLOTS * g:SLOTS * (g + 1), buf, :]).then_inc(done, 16)

            def results(e, s):
                first, tiles = routed(sp, e)

                def at(j):
                    t = nc.s_assert_within(sp.snap(first + j), 0, ALL_TILES - 1, skip_runtime_bounds_check_because=
                                           "16 experts' counts, 768 in all, are at most 28 tiles")
                    return sp.snap(t + 2), t
                store(*at(0), s, d_y0[s])
                with sp.If(tiles > 1):
                    store(*at(1), ESLOTS, d_ymore)
                    with sp.If(tiles > 2):
                        with sp.Fori(2, tiles) as j:
                            T2, t = at(j)
                            row = sp.snap(t * SLOTS)
                            for g in range(2):
                                sp.dma_start(xg[SLOTS * g:SLOTS * (g + 1), s, 1, :], slots[bass.ds(row, SLOTS), g * 512:(g + 1) * 512]).then_inc(d_xmore, 16)
                            store(T2, t, ESLOTS, d_ymore)

            def expert(e, s):
                results(e, s)
                load_gate(e + ESLOTS, s)
                load_up(e + ESLOTS, s)
                load_rows(e + ESLOTS, s)
                load_down(e + ESLOTS, s)

            with sp.Fori(0, (NE - ESLOTS) // ESLOTS) as g:
                for s in range(ESLOTS):
                    expert(g * ESLOTS + s, s)
            expert(NE - ESLOTS - 1, (NE - ESLOTS - 1) % ESLOTS)
            results(NE - 3, (NE - 3) % ESLOTS)
            for r in range(2):
                sp.dma_start(g5[:, r, :], modd[r:r + 1, 3 * D:4 * D].to_broadcast([P, D])).then_inc(d_g5, 16)
            results(NE - 2, (NE - 2) % ESLOTS)
            results(NE - 1, (NE - 1) % ESLOTS)
            for t in range(NT):
                sp.wait_ge(fin, t + 1)
                dst = a["y_prompt"][0] if t == 0 else a["y_sample"][0, (t - 1) * P:t * P, :]
                sp.dma_start(dst, x_sb[:, t, :]).then_inc(d_out, 16)
            sp.wait_ge(d_out, 16 * NT)
            sp.wait_ge(d_outc, 32)

        @block.gpsimd
        def _(pool):
            nc.gpsimd.memset(c32, 0.0).then_inc(zero_done, 1)
            nc.gpsimd.memset(bmod, 0.0).then_inc(zero_done, 1)
            nc.gpsimd.memset(epsc, EPS).then_inc(zero_done, 1)
            nc.gpsimd.memset(yTt[:, 0:D], 0.0).then_inc(zero_done, 1)
            pool.wait_ge(*V.at("slots"))
            for s in range(ESLOTS):
                pool.wait_ge(d_y0[s], 16)
            pool.wait_ge(d_ymore, 16)
            for t in range(NT):
                for c in range(2):
                    nc.gpsimd.indirect_dma_start(slots, bass.IndirectOffsetOnAxis(ap=sidx[:, 2 * t + c:2 * t + c + 1], axis=0),
                                                 h2[:, t, :], None).then_inc(d_scat, 16)
            pool.wait_ge(all_stored, 1)
            for t in range(NT):
                for c in range(2):
                    nc.gpsimd.indirect_dma_start(ybuf[:, t, c, :], None, slots,
                                                 bass.IndirectOffsetOnAxis(ap=sidx[:, 2 * t + c:2 * t + c + 1], axis=0)).then_inc(d_gath[t], 16)

        @block.tensor
        def _(pe):
            mm, tr = nc.tensor.matmul, nc.tensor.transpose
            pe.wait_ge(d_con, 16)
            pe.wait_ge(d_vec, 64)
            tr(B[0][:, 0:28], vrow[0:28, :], ident[0:28, 0:28])
            pe.wait_ge(*V.at("silu c"))
            tr(B[0][:, 32:48], srow[0:16, :], ident[0:16, 0:16]).then_inc(*PE.mark("vecT"))
            for t in range(NT):
                pe.wait_ge(*V.at(f"xn {t}"))
                for k in range(KC):
                    i = tr(B[1 + 2 * t + k // 4][:, (k % 4) * P:(k % 4 + 1) * P], x_sb[:, t, k * P:(k + 1) * P], ident)
                i.then_inc(*PE.mark(f"xT{t}"))

            def modulation(j, bank):
                for k in range(KC):
                    key = (f"mod{j}", k // 2)
                    if k % 2 == 0:
                        arrived(pe, key)
                    for g in range(4):
                        i = mm(bank[32 * g:32 * g + 32, :], (c32_late if j else c32)[:, k, :], rpiece(key, 2048)[:, k % 2, 512 * g:512 * g + 512],
                               start=(k == 0), stop=(k == KC - 1))
                return i

            pe.wait_ge(*V.at("vec out"))
            modulation(0, B[7]).then_inc(*PE.mark("mod0"))
            pe.wait_ge(*V.at("modrow 0"))
            for i4 in range(4):
                i = tr(B[0][:, i4 * P:(i4 + 1) * P], modrow[:, i4 * P:(i4 + 1) * P], ident)
            i.then_inc(*PE.mark("modT"))

            def tok(t):
                b = 1 if t % 2 == 0 else 4
                if t == 2:
                    pe.wait_ge(*A.at("qan 0"))
                    pe.wait_ge(*V.at("ckv 0"))
                else:
                    for x in range(NT):
                        pe.wait_ge(*V.at(f"hT {x}"))
                        pe.wait_ge(*A.at(f"hT {x}"))
                for k in range(KC):
                    key = ("tokw", [0, 0, 0, 1, 1, 1, 2, 2][k])
                    arrived(pe, key)
                    w = rpiece(key, TOKW)[:, k - TOKK[key[1]][0], :]
                    lhs = hT[:, k, t * P:(t + 1) * P]
                    mm(B[b][:, :], lhs, w[:, 0:512], start=(k == 0), stop=(k == KC - 1))
                    mm(B[b + 1][:, 0:288], lhs, w[:, 512:800], start=(k == 0), stop=(k == KC - 1))
                    i = mm(B[b + 2][:, :], lhs, w[:, 800:1312], start=(k == 0), stop=(k == KC - 1))
                i.then_inc(*PE.mark(f"tok {t}"))

            def lora_T(r):
                if r == "c":
                    pe.wait_ge(d_cache, 32)
                    pe.wait_ge(*V.at("mod cols"))
                else:
                    pe.wait_ge(*V.at(f"ckv {r}"))
                    pe.wait_ge(*A.at(f"qan {r}"))
                    pe.wait_ge(*V.at("Tev %s" % {0: "c", 1: 0, 2: 1}[r]))
                    if r == 0:
                        pe.wait_ge(*V.at("modrow 0"))
                    for k in range(4):
                        tr(B[7][:, k * P:(k + 1) * P], qan[:, r % 2, k * P:(k + 1) * P], ident)
                for k in range(2):
                    i = tr(B[0][:, k * P:(k + 1) * P], ckv[:, ROW[r], k * P:(k + 1) * P], ident)
                i.then_inc(*PE.mark(f"T {r}"))

            def kv_b(r):
                pe.wait_ge(*V.at(f"Tev {r}"))
                if r == "c":
                    pe.wait_ge(d_kvb, 16)
                    pe.wait_ge(*A.at("fn 2"))
                    pe.wait_ge(*A.at("qan 1"))
                else:
                    prev = {0: "c", 1: 0, 2: 1}[r]
                    pe.wait_ge(*V.at(f"kh {prev}"))
                    pe.wait_ge(*A.at(f"vv {prev}"))
                for half in range(2):
                    for k in range(2):
                        i = mm(B[3 + half][:, :], ckvT[:, k, ROW[r], :], wkvb[:, k, half * 512:(half + 1) * 512],
                               start=(k == 0), stop=(k == 1))
                i.then_inc(*PE.mark(f"KV {r}"))

            def q_b(t):
                pe.wait_ge(*V.at(f"Tev {t}"))
                if t == 0:
                    pe.wait_ge(d_qb, 16)
                    pe.wait_ge(*A.at("qan 2"))
                    pe.wait_ge(*V.at("ckv 2"))
                else:
                    pe.wait_ge(*A.at(f"qh {t - 1}"))
                for half in range(2):
                    for k in range(4):
                        i = mm(B[1 + half][:, 0:384], qaT[:, k, t * P:(t + 1) * P], wqb[:, k, half * 384:(half + 1) * 384],
                               start=(k == 0), stop=(k == 3))
                i.then_inc(*PE.mark(f"QB {t}"))

            def heads_T(src, step):
                for h in range(H):
                    i = tr(B[5 + h // 4][0:QKH, (h % 4) * P:(h % 4 + 1) * P], src[:, h, :], ident)
                i.then_inc(*PE.mark(step))

            last_x = []

            def xk(r):
                pe.wait_ge(*V.at(f"kn {r}"))
                pe.wait_ge(*A.at(last_x[-1] if last_x else "fA 1"))
                heads_T(kh, f"XK {r}")
                last_x.append(f"kT {r}")

            def xq(t):
                pe.wait_ge(*V.at(f"qn {t}"))
                pe.wait_ge(*A.at(last_x[-1]))
                heads_T(qh, f"XQ {t}")
                last_x.append(f"qT {t}")

            def fourier_seq(g):
                bl, bx = (B[5], B[6]) if g < 2 else (B[7], B[0])
                if g == 0:
                    pe.wait_ge(*A.at("fn 2"))
                    pe.wait_ge(*A.at("qan 1"))
                elif g == 2:
                    pe.wait_ge(*V.at("Tev 2"))
                else:
                    pe.wait_ge(*A.at(f"fA {g - 1}"))
                for s in range(2):
                    mm(bl[:, :], fn[:, 1 + s, g * P:(g + 1) * P], con[:, C_SL + s * 512:C_SL + (s + 1) * 512],
                       start=(s == 0), stop=(s == 1))
                mm(bx[:, 0:256], fn[:, 0, g * P:(g + 1) * P], con[:, C_SC:C_SC + 256], start=True,
                   stop=True).then_inc(*PE.mark(f"FA {g}"))

            def fourier_ch(part):
                if part == 0:
                    pe.wait_ge(*A.at("fA 3"))
                    for pair in range(2):
                        b = (B[7], B[0])[pair]
                        mm(b[:, :], dft_c, fA[:, 2 * pair:2 * pair + 2, 0:256], start=True, stop=False)
                        i = mm(b[:, :], dft_s, fA[:, 2 * pair:2 * pair + 2, 256:512], start=False, stop=True)
                else:
                    pe.wait_ge(*A.at("yT 0"))
                    mm(B[7][:, :], dft_c, fA[:, :, 512:640], start=True, stop=False)
                    i = mm(B[7][:, :], dft_s, fA[:, :, 640:768], start=False, stop=True)
                i.then_inc(*PE.mark(f"FB {part}"))

            does = {"tok": tok, "T": lora_T, "KV": kv_b, "QB": q_b, "XK": xk, "XQ": xq, "FA": fourier_seq, "FB": fourier_ch}
            for what, i in MIDDLE:
                does[what](i)

            def scores(u):
                h, t = UNITS[u]
                if u >= 2:
                    pe.wait_ge(*A.at(f"p {u - 2}"))
                else:
                    pe.wait_ge(*A.at("qT 2"))
                k0, kn = (384, P) if t == 0 else (0, 384)
                mm(B[1 + u % 2][:, 0:kn], qT[0:QKH, h, t * P:(t + 1) * P], kT[0:QKH, h, k0:k0 + kn], start=True,
                   stop=True).then_inc(*PE.mark(f"S {u}"))

            def fill(n):
                kind, c = FILLERS[n]
                bank = B[7] if n % 2 == 0 else B[0]
                if n >= 2:
                    pk, pc = FILLERS[n - 2]
                    pe.wait_ge(*(A.at(f"ge {pc}") if pk == "g" else V.at(f"modrow {pc}")))
                else:
                    pe.wait_ge(*A.at("yT 1"))
                if kind == "mod":
                    modulation(c, bank).then_inc(*PE.mark(f"fill mod {c}"))
                    return
                q = [q for q in GCH if c in GCH[q]][0]
                arrived(pe, ("gate", q))
                w = rpiece(("gate", q), 512)
                c0 = (c - GCH[q][0]) * P
                for k in range(KC):
                    i = mm(bank[:, 0:NTOK], w[:, k, c0:c0 + P], hT[:, k, :], start=(k == 0), stop=(k == KC - 1))
                i.then_inc(*PE.mark(f"fill g {c}"))

            def probs_T(u):
                h, t = UNITS[u]
                pe.wait_ge(*V.at(f"pn {u}"))
                if u >= 2:
                    pe.wait_ge(*A.at(f"pT {u - 2}"))
                for kt in range(1 if t == 0 else 3):
                    i = tr(B[3 + u % 2][:, kt * P:(kt + 1) * P], probs[:, u % 2, kt * P:(kt + 1) * P], ident)
                i.then_inc(*PE.mark(f"PT {u}"))

            def pv(u):
                h, t = UNITS[u]
                pair = h // 2
                pe.wait_ge(*A.at(f"pT {u}"))
                if u % 6 == 0 and pair >= 2:
                    pe.wait_ge(*V.at(f"oT {pair - 2}"))
                slots = [3] if t == 0 else [0, 1, 2]
                o = B[5 + pair % 2][VH * (h % 2):VH * (h % 2) + VH, t * P:(t + 1) * P]
                for n, s in enumerate(slots):
                    i = mm(o, vv[:, s, h * VH:(h + 1) * VH], pT[:, u % 2, n * P:(n + 1) * P], start=(n == 0), stop=(n == len(slots) - 1))
                i.then_inc(*PE.mark(f"PV {u}"))

            scores(0)
            for u in range(len(UNITS)):
                if u + 1 < len(UNITS):
                    scores(u + 1)
                if u < len(FILLERS):
                    fill(u)
                probs_T(u)
                if u:
                    pv(u - 1)
            pv(len(UNITS) - 1)

            pe.wait_ge(*V.at("oT 3"))
            arrived(pe, ("attn_o", 0))
            arrived(pe, ("fnet", 0))
            wa, wf = rpiece(("attn_o", 0), D), rpiece(("fnet", 0), D)
            for c in range(KC):
                if c >= 2:
                    pe.wait_ge(*V.at(f"u {c - 2}"))
                for k in range(4):
                    mm(B[1 + c % 2][:, 0:NTOK], wa[:, k, c * P:(c + 1) * P], oT[:, k, :], start=(k == 0), stop=(k == 3))
                for k in range(4):
                    i = mm(B[3 + c % 2][:, 0:NTOK], wf[:, k, c * P:(c + 1) * P], yT[:, k, :], start=(k == 0), stop=(k == 3))
                i.then_inc(*PE.mark(f"AF {c}"))

            OB = [(5, 6), (7, 0), (5, 6)]
            pe.wait_ge(*V.at("u 7"))
            arrived(pe, ("out", 0))
            arrived(pe, ("out", 1))
            for t in range(NT):
                if t == 2:
                    pe.wait_ge(*V.at("x1 0"))
                for half in range(2):
                    for k in range(KC):
                        w = rpiece(("out", k // 4), D)[:, k % 4, half * 512:(half + 1) * 512]
                        i = mm(B[OB[t][half]][:, :], uT[:, k, t * P:(t + 1) * P], w, start=(k == 0), stop=(k == KC - 1))
                i.then_inc(*PE.mark(f"out {t}"))
            for t in range(NT):
                pe.wait_ge(*V.at(f"h2 {t}"))
                if t == 2:
                    pe.wait_ge(*A.at("h2T 0"))
                b = 1 if t % 2 == 0 else 3
                for k in range(KC):
                    i = tr(B[b + k // 4][:, (k % 4) * P:(k % 4 + 1) * P], h2[:, t, k * P:(k + 1) * P], ident)
                i.then_inc(*PE.mark(f"h2T {t}"))
            pe.wait_ge(*A.at("h2T 2"))
            pe.wait_ge(d_bc, 9 * 16)
            for t in range(NT):
                for k in range(KC):
                    i = mm(B[7][:, t * 32:t * 32 + 20], h2T[:, k, t * P:(t + 1) * P], wr[:, k, :], start=(k == 0), stop=(k == KC - 1))
            i.then_inc(*PE.mark("router"))
            pe.wait_ge(*V.at("masks"))
            for t in range(NT):
                for x in range(t + 1):
                    mm(B[0][:, t * 16:(t + 1) * 16], ones if x < t else tri, MM[:, x, :], start=(x == 0), stop=(x == t))
            for x in range(NT):
                i = mm(B[0][:, 48:64], ones, MM[:, x, :], start=(x == 0), stop=(x == NT - 1))
            i.then_inc(*PE.mark("rank"))

            pe.wait_ge(*V.at("tab"))

            def tile(T1, s, j, rows_in, weights_in):
                wgu = big[:, 3 * s * PIECE:(3 * s + 2) * PIECE].rearrange("p (w k n) -> p w k n", w=2, k=KC)
                wdn = piece(3 * s + 2).rearrange("p (k n) -> p k n", n=D)
                pe.wait_ge(*rows_in)
                for q in range(4):
                    i = tr(B[2][:, q * P:(q + 1) * P], xg[:, s, j, q * P:(q + 1) * P], ident)
                i.then_inc(t_xeTp, 1)
                pe.wait_ge(t_xeTs, T1)
                pe.wait_ge(d_gu[s], weights_in[0])
                for w in range(2):
                    for k in range(KC):
                        for g in range(2):
                            i = mm(B[4 * w][SLOTS * g:SLOTS * (g + 1), 0:256], xeT[:, k % 4, k // 4, :], wgu[:, w, k, g * 256:(g + 1) * 256],
                                   start=(k == 0), stop=(k == KC - 1))
                    i.then_inc(t_u if w else t_g, 1)
                pe.wait_ge(t_act, T1)
                for q in range(2):
                    i = tr(B[3][:, q * P:(q + 1) * P], actv[:, q * P:(q + 1) * P], ident)
                i.then_inc(t_aTp, 1)
                pe.wait_ge(t_aTs, T1)
                pe.wait_ge(d_dn[s], weights_in[1])
                pe.wait_ge(t_ye, T1)
                for f in range(4):
                    for g in range(2):
                        i = mm(B[1][SLOTS * g:SLOTS * (g + 1), :], actT[:, f % 2, f // 2, :], wdn[:, f, g * 512:(g + 1) * 512],
                               start=(f == 0), stop=(f == 3))
                i.then_inc(t_y, 1)

            def expert(e, s, n):
                first, tiles = routed(pe, e)
                more = pe.value_load(tab[0:1, bass.ds(33 + e, 1)], min_val=0, max_val=ALL_TILES)
                n_gu, n_dn = (pe.snap(n * 32), pe.snap(n * 16)) if not isinstance(n, int) else (n * 32, n * 16)
                tile(pe.snap(first + 1), s, 0, (d_xg[s], n_gu), (n_gu, n_dn))
                with pe.If(tiles > 1):
                    tile(pe.snap(first + 2), s, 1, (d_xg[s], n_gu), (n_gu, n_dn))
                    with pe.If(tiles > 2):
                        with pe.Fori(2, tiles) as j:
                            tile(pe.snap(first + j + 1), s, 1, (d_xmore, pe.snap((more + j) * 32 - 32)), (n_gu, n_dn))

            with pe.Fori(0, NE // ESLOTS) as g:
                for s in range(ESLOTS):
                    expert(g * ESLOTS + s, s, g + 1)
            expert(NE - 1, (NE - 1) % ESLOTS, NE // ESLOTS + 1)

        @block.vector
        def _(v):
            ts, tt, cp, stt = nc.vector.tensor_scalar, nc.vector.tensor_tensor, nc.vector.tensor_copy, nc.vector.scalar_tensor_tensor

            def order(eng=v):
                eng.drain()

            def rsqrt(r, m, w):
                tt(w, r, r, ALU.mult)
                order()
                tt(w, w, m, ALU.mult)
                order()
                ts(w, w, -0.5, 1.5, ALU.mult, ALU.add)
                order()
                return tt(r, r, w, ALU.mult)

            v.wait_ge(*A.at("exp c"))
            ts(erow[0:16, :], erow[0:16, :], 1.0, None, ALU.add)
            order()
            nc.vector.reciprocal(erow[0:16, :], erow[0:16, :])
            order()
            tt(srow[0:16, :], vrow[0:16, :], erow[0:16, :], ALU.mult).then_inc(*V.mark("silu c"))
            v.wait_ge(*PE.at("vecT"))
            cp(g1T, B[0][:, 16:24])
            cp(qgT, B[0][:, 24:28])
            v.wait_ge(zero_done, 3)
            cp(c32[:, :, 0:2], B[0][:, 32:48].rearrange("p (r k) -> p k r", r=2)).then_inc(*V.mark("vec out"))
            v.wait_ge(*A.at("rsx"))
            ts(msx, ssx, EPS, None, ALU.add)
            order()
            rsqrt(rsx, msx, nwx)
            order()
            for t in range(NT):
                ts(x_sb[:, t, :], x_sb[:, t, :], rsx[:, t:t + 1], None, ALU.mult).then_inc(*V.mark(f"xn {t}"))
            v.wait_ge(*PE.at("mod0"))
            v.wait_ge(d_bmod, 32)
            tt(modrow, B[7][:, :], bmod[:, 0, :], ALU.add).then_inc(*V.mark("modrow 0"))
            v.wait_ge(*PE.at("modT"))
            mv = B[0][:, :].rearrange("p (i g x) -> p g i x", i=4, g=4)
            for r in range(2):
                cp(shT[:, r, :].rearrange("p (g i) -> p g i", g=2), mv[:, 0:2, :, r])
                i = stt(out=a1T[:, r, :].rearrange("p (g i) -> p g i", g=2), in0=mv[:, 2:4, :, r], scalar=1.0,
                        in1=g1T.rearrange("p (g i) -> p g i", g=2), op0=ALU.add, op1=ALU.mult)
            i.then_inc(*V.mark("mod cols"))
            order()
            cp(c32_late, c32)
            for t in range(NT):
                r = min(t, 1)
                for k in range(KC // 2):
                    i = ts(hT[:, k, t * P:(t + 1) * P], B[1 + 2 * t + k // 4][:, (k % 4) * P:(k % 4 + 1) * P],
                           a1T[:, r, k:k + 1], shT[:, r, k:k + 1], ALU.mult, ALU.add)
                i.then_inc(*V.mark(f"hT {t}"))

            def tok(t):
                b = 1 if t % 2 == 0 else 4
                v.wait_ge(*A.at(f"rs {t}"))
                if t == 0:
                    v.wait_ge(d_small, 80)
                ts(ms[:, 8:10], ss[:, 8:10], EPS, None, ALU.add)
                order()
                rsqrt(rs[:, 8:10], ms[:, 8:10], nw[:, 8:10]).then_inc(*V.mark(f"nr {t}"))
                order()
                v.wait_ge(*A.at(f"kpe {t}"))
                stt(out=ckv[:, t, :], in0=B[b + 1][:, 0:256], scalar=rs[:, 9:10], in1=kvg, op0=ALU.mult,
                    op1=ALU.mult).then_inc(*V.mark(f"ckv {t}"))

            def lora(r):
                v.wait_ge(*PE.at(f"T {r}"))
                if r != "c":
                    for k in range(4):
                        ts(qaT[:, k, r * P:(r + 1) * P], B[7][:, k * P:(k + 1) * P], qgT[:, k:k + 1], None, ALU.mult)
                cp(ckvT[:, :, ROW[r], :], B[0][:, 0:256].rearrange("p (k n) -> p k n", k=2)).then_inc(*V.mark(f"Tev {r}"))

            def k_in(r):
                v.wait_ge(*A.at(f"vv {r}"))
                if r != "c":
                    v.wait_ge(*PE.at("XK %s" % {0: "c", 1: 0, 2: 1}[r]))
                for half in range(2):
                    cp(kh[:, 4 * half:4 * half + 4, 0:NOPE], B[3 + half][:, :].rearrange("p (h n) -> p h n", h=4)[:, :, 0:NOPE])
                if r == "c":
                    v.wait_ge(d_cache, 32)
                else:
                    v.wait_ge(*A.at(f"kpe {r}"))
                cp(kh[:, :, NOPE:QKH], kpe[:, ROW[r], :].unsqueeze(1).to_broadcast([P, H, ROPE])).then_inc(*V.mark(f"kh {r}"))

            def head_norm(x, gain, t, rs_step, step):
                order()
                sqv = sq.rearrange("p (h n) -> p h n", h=H)
                tt(sqv, x, x, ALU.mult)
                order()
                nc.vector.tensor_reduce(ss[:, 0:8], sqv, AX.X, ALU.add)
                order()
                ts(ms[:, 0:8], ss[:, 0:8], 1.0 / QKH, EPS, ALU.mult, ALU.add).then_inc(*V.mark(rs_step))
                v.wait_ge(*A.at(rs_step))
                rsqrt(rs[:, 0:8], ms[:, 0:8], nw[:, 0:8])
                order()
                tt(x, x, rs[:, 0:8].unsqueeze(2).to_broadcast([P, H, QKH]), ALU.mult)
                order()
                i = tt(x, x, gain.unsqueeze(1).to_broadcast([P, H, QKH]), ALU.mult)
                if t in (1, 2):
                    order()
                    pe4 = x[:, :, NOPE:QKH].rearrange("p h (a b f) -> p h a b f", a=2, b=2)
                    x1, x2 = pe4[:, :, :, 0, :], pe4[:, :, :, 1, :]
                    c0 = (t - 1) * 16
                    cos = con[:, C_RC + c0:C_RC + c0 + 16].rearrange("p (a f) -> p a f", a=2).unsqueeze(1).to_broadcast([P, H, 2, 8])
                    sin = con[:, C_RS + c0:C_RS + c0 + 16].rearrange("p (a f) -> p a f", a=2).unsqueeze(1).to_broadcast([P, H, 2, 8])
                    r1, r2, r3, r4 = (sq[:, 128 * q:128 * q + 128].rearrange("p (h a f) -> p h a f", h=H, a=2) for q in range(4))
                    tt(r1, x1, cos, ALU.mult)
                    tt(r2, x2, sin, ALU.mult)
                    tt(r3, x1, sin, ALU.mult)
                    tt(r4, x2, cos, ALU.mult)
                    order()
                    tt(x1, r1, r2, ALU.subtract)
                    i = tt(x2, r3, r4, ALU.add)
                i.then_inc(*V.mark(step))

            def kn(r):
                head_norm(kh, kng, r, f"rk {r}", f"kn {r}")

            def qn(t):
                v.wait_ge(*A.at(f"qh {t}"))
                head_norm(qh, qng, t, f"rq {t}", f"qn {t}")

            does = {"tok": tok, "T": lora, "kh": k_in, "kn": kn, "qn": qn}
            for what, i in DVE_MIDDLE:
                does[what](i)

            def row_max(u):
                h, t = UNITS[u]
                v.wait_ge(*PE.at(f"S {u}"))
                nc.vector.tensor_reduce(mx[:, u % 2:u % 2 + 1], B[1 + u % 2][:, 0:P if t == 0 else 384], AX.X, ALU.max)
                order()
                ts(mx[:, 2 + u % 2:3 + u % 2], mx[:, u % 2:u % 2 + 1], -SCALE, None, ALU.mult).then_inc(*V.mark(f"mx {u}"))

            def normalise(u):
                h, t = UNITS[u]
                v.wait_ge(*A.at(f"p {u}"))
                nc.vector.reciprocal(ri[:, u % 2:u % 2 + 1], sm[:, u % 2:u % 2 + 1])
                order()
                pr = probs[:, u % 2, 0:P if t == 0 else 384]
                ts(pr, pr, ri[:, u % 2:u % 2 + 1], None, ALU.mult).then_inc(*V.mark(f"pn {u}"))

            def filled(n):
                kind, c = FILLERS[n]
                if kind == "mod":
                    v.wait_ge(*PE.at(f"fill mod {c}"))
                    if c == 2:
                        v.wait_ge(d_mod1, 32)
                    tt(modrow, B[7 if n % 2 == 0 else 0][:, :], bmod[:, c, :], ALU.add).then_inc(*V.mark(f"modrow {c}"))
                else:
                    v.wait_ge(*A.at(f"ge {c}"))
                    ts(gates[:, c, :], gates[:, c, :], 1.0, None, ALU.add)
                    order()
                    nc.vector.reciprocal(gates[:, c, :], gates[:, c, :])

            def pair_out(pair):
                v.wait_ge(*PE.at(f"PV {6 * pair + 5}"))
                cp(oT[:, pair, :], B[5 + pair % 2][:, 0:NTOK]).then_inc(*V.mark(f"oT {pair}"))

            row_max(0)
            for u in range(len(UNITS)):
                normalise(u)
                if u + 1 < len(UNITS):
                    row_max(u + 1)
                if 1 <= u <= len(FILLERS):
                    filled(u - 1)
                if u and u % 6 == 0:
                    pair_out(u // 6 - 1)
            pair_out(3)
            for c in range(KC):
                v.wait_ge(*PE.at(f"AF {c}"))
                order()
                tt(uT[:, c, :], B[1 + c % 2][:, 0:NTOK], gates[:, c, :], ALU.mult)
                tt(otmp[:, 0:NTOK], B[3 + c % 2][:, 0:NTOK], gates[:, 8 + c, :], ALU.mult)
                order()
                tt(uT[:, c, :], uT[:, c, :], otmp[:, 0:NTOK], ALU.add).then_inc(*V.mark(f"u {c}"))
            v.wait_ge(d_bc, 9 * 16)
            for r in range(2):
                stt(out=bc[:, 2, r, :], in0=bc[:, 2, r, :], scalar=1.0, in1=g2b, op0=ALU.add, op1=ALU.mult)
            v.wait_ge(d_xre, 32)
            for t in range(NT):
                r = min(t, 1)
                v.wait_ge(*PE.at(f"out {t}"))
                order()
                for half in range(2):
                    o = slice(half * 512, half * 512 + 512)
                    tt(otmp[:, o], B[((5, 6), (7, 0), (5, 6))[t][half]][:, :], bc[:, 0, r, o], ALU.mult)
                order()
                tt(x_sb[:, t, :], x_sb[:, t, :], otmp[:, :], ALU.add).then_inc(*V.mark(f"x1 {t}"))
                v.wait_ge(*A.at(f"rs2 {t}"))
                c = slice(t, t + 1)
                ts(msx[:, c], ssx[:, c], EPS, None, ALU.add)
                order()
                rsqrt(rsx[:, c], msx[:, c], nwx[:, c])
                order()
                stt(out=h2[:, t, :], in0=x_sb[:, t, :], scalar=rsx[:, c], in1=bc[:, 2, r, :], op0=ALU.mult, op1=ALU.mult)
                order()
                tt(h2[:, t, :], h2[:, t, :], bc[:, 1, r, :], ALU.add).then_inc(*V.mark(f"h2 {t}"))

            def b4(x):
                return x.unsqueeze(2).to_broadcast([P, NT, 4])
            desc = con[:, C_DESC:C_DESC + 4].unsqueeze(1).to_broadcast([P, NT, 4])

            def first_max(out, x, m):
                nc.vector.tensor_reduce(m, x, AX.X, ALU.max)
                order()
                tt(t4, x, b4(m), ALU.is_ge)
                order()
                tt(t4, t4, desc, ALU.mult)
                order()
                nc.vector.tensor_reduce(rr, t4, AX.X, ALU.max)
                order()
                tt(out, t4, b4(rr), ALU.is_equal)
                order()

            v.wait_ge(*PE.at("router"))
            tt(lg, B[7][:, 0:96].rearrange("p (t n) -> p t n", t=NT)[:, :, 0:20], rb.unsqueeze(1).to_broadcast([P, NT, 20]), ALU.add)
            order()
            first_max(ohg, lg[:, :, 0:4], rm)
            tt(e2, lg[:, :, 0:4], b4(rm), ALU.subtract).then_inc(*V.mark("gmax"))
            tt(prod, lg[:, :, 4:20].rearrange("p t (g e) -> p t g e", g=4), ohg.unsqueeze(3).to_broadcast([P, NT, 4, 4]), ALU.mult)
            order()
            nc.vector.tensor_reduce(esel, prod.rearrange("p t g e -> p t e g"), AX.X, ALU.add)
            order()
            first_max(oh1, esel, rm1)
            v.wait_ge(*A.at("gexp"))
            nc.vector.tensor_reduce(rsum, e2, AX.X, ALU.add)
            order()
            nc.vector.reciprocal(gp, rsum)
            stt(out=e2, in0=oh1, scalar=-1e38, in1=esel, op0=ALU.mult, op1=ALU.add)
            order()
            first_max(oh2, e2, rm2)
            tt(rd, rm2, rm1, ALU.subtract).then_inc(*V.mark("top2"))
            for m, oh in ((M1, oh1), (M2, oh2)):
                tt(m.rearrange("p t (g e) -> p t g e", g=4), ohg.unsqueeze(3).to_broadcast([P, NT, 4, 4]),
                   oh.unsqueeze(2).to_broadcast([P, NT, 4, 4]), ALU.mult)
            order()
            tt(MM, M1, M2, ALU.add).then_inc(*V.mark("masks"))
            v.wait_ge(*A.at("dexp"))
            ts(rr, rd, 1.0, None, ALU.add)
            order()
            nc.vector.reciprocal(rr, rr)
            order()
            tt(wsl[:, :, 0], rr, gp, ALU.mult)
            order()
            tt(wsl[:, :, 1], wsl[:, :, 0], rd, ALU.mult)
            v.wait_ge(*PE.at("rank"))
            cp(cnt, B[0][:, 48:64])
            nc.vector.memset(nt2, 1.0)
            order()
            for k in range(1, MAX_TILES):
                stt(out=nt2[:, 0, :], in0=cnt, scalar=float(SLOTS * k), in1=nt2[:, 0, :], op0=ALU.is_gt, op1=ALU.add)
                order()
            ts(nt2[:, 1, :], nt2[:, 0, :], -2.0, 0.0, ALU.add, ALU.max)
            ts(nt2[:, 2, :], nt2[:, 0, :], -1.0, None, ALU.add)
            nc.vector.memset(cA[:, :, 0:1], 0.0)
            nc.vector.memset(cB[:, :, 0:1], 0.0)
            order()
            cp(cA[:, :, 1:17], nt2)
            order()
            src, dst = cA, cB
            for sh in (1, 2, 4, 8):
                cp(dst[:, :, 1:1 + sh], src[:, :, 1:1 + sh])
                tt(dst[:, :, 1 + sh:17], src[:, :, 1 + sh:17], src[:, :, 1:17 - sh], ALU.add)
                order()
                src, dst = dst, src
            cp(tab[0:1, 0:16], nt2[0:1, 0, :])
            cp(tab[0:1, 16:67], src[0:1].rearrange("p v n -> p (v n)")).then_inc(*V.mark("tab"))
            stt(out=slot, in0=src[:, 0, 0:16].unsqueeze(1).to_broadcast([P, NT, 16]), scalar=float(SLOTS),
                in1=B[0][:, 0:48].rearrange("p (t n) -> p t n", t=NT), op0=ALU.mult, op1=ALU.add)
            order()
            for c, m in enumerate((M1, M2)):
                tt(tmp48, slot, m, ALU.mult)
                order()
                nc.vector.tensor_reduce(fsl[:, :, c], tmp48, AX.X, ALU.add)
                order()

            cp(sidx[:, :], fsl.rearrange("p t c -> p (t c)")).then_inc(*V.mark("slots"))

            v.drain().then_inc(t_ye, 1)

            def tile(T1, buf, stored):
                v.wait_ge(t_exp, T1)
                ts(eg, eg, 1.0, None, ALU.add)
                order()
                nc.vector.reciprocal(eg, eg)
                order()
                tt(eg, eg, B[0][:, 0:256], ALU.mult)
                order()
                v.wait_ge(t_u, T1)
                tt(actv, eg, B[4][:, 0:256], ALU.mult).then_inc(t_act, 1)
                v.wait_ge(*stored)
                v.wait_ge(t_y, T1)
                cp(ye[:, buf, :], B[1][:, :]).then_inc(t_ye, 1)

            def expert(e, s, n):
                first, tiles = routed(v, e)
                extra = v.value_load(tab[0:1, bass.ds(50 + e, 1)], min_val=0, max_val=ALL_TILES)
                tile(v.snap(first + 1), s, (d_y0[s], v.snap(n * 32 - 16) if not isinstance(n, int) else n * 32 - 16))
                with v.If(tiles > 1):
                    tile(v.snap(first + 2), ESLOTS, (d_ymore, v.snap(extra * 32 + 16)))
                    with v.If(tiles > 2):
                        with v.Fori(2, tiles) as j:
                            tile(v.snap(first + j + 1), ESLOTS, (d_ymore, v.snap((extra + j) * 32 - 16)))

            with v.Fori(0, NE // ESLOTS) as g:
                for s in range(ESLOTS):
                    expert(g * ESLOTS + s, s, g + 1)
            expert(NE - 1, (NE - 1) % ESLOTS, NE // ESLOTS + 1)
            for s in range(ESLOTS):
                v.wait_ge(d_y0[s], 16 + 32 * len(range(s, NE, ESLOTS)))
            extra = v.value_load(tab[0:1, 66:67], min_val=0, max_val=ALL_TILES)
            stored = v.snap(extra * 32 + 16)
            v.wait_ge(d_ymore, stored)
            cp(nwx, msx).then_inc(all_stored, 1)
            v.wait_ge(d_g5, 32)
            for t in range(NT):
                y0, y1 = ybuf[:, t, 0, :], ybuf[:, t, 1, :]
                v.wait_ge(d_gath[t], 32)
                ts(y0, y0, wsl[:, t, 0:1], None, ALU.mult)
                order()
                stt(out=y0, in0=y1, scalar=wsl[:, t, 1:2], in1=y0, op0=ALU.mult, op1=ALU.add)
                order()
                tt(y0, y0, g5[:, min(t, 1), :], ALU.mult)
                order()
                tt(x_sb[:, t, :], x_sb[:, t, :], y0, ALU.add).then_inc(fin, 1)

        @block.scalar
        def _(act):
            av = nc.scalar.activation

            def rsqrt0(out, mean, bias=0.0):
                av(out, mean, ACT.Ln, bias=bias)
                act.drain()
                return av(out, out, ACT.Exp, scale=-0.5)

            nc.scalar.preload_act_table_set("natural_log_exp_and_others")
            act.wait_ge(d_vec, 64)
            av(erow[0:16, :], vrow[0:16, :], ACT.Exp, scale=-1.0).then_inc(*A.mark("exp c"))
            act.wait_ge(zero_done, 3)
            for t in range(NT):
                act.wait_ge(d_x[t], 16)
                av(sqa, x_sb[:, t, :], ACT.Square, scale=D ** -0.5, accum_out=ssx[:, t:t + 1])
                act.drain()
            rsqrt0(rsx, ssx, epsc).then_inc(*A.mark("rsx"))
            act.wait_ge(*V.at("mod cols"))
            for t in range(NT):
                act.wait_ge(*PE.at(f"xT{t}"))
                r = min(t, 1)
                for k in range(KC // 2, KC):
                    i = av(hT[:, k, t * P:(t + 1) * P], B[1 + 2 * t + k // 4][:, (k % 4) * P:(k % 4 + 1) * P], ACT.Identity,
                           scale=a1T[:, r, k:k + 1], bias=shT[:, r, k:k + 1])
                i.then_inc(*A.mark(f"hT {t}"))
            act.wait_ge(zero_done, 4)
            parts = SLOT_ROWS // P
            cuts = [parts * q // 4 for q in range(5)]
            for q, done in enumerate(d_y0 + [d_ymore]):
                act.dma_start(slots[cuts[q] * P:cuts[q + 1] * P, :].rearrange("(c p) n -> p c n", p=P),
                              yTt[:, 0:D].unsqueeze(1).to_broadcast([P, cuts[q + 1] - cuts[q], D])).then_inc(done, 16)

            def tok(t):
                b = 1 if t % 2 == 0 else 4
                act.wait_ge(*PE.at(f"tok {t}"))
                if t:
                    act.wait_ge(*V.at(f"ckv {t - 1}"))
                av(sqa[:, 0:512], B[b][:, :], ACT.Square, scale=Q_LORA ** -0.5, accum_out=ss[:, 8:9])
                av(sqa[:, 512:768], B[b + 1][:, 0:256], ACT.Square, scale=KV_LORA ** -0.5, accum_out=ss[:, 9:10])
                act.drain()
                rsqrt0(rs[:, 8:10], ss[:, 8:10], epsc).then_inc(*A.mark(f"rs {t}"))
                av(kpe[:, t, :], B[b + 1][:, 256:288], ACT.Copy).then_inc(*A.mark(f"kpe {t}"))
                av(fn[:, t, :], B[b + 2][:, :], ACT.Copy).then_inc(*A.mark(f"fn {t}"))
                act.wait_ge(*V.at(f"nr {t}"))
                if t == 2:
                    act.wait_ge(*PE.at("T 0"))
                av(qan[:, t % 2, :], B[b][:, :], ACT.Copy, scale=rs[:, 8:9]).then_inc(*A.mark(f"qan {t}"))

            def values(r):
                act.wait_ge(*PE.at(f"KV {r}"))
                for half in range(2):
                    i = av(vv[:, KSLOT[r], half * 256:(half + 1) * 256].rearrange("p (h n) -> p h n", h=4),
                           B[3 + half][:, :].rearrange("p (h n) -> p h n", h=4)[:, :, NOPE:128], ACT.Copy)
                i.then_inc(*A.mark(f"vv {r}"))

            def rstart(name):
                act.wait_ge(*V.at(name))
                rsqrt0(rs[:, 0:8], ms[:, 0:8]).then_inc(*A.mark(name))

            def q_in(t):
                act.wait_ge(*PE.at(f"QB {t}"))
                if t:
                    act.wait_ge(*PE.at(f"XQ {t - 1}"))
                for half in range(2):
                    i = av(qh[:, 4 * half:4 * half + 4, :], B[1 + half][:, 0:384].rearrange("p (h n) -> p h n", h=4), ACT.Copy)
                i.then_inc(*A.mark(f"qh {t}"))

            def heads_out(dst, lo, pstep, step):
                act.wait_ge(*PE.at(pstep))
                for half in range(2):
                    i = av(dst[0:QKH, 4 * half:4 * half + 4, lo:lo + P], B[5 + half][0:QKH, :].rearrange("p (h n) -> p h n", h=4), ACT.Copy)
                i.then_inc(*A.mark(step))

            def fourier_seq(g):
                bl, bx = (B[5], B[6]) if g < 2 else (B[7], B[0])
                act.wait_ge(*PE.at(f"FA {g}"))
                av(fA[:, g, 0:512], bl[:, :], ACT.Copy)
                av(fA[:, g, 512:768], bx[:, 0:256], ACT.Copy).then_inc(*A.mark(f"fA {g}"))

            def fourier_ch(part):
                act.wait_ge(*PE.at(f"FB {part}"))
                if part == 0:
                    for done in d_y0 + [d_ymore]:
                        act.wait_ge(done, 16)
                    for pair in range(2):
                        i = av(yT[:, 2 * pair:2 * pair + 2, P:NTOK], (B[7], B[0])[pair][:, :].rearrange("p (g n) -> p g n", g=2), ACT.Copy)
                else:
                    i = av(yT[:, :, 0:P], B[7][:, :].rearrange("p (g n) -> p g n", g=4), ACT.Copy)
                i.then_inc(*A.mark(f"yT {part}"))

            does = {"tok": tok, "vv": values, "rk": lambda r: rstart(f"rk {r}"), "rq": lambda t: rstart(f"rq {t}"), "qh": q_in,
                    "kT": lambda r: heads_out(kT, KSLOT[r] * P, f"XK {r}", f"kT {r}"),
                    "qT": lambda t: heads_out(qT, t * P, f"XQ {t}", f"qT {t}"), "fA": fourier_seq, "yT": fourier_ch}
            for what, i in ACT_MIDDLE:
                does[what](i)

            def exps(u):
                h, t = UNITS[u]
                act.wait_ge(*V.at(f"mx {u}"))
                if u >= 2:
                    act.wait_ge(*PE.at(f"PT {u - 2}"))
                n = P if t == 0 else 384
                av(probs[:, u % 2, 0:n], B[1 + u % 2][:, 0:n], ACT.Exp, scale=SCALE, bias=mx[:, 2 + u % 2:3 + u % 2],
                   accum_out=sm[:, u % 2:u % 2 + 1])
                act.drain().then_inc(*A.mark(f"p {u}"))

            exps(0)
            for u in range(len(UNITS)):
                if u + 1 < len(UNITS):
                    exps(u + 1)
                if u < len(FILLERS) and FILLERS[u][0] == "g":
                    c = FILLERS[u][1]
                    act.wait_ge(*PE.at(f"fill g {c}"))
                    av(gates[:, c, :], B[7 if u % 2 == 0 else 0][:, 0:NTOK], ACT.Exp, scale=-1.0).then_inc(*A.mark(f"ge {c}"))
                act.wait_ge(*PE.at(f"PT {u}"))
                if u >= 2:
                    act.wait_ge(*PE.at(f"PV {u - 2}"))
                n = P if UNITS[u][1] == 0 else 384
                av(pT[:, u % 2, 0:n], B[3 + u % 2][:, 0:n], ACT.Copy).then_inc(*A.mark(f"pT {u}"))

            def h2T_out(t):
                act.wait_ge(*PE.at(f"h2T {t}"))
                b = 1 if t % 2 == 0 else 3
                for half in range(2):
                    i = av(h2T[:, 4 * half:4 * half + 4, t * P:(t + 1) * P], B[b + half][:, :].rearrange("p (k n) -> p k n", k=4), ACT.Copy)
                i.then_inc(*A.mark(f"h2T {t}"))

            for t in range(NT):
                act.wait_ge(*V.at(f"x1 {t}"))
                av(junk, x_sb[:, t, :], ACT.Square, scale=D ** -0.5, accum_out=ssx[:, t:t + 1])
                act.drain()
                rsqrt0(rsx[:, t:t + 1], ssx[:, t:t + 1], epsc).then_inc(*A.mark(f"rs2 {t}"))
                if t:
                    h2T_out(t - 1)
            h2T_out(2)
            act.wait_ge(*V.at("gmax"))
            av(e2, e2, ACT.Exp).then_inc(*A.mark("gexp"))
            act.wait_ge(*V.at("top2"))
            av(rd, rd, ACT.Exp).then_inc(*A.mark("dexp"))

            act.wait_ge(*V.at("tab"))

            def tile(T1):
                act.wait_ge(t_xeTp, T1)
                av(xeT, B[2][:, :].rearrange("p (i g s) -> p i g s", i=4, g=2), ACT.Copy).then_inc(t_xeTs, 1)
                act.wait_ge(t_g, T1)
                av(eg, B[0][:, 0:256], ACT.Exp, scale=-1.0).then_inc(t_exp, 1)
                act.wait_ge(t_aTp, T1)
                av(actT, B[3][:, 0:256].rearrange("p (j g s) -> p j g s", j=2, g=2), ACT.Copy).then_inc(t_aTs, 1)

            def expert(e, s, n):
                first, tiles = routed(act, e)
                tile(act.snap(first + 1))
                with act.If(tiles > 1):
                    with act.Fori(1, tiles) as j:
                        tile(act.snap(first + j + 1))

            with act.Fori(0, NE // ESLOTS) as g:
                for s in range(ESLOTS):
                    expert(g * ESLOTS + s, s, g + 1)
            expert(NE - 1, (NE - 1) % ESLOTS, NE // ESLOTS + 1)


INS = ["x_prompt", "x_sample", "cache_ckv", "cache_kpe", "c", "c_ctx", "w_mod", "b_mod", "norm1_g", "w_in", "q_a_norm_g", "w_q_b",
       "kv_a_norm_g", "w_kv_b", "q_norm_g", "k_norm_g", "w_attn_o", "w_fnet", "w_out", "norm2_g", "w_router_group",
       "b_router_group", "w_router_expert", "b_router_expert", "w_exp_gate", "w_exp_up", "w_exp_down"]
OUTS = [("y_prompt", (1, P, D)), ("y_sample", (1, 2 * P, D)), ("new_ckv", (1, 1, P, KV_LORA)), ("new_kpe", (1, 1, P, ROPE))]


def kernel(**inputs):
    import concourse.bacc as bacc
    from concourse.bass_utils import run_bass_kernel_spmd

    nc = bacc.Bacc("TRN2", target_bir_lowering=False, num_devices=1)
    arrays, aps = {}, {}
    for name in INS:
        x = np.ascontiguousarray(inputs[name])
        arrays[f"in_{name}"] = x
        aps[name] = nc.dram_tensor(f"in_{name}", x.shape, mybir.dt.from_np(x.dtype), kind="ExternalInput").ap()
    arrays["in_const_table"] = constants()
    aps["const_table"] = nc.dram_tensor("in_const_table", (P, NCON), F32, kind="ExternalInput").ap()
    for name, shape in OUTS:
        aps[name] = nc.dram_tensor(f"out_{name}", shape, F32, kind="ExternalOutput").ap()
    program(nc, aps)
    r = run_bass_kernel_spmd(nc, [arrays], core_ids=[0])
    return tuple(r.results[0][f"out_{name}"] for name, _ in OUTS)
```

```python
from contextlib import ExitStack

import numpy as np
import concourse.bass as bass
from concourse import mybir

F32 = mybir.dt.float32
I32 = mybir.dt.int32
ALU = mybir.AluOpType
ACT = mybir.ActivationFunctionType
AX = mybir.AxisListType

P = 128
D = 1024
KC = D // P
NT = 3
NTOK = NT * P
Q_LORA, KV_LORA, ROPE, NOPE, VH, H = 512, 256, 32, 64, 64, 8
QKH = NOPE + ROPE
FNW = 512
TOKW = Q_LORA + KV_LORA + ROPE + FNW
GATE0 = TOKW
GRID_W = 64
NG, EPG = 4, 4
NE = NG * EPG
DE = 512
EPS = 1e-6
SCALE = QKH ** -0.5
SLOTS = 64
MAX_TILES = NTOK // SLOTS
ALL_TILES = NE + 2 * NTOK // SLOTS
SLOT_ROWS = -(-(ALL_TILES + 1) * SLOTS // P) * P
CUT = 704
PIECE = 4096
TOKK = 5
RING1 = 4
ESLOTS = 3

C_ID, C_ONE, C_TRI, C_FS, C_SL, C_SC = 0, 128, 256, 384, 512, 1536
C_RC, C_RS, C_DESC, C_STEP, C_EARLIER, C_IOTA = 1792, 1824, 1856, 1860, 1866, 2122
NCON = 2186


def constants():
    t = np.zeros((P, NCON), np.float64)
    i = np.arange(P)
    t[:, C_ID:C_ID + P] = np.eye(P)
    t[:, C_ONE:C_ONE + P] = 1.0
    t[:, C_TRI:C_TRI + P] = i[:, None] < i[None, :]
    t[:, C_STEP:C_STEP + 6] = np.array([-1] + [SLOTS * k for k in range(1, MAX_TILES)])[None, :]
    t[:, C_EARLIER:C_EARLIER + NE * NE] = np.tril(np.ones((NE, NE)), -1).reshape(1, -1)
    ang = 2 * np.pi * np.outer(i, i) / P
    t[:, C_FS:C_FS + P] = -np.sin(ang) / np.sqrt(P)
    s = 2 * P
    for ch in range(2):
        a = 2 * np.pi * (np.outer(i + ch * P, np.arange(s)) % s) / s
        t[:, C_SL + ch * 512:C_SL + ch * 512 + 256] = np.cos(a) / np.sqrt(s)
        t[:, C_SL + ch * 512 + 256:C_SL + ch * 512 + 512] = np.sin(a) / np.sqrt(s)
    t[:, C_SC:C_SC + P] = np.cos(ang) / np.sqrt(P)
    t[:, C_SC + P:C_SC + 2 * P] = np.sin(ang) / np.sqrt(P)
    freqs = np.float32(10000.0) ** (-np.arange(8, dtype=np.float32) / np.float32(8))
    for tt in range(2):
        pos = i + tt * P
        for ax, q in enumerate((pos // GRID_W, pos % GRID_W)):
            a = (q.astype(np.float32)[:, None] * freqs[None, :]).astype(np.float32).astype(np.float64)
            t[:, C_RC + tt * 16 + ax * 8:C_RC + tt * 16 + ax * 8 + 8] = np.cos(a)
            t[:, C_RS + tt * 16 + ax * 8:C_RS + tt * 16 + ax * 8 + 8] = np.sin(a)
    t[:, C_DESC:C_DESC + 4] = np.arange(4, 0, -1)[None, :]
    t[:, C_IOTA:C_IOTA + SLOTS] = np.arange(SLOTS)[None, :]
    return t.astype(np.float32)


class Steps:

    def __init__(self, sem, names):
        self.sem, self.names, self.count = sem, names, 0
        self.value = {n: i + 1 for i, n in enumerate(names)}
        assert len(self.value) == len(names)

    def at(self, name):
        return self.sem, self.value[name]

    def mark(self, name):
        assert self.names[self.count] == name, (name, self.names[self.count])
        self.count += 1
        return self.sem, 1


PARTS = {"g": 2, "mod": 4}
FILL = [("g", 13), ("g", 14), ("g", 15), ("mod", 1, 0), ("mod", 1, 1), ("g", 12), ("g", 8), ("mod", 1, 2), ("g", 9), ("mod", 1, 3),
        ("g", 10), ("g", 11), ("g", 4), ("mod", 2, 0), ("g", 5), ("mod", 2, 1), ("g", 6), ("g", 7),
        ("g", 0), ("mod", 2, 2), ("g", 1), ("mod", 2, 3), ("g", 2), ("g", 3)]
FILL = [x for f in FILL for x in ([(f[0], f[1], 0), (f[0], f[1], 1)] if len(f) == 2 else [f])]
EARLY_BANK = {13: 5, 14: 6, 15: 0}
EARLY = 6
UNITS = [(h, t) for h in range(H) for t in range(NT)]
AT = [[FILL[n] for n in range(EARLY, len(FILL)) if (n - EARLY) * len(UNITS) // (len(FILL) - EARLY) == u] for u in range(len(UNITS))]


def ends(u):
    return [(k, c) for k, c, part in AT[u] if part == PARTS[k] - 1]
MIDDLE = [("tok", 0), ("T", "c"), ("tok", 1), ("T", 0), ("tok", 2), ("G", 13), ("KV", "c"), ("T", 1), ("G", 14), ("FA", 0), ("FA", 1),
          ("KV", 0), ("XK", "c"), ("QB", 0), ("T", 2), ("FA", 2), ("XK", 0), ("KV", 1), ("FA", 3), ("XQ", 0),
          ("QB", 1), ("XK", 1), ("KV", 2), ("FB", 0), ("XQ", 1), ("QB", 2), ("XK", 2), ("FB", 1), ("G", 15), ("XQ", 2)]
ROW = {"c": 3, 0: 0, 1: 1, 2: 2}
KSLOT = {"c": 0, 1: 1, 2: 2, 0: 3}


DVE_MIDDLE = [("tok", 0), ("T", "c"), ("tok", 1), ("T", 0), ("tok", 2), ("kh", "c"), ("T", 1), ("kn", "c"),
              ("kh", 0), ("kn", 0), ("T", 2), ("qn", 0), ("kh", 1), ("kn", 1), ("qn", 1), ("kh", 2), ("kn", 2), ("qn", 2)]
ACT_MIDDLE = [("tok", 0), ("tok", 1), ("tok", 2), ("vv", "c"), ("rk", "c"), ("ge", 13), ("ge", 14), ("fA", 0), ("fA", 1), ("vv", 0), ("rk", 0),
              ("kT", "c"), ("qh", 0), ("rq", 0), ("fA", 2), ("kT", 0), ("vv", 1), ("rk", 1), ("fA", 3), ("qT", 0),
              ("qh", 1), ("rq", 1), ("kT", 1), ("vv", 2), ("rk", 2), ("yT", 0), ("qT", 1), ("qh", 2), ("rq", 2),
              ("kT", 2), ("yT", 1), ("ge", 15), ("qT", 2)]


def pe_steps():
    s = ["vecT"] + [f"xT{t}" for t in range(NT)] + ["mod0", "modT"]
    s += [f"fill g {i}" if k == "G" else f"{k} {i}" for k, i in MIDDLE]
    s += ["S 0"]
    for u in range(len(UNITS)):
        if u + 1 < len(UNITS):
            s.append(f"S {u + 1}")
        s += ["fill %s %d" % f for f in ends(u)]
        s.append(f"PT {u}")
        if u:
            s.append(f"PV {u - 1}")
    s += [f"PV {len(UNITS) - 1}"]
    s += [f"AF {c}" for c in range(KC)] + [f"out {t} {half}" for t in range(NT) for half in range(2)]
    s += ["h2T 0", "h2T 1", "logT 0", "h2T 2", "logT 1", "logT 2", "router", "rank"]
    return s


def dve_order():
    s = ["silu c", "vec out"] + [f"xn {t}" for t in range(NT)] + ["modrow 0", "mod cols"]
    s += [f"hT {t}" for t in range(NT)]
    for what, i in DVE_MIDDLE:
        s += [n % i for n in {"tok": ["nr %s", "ckv %s"], "T": ["Tev %s"], "kh": ["kh %s"], "kn": ["rk %s", "kn %s"],
                              "qn": ["rq %s", "qn %s"]}[what]]
    s += ["mx 0"]
    for u in range(len(UNITS)):
        s.append(f"pn {u}")
        if u + 1 < len(UNITS):
            s.append(f"mx {u + 1}")
        s += ["modrow %d" % c for k, c in (ends(u - 1) if u else []) if k == "mod"]
        if u and u % 6 == 0:
            s.append(f"oT {u // 6 - 1}")
    s += ["oT 3"] + [f"u {c}" for c in range(KC)]
    for t in range(NT):
        s += [f"{w} {t} {half}" for w in ("x1", "h2") for half in range(2)]
    return s + ["masks", "slots", "tab"]


def act_order():
    s = ["exp c", "rsx", *(f"hT {t}" for t in range(NT))]
    for what, i in ACT_MIDDLE:
        s += [n % i for n in {"tok": ["rs %s", "kpe %s", "fn %s", "qan %s"], "vv": ["vv %s"], "rk": ["rk %s"],
                              "qh": ["qh %s"], "rq": ["rq %s"], "kT": ["kT %s"], "qT": ["qT %s"], "fA": ["fA %s"],
                              "yT": ["yT %s"], "ge": ["ge %s"]}[what]]
    s += ["p 0"]
    for u in range(len(UNITS)):
        if u + 1 < len(UNITS):
            s.append(f"p {u + 1}")
        s += ["ge %d" % c for k, c in ends(u) if k == "g"]
        s.append(f"pT {u}")
    for t in range(NT):
        s += [f"rs2 {t}"]
        if t:
            s.append(f"h2T {t - 1}")
    return s + ["h2T 2", "logT 1", "logT 2", "weights"]


def program(nc, a):
    ctx = ExitStack()
    with ctx:
        def sb(name, shape, dt=F32):
            return ctx.enter_context(nc.sbuf_tensor(name, shape, dt))

        def sem(name):
            return ctx.enter_context(nc.semaphore(name))

        con = sb("con", [P, NCON])
        x_sb = sb("x_sb", [P, NT, D])
        hT = sb("hT", [P, KC, NTOK])
        work = sb("work", [P, 5632])
        yTt = sb("yTt", [P, 1536])
        big = sb("big", [P, 9 * PIECE])
        small = sb("small", [P, 726])
        tab = sb("tab", [1, 67], I32)
        sidx = sb("sidx", [P, 6], I32)

        ident, ones = con[:, C_ID:C_ID + P], con[:, C_ONE:C_ONE + P]
        tri, steps6 = con[:, C_TRI:C_TRI + P], con[:, C_STEP:C_STEP + 6]
        iota = con[:, C_IOTA:C_IOTA + SLOTS]
        earlier = con[:, C_EARLIER:C_EARLIER + NE * NE].rearrange("p (n k) -> p n k", n=NE)
        dft_c, dft_s = con[:, C_SC:C_SC + P], con[:, C_FS:C_FS + P]

        def piece(n):
            return big[:, n * PIECE:(n + 1) * PIECE]

        wqb = x_sb[:, :, :].rearrange("p a b -> p (a b)").rearrange("p (k n) -> p k n", k=4)
        vv = work[:, 0:2048].rearrange("p (s n) -> p s n", s=4)
        qaT = work[:, 2048:3584].rearrange("p (k n) -> p k n", k=4)
        ckvT = work[:, 3584:4608].rearrange("p (k r n) -> p k r n", k=2, r=4)
        ckv = work[:, 4608:5632].rearrange("p (r n) -> p r n", r=4)
        wf_a, wf_b = x_sb[:, :, :], work[:, 2048:3072]
        yT = yTt[:, :].rearrange("p (g n) -> p g n", g=4)
        misc = piece(4)
        wkvb = misc[:, 0:2048].rearrange("p (k n) -> p k n", k=2)
        bmod = misc[:, 2048:3584].rearrange("p (j n) -> p j n", j=3)
        modrow = misc[:, 3584:4096]
        A0 = 5 * PIECE
        gates = big[:, A0:A0 + 6144].rearrange("p (c n) -> p c n", c=16)
        qan = big[:, A0:A0 + 1024].rearrange("p (b n) -> p b n", b=2)
        fn = big[:, A0 + 1024:A0 + 2560].rearrange("p (t n) -> p t n", t=NT)
        qh = big[:, A0 + 2560:A0 + 3328].rearrange("p (h n) -> p h n", h=H)
        kh = big[:, A0 + 3328:A0 + 4096].rearrange("p (h n) -> p h n", h=H)
        sq = big[:, A0 + 4096:A0 + 4864]
        sqa = big[:, A0 + 4864:A0 + 5888]
        qT = big[:, A0 + 6144:A0 + 9216].rearrange("p (h n) -> p h n", h=H)
        uT = qT
        kT = big[:, A0 + 9216:A0 + 13312].rearrange("p (h n) -> p h n", h=H)
        fA = big[:, A0 + 13312:A0 + 16384].rearrange("p (g n) -> p g n", g=4)
        c32 = big[:, A0 + 13312:A0 + 13568].rearrange("p (k m) -> p k m", k=KC)
        c32_late = bmod[:, 0, 0:256].rearrange("p (k m) -> p k m", k=KC)
        vrow = big[:, A0 + 13568:A0 + 13696]
        srow = big[:, A0 + 13696:A0 + 13824]
        erow = big[:, A0 + 13824:A0 + 13952]
        probs = big[:, A0 + 13312:A0 + 14080].rearrange("p (b n) -> p b n", b=2)
        pT = big[:, A0 + 14080:A0 + 14848].rearrange("p (b n) -> p b n", b=2)
        oT = big[:, A0 + 14848:A0 + 16384].rearrange("p (c n) -> p c n", c=4)
        bc = big[:, A0:A0 + 6144].rearrange("p (v r n) -> p v r n", v=3, r=2)
        g2b = big[:, A0 + 9216:A0 + 10240]
        otmp = big[:, A0 + 10240:A0 + 11264]
        junk = big[:, A0 + 11424:A0 + 12448]
        g5 = piece(5)[:, 0:2048].rearrange("p (r n) -> p r n", r=2)
        wr = big[:, A0 + 11264:A0 + 11424].rearrange("p (k n) -> p k n", k=KC)
        h2T = big[:, A0 + 13312:A0 + 16384].rearrange("p (k n) -> p k n", k=KC)
        h2 = hT[:, :, :].rearrange("p a b -> p (a b)").rearrange("p (t n) -> p t n", t=NT)
        ybuf = big[:, 3 * PIECE:3 * PIECE + 6144].rearrange("p (t c n) -> p t c n", t=NT, c=2)
        xg = work[:, 0:3072].rearrange("p (s j n) -> p s j n", s=ESLOTS, j=2)
        xeT = work[:, 3072:3584].rearrange("p (i g s) -> p i g s", i=4, g=2)
        eg = work[:, 3584:3840]
        tile0 = work[:, 3584:3776].rearrange("p (t n) -> p t n", t=NT)
        actv = work[:, 3840:4096]
        actT = work[:, 4096:4352].rearrange("p (j g s) -> p j g s", j=2, g=2)
        ye = hT[:, :, :].rearrange("p a b -> p (a b)").rearrange("p (s n) -> p s n", n=512)

        off = [0]

        def take(n):
            v = small[:, off[0]:off[0] + n]
            off[0] += n
            return v
        kvg, qng, kng, rb = take(256), take(96), take(96), take(20)
        g1T, qgT, shT, a1T = take(8), take(4), take(16), take(16)
        kpe = take(128).rearrange("p (r n) -> p r n", r=4)
        ssx, ssy, srt, msx, rsx, nwx = (take(3) for _ in range(6))
        ss, ms, rs, nw = take(10), take(10), take(10), take(10)
        mx, sm, ri = take(4), take(4), take(4)
        epsc = take(1)
        fsl = take(6).rearrange("p (t c) -> p t c", t=NT)
        wsl = take(6).rearrange("p (t c) -> p t c", t=NT)
        shT = shT.rearrange("p (r k) -> p r k", r=2)
        a1T = a1T.rearrange("p (r k) -> p r k", r=2)
        assert off[0] <= 726
        ro = [4352]

        def rtake(n, pat=None, **kw):
            v = work[:, ro[0]:ro[0] + n]
            ro[0] += n
            return v.rearrange(pat, **kw) if pat else v
        lg = rtake(60, "p (t n) -> p t n", t=NT)
        rm, rsum, gp, rm1, rm2, rd, rr = (rtake(3) for _ in range(7))
        t4, ohg, esel, oh1, oh2, e2 = (rtake(12, "p (t n) -> p t n", t=NT) for _ in range(6))
        prod = rtake(48, "p (t g e) -> p t g e", t=NT, g=4)
        MMf = rtake(64)
        MM = MMf[:, 0:48].rearrange("p (t n) -> p t n", t=NT)
        slot = rtake(48, "p (t n) -> p t n", t=NT)
        M12 = rtake(96, "p (c t n) -> p c t n", c=2, t=NT)
        logT = rtake(NTOK)
        over = rtake(NE * 6, "p (e k) -> p e k", e=NE)
        before = rtake(NE * NE, "p (e k) -> p e k", e=NE)
        assert ro[0] <= 5632 - 99
        nt3, cum = rtake(48, "p (v n) -> p v n", v=3), rtake(51, "p (v n) -> p v n", v=3)

        B = [ctx.enter_context(nc.psum_tensor(f"bank{i}", [P, 512], F32)) for i in range(8)]
        modd = nc.dram_tensor("mod_rows", (2, 4096), F32, kind="Internal").ap()
        slots = nc.dram_tensor("slots", (SLOT_ROWS, D), F32, kind="Internal").ap()

        pe_done, v_done, a_done = sem("pe_done"), sem("dve_done"), sem("act_done")
        PE = Steps(pe_done, pe_steps())
        V = Steps(v_done, dve_order())
        A = Steps(a_done, act_order())
        zero_done = sem("zero_done")
        d_vec, d_con, d_con2, d_fnet, d_small, d_cache, d_kvb, d_qb, d_bmod = map(sem, ("d_vec", "d_con", "d_con2", "d_fnet", "d_small", "d_cache", "d_kvb", "d_qb", "d_bmod"))
        d_x = [sem(f"d_x{t}") for t in range(NT)]
        d_xre, d_mod1, d_mod2, d_bc, d_g5, d_out, d_outc = map(sem, ("d_xre", "d_mod1", "d_mod2", "d_bc", "d_g5", "d_out", "d_outc"))
        d_tokw = [sem(f"d_tokw{q}") for q in range(2)]
        d_ring = [sem(f"d_ring{i}") for i in range(RING1)]
        d_gu = [sem(f"d_gu{s}") for s in range(ESLOTS)]
        d_dn = [sem(f"d_dn{s}") for s in range(ESLOTS)]
        d_scat, d_xmore, d_ymore = map(sem, ("d_scatter", "d_xg_more", "d_y_more"))
        d_xg = [sem(f"d_xg{s}") for s in range(ESLOTS)]
        d_y0 = [sem(f"d_y_slot{s}") for s in range(ESLOTS)]
        d_gath = [sem(f"d_gather{t}") for t in range(NT)]
        all_stored, onehot0, gathered0, rows0 = map(sem, ("all_stored", "onehot_tile0", "gathered_tile0", "rows_tile0"))
        t_g, t_u, t_xeTp, t_xeTs = map(sem, ("t_gate", "t_up", "t_xeT_psum", "t_xeT_sbuf"))
        t_exp, t_act, t_aTp, t_aTs, t_y, t_ye = map(sem, ("t_exp", "t_act", "t_actT_psum", "t_actT_sbuf", "t_down", "t_y_sbuf"))
        fin, fin_pool, weighted, summed, gated = map(sem, ("y_ready", "y_ready_pool", "y_weighted", "y_summed", "y_gated"))

        tokw0 = big[:, A0 + 6144:A0 + 6144 + TOKK * TOKW].rearrange("p (k n) -> p k n", k=TOKK)
        win = a["w_in"][0].rearrange("(k p) n -> p k n", p=P)
        wmod = a["w_mod"][0].rearrange("(k p) n -> p k n", p=P)
        ring, n = {}, 0
        order = [("mod0", q) for q in range(4)] + [("tokw", 1), ("gate", 0), ("mod1", 0), ("mod1", 1), ("gate", 1), ("mod1", 2),
                                                   ("mod1", 3), ("gate", 2), ("mod2", 0), ("mod2", 1), ("gate", 3), ("mod2", 2),
                                                   ("mod2", 3), ("attn_o", 0), ("out", 0), ("out", 1)]
        for n, key in enumerate(order):
            ring[key] = (n % RING1, n // RING1 + 1)

        def arrived(eng, key):
            s, k = ring[key]
            eng.wait_ge(d_ring[s], 16 * k)

        def rpiece(key, width):
            s = ring[key][0]
            return big[:, s * PIECE:s * PIECE + (PIECE // width) * width].rearrange("p (k n) -> p k n", n=width)

        used = {("mod0", q): "mod0" for q in range(4)}
        used[("tokw", 1)] = "tok 2"
        GCH = {0: [12, 13, 14, 15], 1: [8, 9, 10, 11], 2: [4, 5, 6, 7], 3: [0, 1, 2, 3]}
        used |= {("gate", q): "fill g %d" % [f[1] for f in FILL if f[0] == "g" and f[1] in GCH[q]][-1] for q in range(4)}
        last = None
        for k, c, part in reversed(FILL[EARLY:]):
            if part == PARTS[k] - 1:
                last = "fill %s %d" % (k, c)
            if k == "mod":
                used[(f"mod{c}", part)] = last

        def routed(eng, e):
            return (eng.value_load(tab[0:1, bass.ds(16 + e, 1)], min_val=0, max_val=ALL_TILES),
                    eng.value_load(tab[0:1, bass.ds(e, 1)], min_val=1, max_val=MAX_TILES))

        block = ctx.enter_context(nc.Block())

        @block.sync
        def _(sp):
            sp.dma_start(vrow[0:8, :], a["c_ctx"].rearrange("(k n) -> k n", n=P)).then_inc(d_vec, 16)
            sp.dma_start(vrow[8:16, :], a["c"].rearrange("b (k n) -> (b k) n", n=P)).then_inc(d_vec, 16)
            sp.dma_start(vrow[16:24, :], a["norm1_g"].rearrange("b (k n) -> (b k) n", n=P)).then_inc(d_vec, 16)
            sp.dma_start(vrow[24:28, :], a["q_a_norm_g"].rearrange("b (k n) -> (b k) n", n=P)).then_inc(d_vec, 16)
            sp.dma_start(con[:, 0:128], a["const_table"][:, 0:128]).then_inc(d_con, 16)
            sp.dma_start(x_sb[:, 0, :], a["x_prompt"][0]).then_inc(d_x[0], 16)
            for q in range(4):
                if q < 2:
                    sp.dma_start(x_sb[:, 1 + q, :], a["x_sample"][0, q * P:(q + 1) * P, :]).then_inc(d_x[1 + q], 16)
                sp.dma_start(rpiece(("mod0", q), 2048), wmod[:, 2 * q:2 * q + 2, 0:2048]).then_inc(d_ring[q], 16)
            sp.wait_ge(zero_done, 2)
            for r in range(2):
                sp.dma_start(bmod[r:r + 97:32, :, :], a["b_mod"][0].rearrange("(j g n) -> g j n", j=3, g=4)).then_inc(d_bmod, 16)

            def load(key):
                n = order.index(key)
                if n >= RING1:
                    sp.wait_ge(*PE.at(used[order[n - RING1]]))
                kind, q = key
                s = ring[key][0]
                if kind.startswith("mod"):
                    j = int(kind[3])
                    dst, src = rpiece(key, 2048), wmod[:, 2 * q:2 * q + 2, 2048 * j:2048 * j + 2048]
                elif kind == "tokw":
                    dst, src = rpiece(key, TOKW)[:, 0:KC - TOKK, :], win[:, TOKK:KC, 0:TOKW]
                elif kind == "gate":
                    dst = rpiece(key, 512)
                    c0 = GATE0 + GCH[q][0] * P
                    src = win[:, :, c0:c0 + 512]
                elif kind == "out":
                    dst, src = rpiece(key, D), a["w_out"][0].rearrange("(k p) n -> p k n", p=P)[:, 4 * q:4 * q + 4, :]
                else:
                    dst, src = rpiece(key, D), a["w_attn_o"][0].rearrange("(k p) n -> p k n", p=P)
                sp.dma_start(dst, src).then_inc(d_ring[s], 16)

            wg = a["w_exp_gate"][0].rearrange("e (k p) n -> p e k n", p=P)
            wu = a["w_exp_up"][0].rearrange("e (k p) n -> p e k n", p=P)
            wd = a["w_exp_down"][0].rearrange("e (k p) n -> p e k n", p=P)

            def load_gate(e, s):
                sp.dma_start(piece(3 * s).rearrange("p (k n) -> p k n", n=DE), wg[:, e]).then_inc(d_gu[s], 16)

            def load_up(e, s):
                sp.dma_start(piece(3 * s + 1).rearrange("p (k n) -> p k n", n=DE), wu[:, e]).then_inc(d_gu[s], 16)

            def load_down(e, s):
                sp.dma_start(piece(3 * s + 2).rearrange("p (k n) -> p k n", n=D), wd[:, e]).then_inc(d_dn[s], 16)

            for q, (k0, k1) in enumerate(((0, 2), (2, TOKK))):
                sp.dma_start(tokw0[:, k0:k1, :], win[:, k0:k1, 0:TOKW]).then_inc(d_tokw[q], 16)
            sp.dma_start(kvg, a["kv_a_norm_g"].to_broadcast([P, KV_LORA])).then_inc(d_small, 16)
            sp.dma_start(qng, a["q_norm_g"].to_broadcast([P, QKH])).then_inc(d_small, 16)
            sp.dma_start(kng, a["k_norm_g"].to_broadcast([P, QKH])).then_inc(d_small, 16)
            sp.dma_start(rb[:, 0:4], a["b_router_group"].to_broadcast([P, NG])).then_inc(d_small, 16)
            sp.dma_start(rb[:, 4:20], a["b_router_expert"].to_broadcast([P, NE])).then_inc(d_small, 16)
            sp.dma_start(ckv[:, 3, :], a["cache_ckv"][0, 0]).then_inc(d_cache, 16)
            sp.dma_start(kpe[:, 3, :], a["cache_kpe"][0, 0]).then_inc(d_cache, 16)
            load(("tokw", 1))
            sp.dma_start(wkvb, a["w_kv_b"][0].rearrange("(k p) n -> p k n", p=P)).then_inc(d_kvb, 16)
            load(("gate", 0))
            sp.dma_start(con[:, 128:NCON], a["const_table"][:, 128:NCON]).then_inc(d_con2, 16)
            sp.wait_ge(*PE.at("xT2"))
            sp.dma_start(wqb, a["w_q_b"][0].rearrange("(k p) n -> p k n", p=P)).then_inc(d_qb, 16)
            sp.wait_ge(*V.at("ckv 0"))
            sp.wait_ge(*A.at("kpe 0"))
            sp.dma_start(a["new_ckv"][0, 0], ckv[:, 0, :]).then_inc(d_outc, 16)
            sp.dma_start(a["new_kpe"][0, 0], kpe[:, 0, :]).then_inc(d_outc, 16)
            for key in order[6:9]:
                load(key)
            sp.wait_ge(*PE.at("QB 2"))
            wfn = a["w_fnet"][0].rearrange("(k p) n -> p k n", p=P)
            sp.dma_start(wf_a, wfn[:, 0:3, :]).then_inc(d_fnet, 16)
            sp.dma_start(wf_b, wfn[:, 3, :]).then_inc(d_fnet, 16)
            for key in order[9:14]:
                load(key)
            sp.wait_ge(*V.at("modrow 1"))
            for r in range(2):
                sp.dma_start(modd[r, 0:2048].rearrange("(g n) -> g n", g=4), modrow[r:r + 97:32, :]).then_inc(d_mod1, 16)
            for key in order[14:17]:
                load(key)
            sp.wait_ge(*V.at("modrow 2"))
            for r in range(2):
                sp.dma_start(modd[r, 2048:4096].rearrange("(g n) -> g n", g=4), modrow[r:r + 97:32, :]).then_inc(d_mod2, 16)
            sp.wait_ge(*PE.at("fill mod 2"))
            load(order[17])
            load_gate(0, 0)
            for key in order[18:20]:
                load(key)
            sp.wait_ge(*PE.at("AF 7"))
            sp.dma_start(x_sb[:, 0, :], a["x_prompt"][0]).then_inc(d_xre, 16)
            sp.dma_start(x_sb[:, 1:3, :], a["x_sample"][0].rearrange("(t p) n -> p t n", p=P)).then_inc(d_xre, 16)
            sp.wait_ge(*V.at("u 7"))
            sp.wait_ge(d_mod1, 32)
            sp.wait_ge(d_mod2, 32)
            for v in range(3):
                for r in range(2):
                    sp.dma_start(bc[:, v, r, :], modd[r:r + 1, v * D:(v + 1) * D].to_broadcast([P, D])).then_inc(d_bc, 16)
            sp.dma_start(g2b, a["norm2_g"].to_broadcast([P, D])).then_inc(d_bc, 16)
            sp.dma_start(wr[:, :, 0:NG], a["w_router_group"][0].rearrange("(k p) n -> p k n", p=P)).then_inc(d_bc, 16)
            sp.dma_start(wr[:, :, NG:NG + NE], a["w_router_expert"][0].rearrange("(k p) n -> p k n", p=P)).then_inc(d_bc, 16)

            load_up(0, 0)
            load_up(1, 1)
            sp.wait_ge(*PE.at("out 2 1"))
            load_down(0, 0)
            load_gate(1, 1)
            sp.wait_ge(*V.at("h2 2 1"))
            load_down(1, 1)
            load_gate(2, 2)

            def rows(t):
                t = nc.s_assert_within(t, 0, ALL_TILES - 1, skip_runtime_bounds_check_because=
                                       "16 experts' counts, 768 in all, are at most 28 tiles")
                return sp.snap(t * SLOTS)

            def load_tile(row, s, j, done):
                for g in range(2):
                    sp.dma_start(xg[SLOTS * g:SLOTS * (g + 1), s, j, :], slots[bass.ds(row, SLOTS), g * 512:(g + 1) * 512]).then_inc(done, 16)

            def count_only(s, dst):
                for g in range(2):
                    sp.dma_start(dst[g:g + 1, :], a["const_table"][0:1, 0:512]).then_inc(d_xg[s], 16)

            def second(first, tiles, s, spare):
                with sp.If(tiles > 1):
                    load_tile(rows(first + 1), s, 1, d_xg[s])
                with sp.If(tiles < 2):
                    count_only(s, spare)

            def load_rows(row, first, tiles, s):
                load_tile(row, s, 0, d_xg[s])
                second(first, tiles, s, xg[:, s, 1, :])

            sp.wait_ge(d_scat, 6 * 16)
            sp.wait_ge(*V.at("tab"))
            load_up(2, 2)
            second(*routed(sp, 0), 0, yTt[:, 512:1024])
            first, tiles = routed(sp, 1)
            load_rows(rows(first), first, tiles, 1)
            load_down(2, 2)
            first, tiles = routed(sp, 2)
            load_rows(rows(first), first, tiles, 2)
            count_only(0, yTt[:, 0:512])

            def store(T2, row, buf, done):
                sp.wait_ge(t_ye, T2)
                for g in range(2):
                    sp.dma_start(slots[bass.ds(row, SLOTS), g * 512:(g + 1) * 512], ye[SLOTS * g:SLOTS * (g + 1), buf, :]).then_inc(done, 16)

            def results(e, s, first, tiles):
                store(sp.snap(first + 2), rows(first), s, d_y0[s])
                with sp.If(tiles > 1):
                    store(sp.snap(first + 3), rows(first + 1), ESLOTS, d_ymore)
                    with sp.If(tiles > 2):
                        with sp.Fori(2, tiles) as j:
                            row = rows(first + j)
                            load_tile(row, s, 1, d_xmore)
                            store(sp.snap(first + j + 2), row, ESLOTS, d_ymore)

            def expert(e, s):
                first, tiles = routed(sp, e)
                next_first, next_tiles = routed(sp, e + ESLOTS)
                next_row, last = rows(next_first), sp.snap(first + tiles)

                def refill():
                    load_rows(next_row, next_first, next_tiles, s)
                    load_gate(e + ESLOTS, s)
                    load_up(e + ESLOTS, s)

                with sp.If(tiles < 3):
                    sp.wait_ge(t_u, last)
                    refill()
                results(e, s, first, tiles)
                with sp.If(tiles > 2):
                    refill()
                load_down(e + ESLOTS, s)

            with sp.Fori(0, (NE - ESLOTS) // ESLOTS) as g:
                for s in range(ESLOTS):
                    expert(g * ESLOTS + s, s)
            expert(NE - ESLOTS - 1, (NE - ESLOTS - 1) % ESLOTS)
            results(NE - 3, (NE - 3) % ESLOTS, *routed(sp, NE - 3))
            for r in range(2):
                sp.dma_start(g5[:, r, :], modd[r:r + 1, 3 * D:4 * D].to_broadcast([P, D])).then_inc(d_g5, 16)
            results(NE - 2, (NE - 2) % ESLOTS, *routed(sp, NE - 2))
            results(NE - 1, (NE - 1) % ESLOTS, *routed(sp, NE - 1))
            for t in range(NT):
                sp.wait_ge(fin, t + 1)
                sp.wait_ge(fin_pool, t + 1)
                dst = a["y_prompt"][0] if t == 0 else a["y_sample"][0, (t - 1) * P:t * P, :]
                sp.dma_start(dst, x_sb[:, t, :]).then_inc(d_out, 16)
            sp.wait_ge(d_out, 16 * NT)
            sp.wait_ge(d_outc, 32)

        @block.gpsimd
        def _(pool):
            nc.gpsimd.memset(c32, 0.0).then_inc(zero_done, 1)
            nc.gpsimd.memset(bmod, 0.0).then_inc(zero_done, 1)
            nc.gpsimd.memset(epsc, EPS).then_inc(zero_done, 1)
            nc.gpsimd.memset(yTt[:, 0:D], 0.0).then_inc(zero_done, 1)
            pool.wait_ge(*V.at("slots"))
            for s in range(ESLOTS):
                pool.wait_ge(d_y0[s], 16)
            pool.wait_ge(d_ymore, 16)
            for t in range(NT):
                for c in range(2):
                    nc.gpsimd.indirect_dma_start(slots, bass.IndirectOffsetOnAxis(ap=sidx[:, 2 * t + c:2 * t + c + 1], axis=0),
                                                 h2[:, t, :], None).then_inc(d_scat, 16)
            pool.wait_ge(all_stored, 1)
            for t in range(NT):
                for c in range(2):
                    nc.gpsimd.indirect_dma_start(ybuf[:, t, c, :], None, slots,
                                                 bass.IndirectOffsetOnAxis(ap=sidx[:, 2 * t + c:2 * t + c + 1], axis=0)).then_inc(d_gath[t], 16)
            pool.wait_ge(d_g5, 32)
            for t in range(NT):
                y0, y1, gate = ybuf[:, t, 0, CUT:D], ybuf[:, t, 1, CUT:D], g5[:, min(t, 1), CUT:D]
                pool.wait_ge(weighted, 2 * t + 2)
                nc.gpsimd.tensor_tensor(y0, y0, y1, ALU.add).then_inc(summed, 1)
                pool.wait_ge(summed, t + 1)
                nc.gpsimd.tensor_tensor(y0, y0, gate, ALU.mult).then_inc(gated, 1)
                pool.wait_ge(gated, t + 1)
                nc.gpsimd.tensor_tensor(x_sb[:, t, CUT:D], x_sb[:, t, CUT:D], y0, ALU.add).then_inc(fin_pool, 1)

        @block.tensor
        def _(pe):
            mm, tr = nc.tensor.matmul, nc.tensor.transpose
            pe.wait_ge(d_con, 16)
            pe.wait_ge(d_vec, 64)
            tr(B[0][:, 0:28], vrow[0:28, :], ident[0:28, 0:28])
            pe.wait_ge(*V.at("silu c"))
            tr(B[0][:, 32:48], srow[0:16, :], ident[0:16, 0:16]).then_inc(*PE.mark("vecT"))
            for t in range(NT):
                pe.wait_ge(*V.at(f"xn {t}"))
                for k in range(KC):
                    i = tr(B[1 + 2 * t + k // 4][:, (k % 4) * P:(k % 4 + 1) * P], x_sb[:, t, k * P:(k + 1) * P], ident)
                i.then_inc(*PE.mark(f"xT{t}"))

            def modulation(j, bank, quarters=range(4)):
                for q in quarters:
                    arrived(pe, (f"mod{j}", q))
                    for k in (2 * q, 2 * q + 1):
                        for g in range(4):
                            i = mm(bank[32 * g:32 * g + 32, :], (c32_late if j else c32)[:, k, :],
                                   rpiece((f"mod{j}", q), 2048)[:, k % 2, 512 * g:512 * g + 512], start=(k == 0), stop=(k == KC - 1))
                return i

            pe.wait_ge(*V.at("vec out"))
            modulation(0, B[7]).then_inc(*PE.mark("mod0"))
            pe.wait_ge(*V.at("modrow 0"))
            for i4 in range(4):
                i = tr(B[0][:, i4 * P:(i4 + 1) * P], modrow[:, i4 * P:(i4 + 1) * P], ident)
            i.then_inc(*PE.mark("modT"))

            def tok(t):
                b = 1 if t % 2 == 0 else 4
                if t == 2:
                    pe.wait_ge(*A.at("qan 0"))
                    pe.wait_ge(*V.at("ckv 0"))
                else:
                    for x in ((0,), (1, 2))[t]:
                        pe.wait_ge(*V.at(f"hT {x}"))
                        pe.wait_ge(*A.at(f"hT {x}"))
                for k in range(KC):
                    if k < TOKK:
                        pe.wait_ge(d_tokw[0 if k < 2 else 1], 16)
                        w = tokw0[:, k, :]
                    else:
                        arrived(pe, ("tokw", 1))
                        w = rpiece(("tokw", 1), TOKW)[:, k - TOKK, :]
                    lhs = hT[:, k, t * P:(t + 1) * P]
                    mm(B[b][:, :], lhs, w[:, 0:512], start=(k == 0), stop=(k == KC - 1))
                    mm(B[b + 1][:, 0:288], lhs, w[:, 512:800], start=(k == 0), stop=(k == KC - 1))
                    i = mm(B[7 if t == 0 else b + 2][:, :], lhs, w[:, 800:1312], start=(k == 0), stop=(k == KC - 1))
                i.then_inc(*PE.mark(f"tok {t}"))

            def lora_T(r):
                if r == "c":
                    pe.wait_ge(d_cache, 32)
                    pe.wait_ge(*V.at("mod cols"))
                else:
                    pe.wait_ge(*V.at(f"ckv {r}"))
                    pe.wait_ge(*A.at(f"qan {r}"))
                    pe.wait_ge(*V.at("Tev %s" % {0: "c", 1: 0, 2: 1}[r]))
                    if r == 0:
                        pe.wait_ge(*A.at("fn 0"))
                    for k in range(4):
                        tr(B[7][:, k * P:(k + 1) * P], qan[:, r % 2, k * P:(k + 1) * P], ident)
                for k in range(2):
                    i = tr(B[0][:, k * P:(k + 1) * P], ckv[:, ROW[r], k * P:(k + 1) * P], ident)
                i.then_inc(*PE.mark(f"T {r}"))

            def kv_b(r):
                pe.wait_ge(*V.at(f"Tev {r}"))
                if r == "c":
                    pe.wait_ge(d_kvb, 16)
                    pe.wait_ge(*A.at("fn 2"))
                    pe.wait_ge(*A.at("qan 1"))
                else:
                    prev = {0: "c", 1: 0, 2: 1}[r]
                    pe.wait_ge(*V.at(f"kh {prev}"))
                    pe.wait_ge(*A.at(f"vv {prev}"))
                for half in range(2):
                    for k in range(2):
                        i = mm(B[3 + half][:, :], ckvT[:, k, ROW[r], :], wkvb[:, k, half * 512:(half + 1) * 512],
                               start=(k == 0), stop=(k == 1))
                i.then_inc(*PE.mark(f"KV {r}"))

            def q_b(t):
                pe.wait_ge(*V.at(f"Tev {t}"))
                if t == 0:
                    pe.wait_ge(d_qb, 16)
                    pe.wait_ge(*A.at("qan 2"))
                    pe.wait_ge(*V.at("ckv 2"))
                else:
                    pe.wait_ge(*A.at(f"qh {t - 1}"))
                for half in range(2):
                    for k in range(4):
                        i = mm(B[1 + half][:, 0:384], qaT[:, k, t * P:(t + 1) * P], wqb[:, k, half * 384:(half + 1) * 384],
                               start=(k == 0), stop=(k == 3))
                i.then_inc(*PE.mark(f"QB {t}"))

            def heads_T(src, step):
                for h in range(H):
                    i = tr(B[5 + h // 4][0:QKH, (h % 4) * P:(h % 4 + 1) * P], src[:, h, :], ident)
                i.then_inc(*PE.mark(step))

            last_x = []

            def xk(r):
                pe.wait_ge(*V.at(f"kn {r}"))
                pe.wait_ge(*A.at(last_x[-1] if last_x else "fA 1"))
                heads_T(kh, f"XK {r}")
                last_x.append(f"kT {r}")

            def xq(t):
                pe.wait_ge(*V.at(f"qn {t}"))
                pe.wait_ge(*A.at(last_x[-1]))
                heads_T(qh, f"XQ {t}")
                last_x.append(f"qT {t}")

            def fourier_seq(g):
                bl, bx = (B[5], B[6]) if g < 2 else (B[7], B[0])
                if g == 0:
                    pe.wait_ge(d_con2, 16)
                    pe.wait_ge(*A.at("fn 2"))
                    pe.wait_ge(*A.at("ge 14"))
                elif g == 2:
                    pe.wait_ge(*V.at("Tev 2"))
                else:
                    pe.wait_ge(*A.at(f"fA {g - 1}"))
                for s in range(2):
                    mm(bl[:, :], fn[:, 1 + s, g * P:(g + 1) * P], con[:, C_SL + s * 512:C_SL + (s + 1) * 512],
                       start=(s == 0), stop=(s == 1))
                mm(bx[:, 0:256], fn[:, 0, g * P:(g + 1) * P], con[:, C_SC:C_SC + 256], start=True,
                   stop=True).then_inc(*PE.mark(f"FA {g}"))

            def fourier_ch(part):
                if part == 0:
                    pe.wait_ge(*A.at("fA 3"))
                    for pair in range(2):
                        b = (B[7], B[0])[pair]
                        mm(b[:, :], dft_c, fA[:, 2 * pair:2 * pair + 2, 0:256], start=True, stop=False)
                        i = mm(b[:, :], dft_s, fA[:, 2 * pair:2 * pair + 2, 256:512], start=False, stop=True)
                else:
                    pe.wait_ge(*A.at("yT 0"))
                    mm(B[7][:, :], dft_c, fA[:, :, 512:640], start=True, stop=False)
                    i = mm(B[7][:, :], dft_s, fA[:, :, 640:768], start=False, stop=True)
                i.then_inc(*PE.mark(f"FB {part}"))

            def scores(u):
                h, t = UNITS[u]
                if u >= 2:
                    pe.wait_ge(*A.at(f"p {u - 2}"))
                else:
                    pe.wait_ge(*A.at("qT 2"))
                k0, kn = (384, P) if t == 0 else (0, 384)
                mm(B[1 + u % 2][:, 0:kn], qT[0:QKH, h, t * P:(t + 1) * P], kT[0:QKH, h, k0:k0 + kn], start=True,
                   stop=True).then_inc(*PE.mark(f"S {u}"))

            def fill(kind, c, part):
                if kind == "mod":
                    if part == 0:
                        pe.wait_ge(*(A.at("yT 1") if c == 1 else V.at("modrow 1")))
                    i = modulation(c, B[7], [part])
                else:
                    early = c in EARLY_BANK
                    bank = B[EARLY_BANK[c]] if early else B[0]
                    if part == 0:
                        if c == 15:
                            pe.wait_ge(*A.at("yT 0"))
                        elif early:
                            for prior in ("fn 1", "qan 1"):
                                pe.wait_ge(*A.at(prior))
                            pe.wait_ge(*V.at("ckv 1"))
                        else:
                            prev = [x[1] for x in FILL if x[0] == "g"][::2]
                            pe.wait_ge(*A.at("ge %d" % prev[prev.index(c) - 1]))
                            pe.wait_ge(*A.at("yT 0"))
                    q = [q for q in GCH if c in GCH[q]][0]
                    arrived(pe, ("gate", q))
                    w = rpiece(("gate", q), 512)
                    c0 = (c - GCH[q][0]) * P
                    for k in range(4 * part, 4 * part + 4):
                        i = mm(bank[:, 0:NTOK], w[:, k, c0:c0 + P], hT[:, k, :], start=(k == 0), stop=(k == KC - 1))
                if part == PARTS[kind] - 1:
                    i.then_inc(*PE.mark(f"fill {kind} {c}"))

            def probs_T(u):
                h, t = UNITS[u]
                pe.wait_ge(*V.at(f"pn {u}"))
                if u >= 2:
                    pe.wait_ge(*A.at(f"pT {u - 2}"))
                for kt in range(1 if t == 0 else 3):
                    i = tr(B[3 + u % 2][:, kt * P:(kt + 1) * P], probs[:, u % 2, kt * P:(kt + 1) * P], ident)
                i.then_inc(*PE.mark(f"PT {u}"))

            def pv(u):
                h, t = UNITS[u]
                pair = h // 2
                pe.wait_ge(*A.at(f"pT {u}"))
                if u % 6 == 0 and pair >= 2:
                    pe.wait_ge(*V.at(f"oT {pair - 2}"))
                slots = [3] if t == 0 else [0, 1, 2]
                o = B[5 + pair % 2][VH * (h % 2):VH * (h % 2) + VH, t * P:(t + 1) * P]
                for n, s in enumerate(slots):
                    i = mm(o, vv[:, s, h * VH:(h + 1) * VH], pT[:, u % 2, n * P:(n + 1) * P], start=(n == 0), stop=(n == len(slots) - 1))
                i.then_inc(*PE.mark(f"PV {u}"))

            def early_gate(c):
                for part in range(2):
                    fill("g", c, part)

            does = {"tok": tok, "T": lora_T, "KV": kv_b, "QB": q_b, "XK": xk, "XQ": xq, "FA": fourier_seq, "FB": fourier_ch,
                    "G": early_gate}
            for what, i in MIDDLE:
                does[what](i)
            scores(0)
            for u in range(len(UNITS)):
                if u + 1 < len(UNITS):
                    scores(u + 1)
                for f in AT[u]:
                    fill(*f)
                probs_T(u)
                if u:
                    pv(u - 1)
            pv(len(UNITS) - 1)

            pe.wait_ge(*V.at("oT 3"))
            arrived(pe, ("attn_o", 0))
            pe.wait_ge(d_fnet, 32)
            wa = rpiece(("attn_o", 0), D)
            for c in range(KC):
                if c >= 2:
                    pe.wait_ge(*V.at(f"u {c - 2}"))
                for k in range(4):
                    mm(B[1 + c % 2][:, 0:NTOK], wa[:, k, c * P:(c + 1) * P], oT[:, k, :], start=(k == 0), stop=(k == 3))
                for k in range(4):
                    i = mm(B[3 + c % 2][:, 0:NTOK], (wf_a[:, k, :] if k < 3 else wf_b)[:, c * P:(c + 1) * P], yT[:, k, :], start=(k == 0), stop=(k == 3))
                i.then_inc(*PE.mark(f"AF {c}"))

            OB = [(5, 6), (7, 0), (5, 6)]
            for t in range(NT):
                if t == 2:
                    pe.wait_ge(*V.at("x1 0 1"))
                for half in range(2):
                    for k in range(KC):
                        if t == 0 and half == 0:
                            pe.wait_ge(*V.at(f"u {k}"))
                            arrived(pe, ("out", k // 4))
                        w = rpiece(("out", k // 4), D)[:, k % 4, half * 512:(half + 1) * 512]
                        i = mm(B[OB[t][half]][:, :], uT[:, k, t * P:(t + 1) * P], w, start=(k == 0), stop=(k == KC - 1))
                    i.then_inc(*PE.mark(f"out {t} {half}"))
            def h2_T(t):
                if t == 2:
                    pe.wait_ge(*A.at("h2T 0"))
                b = 1 if t % 2 == 0 else 3
                for k in range(KC):
                    if k % 4 == 0:
                        pe.wait_ge(*V.at(f"h2 {t} {k // 4}"))
                    i = tr(B[b + k // 4][:, (k % 4) * P:(k % 4 + 1) * P], h2[:, t, k * P:(k + 1) * P], ident)
                i.then_inc(*PE.mark(f"h2T {t}"))

            def logits_T(t):
                pe.wait_ge(*A.at(f"h2T {t}"))
                pe.wait_ge(d_bc, 9 * 16)
                for k in range(KC):
                    i = mm(B[(0, 0, 5)[t]][0:20, t % 2 * P:t % 2 * P + P], wr[:, k, :], h2T[:, k, t * P:(t + 1) * P],
                           start=(k == 0), stop=(k == KC - 1))
                i.then_inc(*PE.mark(f"logT {t}"))

            h2_T(0)
            h2_T(1)
            logits_T(0)
            h2_T(2)
            logits_T(1)
            logits_T(2)
            for t in range(NT):
                pe.wait_ge(*A.at(f"logT {max(t, 1)}"))
                i = tr(B[7][:, t * 32:t * 32 + 20], logT[0:20, t * P:(t + 1) * P], ident[0:20, 0:20])
            i.then_inc(*PE.mark("router"))
            pe.wait_ge(*V.at("masks"))
            mm(B[0][:, 0:64], tri, MMf, start=True, stop=False)
            for x in range(NT):
                i = mm(B[0][:, 16 + 16 * x:64], ones, MMf[:, 0:48 - 16 * x], start=False, stop=(x == NT - 1))
            i.then_inc(*PE.mark("rank"))

            pe.wait_ge(onehot0, 1)
            for t in range(NT):
                for g in range(2):
                    i = mm(B[1][SLOTS * g:SLOTS * (g + 1), :], tile0[:, t, :], h2[:, t, g * 512:(g + 1) * 512], start=(t == 0), stop=(t == NT - 1))
            i.then_inc(gathered0, 1)

            def rows_T(s, j, rows_in):
                pe.wait_ge(*rows_in)
                for q in range(4):
                    i = tr(B[2][:, q * P:(q + 1) * P], xg[:, s, j, q * P:(q + 1) * P], ident)
                i.then_inc(t_xeTp, 1)

            rows_T(0, 0, (rows0, 1))
            pe.wait_ge(*V.at("tab"))

            def tile(T1, s, weights_in, between):
                wgu = big[:, 3 * s * PIECE:(3 * s + 2) * PIECE].rearrange("p (w k n) -> p w k n", w=2, k=KC)
                wdn = piece(3 * s + 2).rearrange("p (k n) -> p k n", n=D)
                pe.wait_ge(t_xeTs, T1)
                pe.wait_ge(d_gu[s], weights_in[0])
                for w in range(2):
                    for k in range(KC):
                        for g in range(2):
                            i = mm(B[4 * w][SLOTS * g:SLOTS * (g + 1), 0:256], xeT[:, k % 4, k // 4, :], wgu[:, w, k, g * 256:(g + 1) * 256],
                                   start=(k == 0), stop=(k == KC - 1))
                    i.then_inc(t_u if w else t_g, 1)
                between()
                pe.wait_ge(t_act, T1)
                for q in range(2):
                    i = tr(B[3][:, q * P:(q + 1) * P], actv[:, q * P:(q + 1) * P], ident)
                i.then_inc(t_aTp, 1)
                pe.wait_ge(t_aTs, T1)
                pe.wait_ge(d_dn[s], weights_in[1])
                pe.wait_ge(t_ye, T1)
                for f in range(4):
                    for g in range(2):
                        i = mm(B[1][SLOTS * g:SLOTS * (g + 1), :], actT[:, f % 2, f // 2, :], wdn[:, f, g * 512:(g + 1) * 512],
                               start=(f == 0), stop=(f == 3))
                i.then_inc(t_y, 1)

            def expert(e, s, n, last=False):
                first, tiles = routed(pe, e)
                more = pe.value_load(tab[0:1, bass.ds(33 + e, 1)], min_val=0, max_val=ALL_TILES)
                times = (lambda c, k: pe.snap(c * k)) if not isinstance(n, int) else (lambda c, k: c * k)
                n_gu, n_dn, n_xg = times(n, 32), times(n, 16), times(n, 64)
                s_next = (s + 1) % ESLOTS
                n_next = n_xg if s_next else times(n + 1, 64)

                def next_expert():
                    if not last:
                        rows_T(s_next, 0, (d_xg[s_next], n_next))

                def after_first():
                    with pe.If(tiles > 1):
                        rows_T(s, 1, (d_xg[s], n_xg))
                    if not last:
                        with pe.If(tiles < 2):
                            next_expert()

                def after_second():
                    if not last:
                        with pe.If(tiles < 3):
                            next_expert()

                tile(pe.snap(first + 1), s, (n_gu, n_dn), after_first)
                with pe.If(tiles > 1):
                    tile(pe.snap(first + 2), s, (n_gu, n_dn), after_second)
                    with pe.If(tiles > 2):
                        with pe.Fori(2, tiles) as j:
                            rows_T(s, 1, (d_xmore, pe.snap((more + j) * 32 - 32)))
                            tile(pe.snap(first + j + 1), s, (n_gu, n_dn), lambda: None)
                        next_expert()

            with pe.Fori(0, NE // ESLOTS) as g:
                for s in range(ESLOTS):
                    expert(g * ESLOTS + s, s, g + 1)
            expert(NE - 1, (NE - 1) % ESLOTS, NE // ESLOTS + 1, last=True)

        @block.vector
        def _(v):
            ts, tt, cp, stt = nc.vector.tensor_scalar, nc.vector.tensor_tensor, nc.vector.tensor_copy, nc.vector.scalar_tensor_tensor

            def order(eng=v):
                eng.drain()

            def rsqrt(r, m, w):
                tt(w, r, r, ALU.mult)
                order()
                tt(w, w, m, ALU.mult)
                order()
                ts(w, w, -0.5, 1.5, ALU.mult, ALU.add)
                order()
                return tt(r, r, w, ALU.mult)

            v.wait_ge(*A.at("exp c"))
            ts(erow[0:16, :], erow[0:16, :], 1.0, None, ALU.add)
            order()
            nc.vector.reciprocal(erow[0:16, :], erow[0:16, :])
            order()
            tt(srow[0:16, :], vrow[0:16, :], erow[0:16, :], ALU.mult).then_inc(*V.mark("silu c"))
            v.wait_ge(*PE.at("vecT"))
            cp(g1T, B[0][:, 16:24])
            cp(qgT, B[0][:, 24:28])
            v.wait_ge(zero_done, 3)
            cp(c32[:, :, 0:2], B[0][:, 32:48].rearrange("p (r k) -> p k r", r=2)).then_inc(*V.mark("vec out"))
            v.wait_ge(*A.at("rsx"))
            ts(msx, ssx, EPS, None, ALU.add)
            order()
            rsqrt(rsx, msx, nwx)
            order()
            for t in range(NT):
                ts(x_sb[:, t, :], x_sb[:, t, :], rsx[:, t:t + 1], None, ALU.mult).then_inc(*V.mark(f"xn {t}"))
            v.wait_ge(*PE.at("mod0"))
            v.wait_ge(d_bmod, 32)
            tt(modrow, B[7][:, :], bmod[:, 0, :], ALU.add).then_inc(*V.mark("modrow 0"))
            v.wait_ge(*PE.at("modT"))
            mv = B[0][:, :].rearrange("p (i g x) -> p g i x", i=4, g=4)
            for r in range(2):
                cp(shT[:, r, :].rearrange("p (g i) -> p g i", g=2), mv[:, 0:2, :, r])
                i = stt(out=a1T[:, r, :].rearrange("p (g i) -> p g i", g=2), in0=mv[:, 2:4, :, r], scalar=1.0,
                        in1=g1T.rearrange("p (g i) -> p g i", g=2), op0=ALU.add, op1=ALU.mult)
            i.then_inc(*V.mark("mod cols"))
            order()
            cp(c32_late, c32)
            for t in range(NT):
                r = min(t, 1)
                for k in range(KC // 2):
                    i = ts(hT[:, k, t * P:(t + 1) * P], B[1 + 2 * t + k // 4][:, (k % 4) * P:(k % 4 + 1) * P],
                           a1T[:, r, k:k + 1], shT[:, r, k:k + 1], ALU.mult, ALU.add)
                i.then_inc(*V.mark(f"hT {t}"))

            def tok(t):
                b = 1 if t % 2 == 0 else 4
                v.wait_ge(*A.at(f"rs {t}"))
                if t == 0:
                    v.wait_ge(d_small, 80)
                ts(ms[:, 8:10], ss[:, 8:10], EPS, None, ALU.add)
                order()
                rsqrt(rs[:, 8:10], ms[:, 8:10], nw[:, 8:10]).then_inc(*V.mark(f"nr {t}"))
                order()
                v.wait_ge(*A.at(f"kpe {t}"))
                stt(out=ckv[:, t, :], in0=B[b + 1][:, 0:256], scalar=rs[:, 9:10], in1=kvg, op0=ALU.mult,
                    op1=ALU.mult).then_inc(*V.mark(f"ckv {t}"))

            def lora(r):
                v.wait_ge(*PE.at(f"T {r}"))
                if r != "c":
                    for k in range(4):
                        ts(qaT[:, k, r * P:(r + 1) * P], B[7][:, k * P:(k + 1) * P], qgT[:, k:k + 1], None, ALU.mult)
                cp(ckvT[:, :, ROW[r], :], B[0][:, 0:256].rearrange("p (k n) -> p k n", k=2)).then_inc(*V.mark(f"Tev {r}"))

            def k_in(r):
                v.wait_ge(*A.at(f"vv {r}"))
                if r != "c":
                    v.wait_ge(*PE.at("XK %s" % {0: "c", 1: 0, 2: 1}[r]))
                for half in range(2):
                    cp(kh[:, 4 * half:4 * half + 4, 0:NOPE], B[3 + half][:, :].rearrange("p (h n) -> p h n", h=4)[:, :, 0:NOPE])
                if r == "c":
                    v.wait_ge(d_cache, 32)
                else:
                    v.wait_ge(*A.at(f"kpe {r}"))
                cp(kh[:, :, NOPE:QKH], kpe[:, ROW[r], :].unsqueeze(1).to_broadcast([P, H, ROPE])).then_inc(*V.mark(f"kh {r}"))

            def head_norm(x, gain, t, rs_step, step):
                order()
                sqv = sq.rearrange("p (h n) -> p h n", h=H)
                tt(sqv, x, x, ALU.mult)
                order()
                nc.vector.tensor_reduce(ss[:, 0:8], sqv, AX.X, ALU.add)
                order()
                ts(ms[:, 0:8], ss[:, 0:8], 1.0 / QKH, EPS, ALU.mult, ALU.add).then_inc(*V.mark(rs_step))
                v.wait_ge(*A.at(rs_step))
                rsqrt(rs[:, 0:8], ms[:, 0:8], nw[:, 0:8])
                order()
                for h in range(H):
                    i = stt(out=x[:, h, :], in0=x[:, h, :], scalar=rs[:, h:h + 1], in1=gain, op0=ALU.mult, op1=ALU.mult)
                if t in (1, 2):
                    v.wait_ge(d_con2, 16)
                    order()
                    pe4 = x[:, :, NOPE:QKH].rearrange("p h (a b f) -> p h a b f", a=2, b=2)
                    x1, x2 = pe4[:, :, :, 0, :], pe4[:, :, :, 1, :]
                    c0 = (t - 1) * 16
                    cos = con[:, C_RC + c0:C_RC + c0 + 16].rearrange("p (a f) -> p a f", a=2).unsqueeze(1).to_broadcast([P, H, 2, 8])
                    sin = con[:, C_RS + c0:C_RS + c0 + 16].rearrange("p (a f) -> p a f", a=2).unsqueeze(1).to_broadcast([P, H, 2, 8])
                    r1, r2, r3, r4 = (sq[:, 128 * q:128 * q + 128].rearrange("p (h a f) -> p h a f", h=H, a=2) for q in range(4))
                    tt(r1, x1, cos, ALU.mult)
                    tt(r2, x2, sin, ALU.mult)
                    tt(r3, x1, sin, ALU.mult)
                    tt(r4, x2, cos, ALU.mult)
                    order()
                    tt(x1, r1, r2, ALU.subtract)
                    i = tt(x2, r3, r4, ALU.add)
                i.then_inc(*V.mark(step))

            def kn(r):
                head_norm(kh, kng, r, f"rk {r}", f"kn {r}")

            def qn(t):
                v.wait_ge(*A.at(f"qh {t}"))
                head_norm(qh, qng, t, f"rq {t}", f"qn {t}")

            does = {"tok": tok, "T": lora, "kh": k_in, "kn": kn, "qn": qn}
            for what, i in DVE_MIDDLE:
                does[what](i)

            def row_max(u):
                h, t = UNITS[u]
                v.wait_ge(*PE.at(f"S {u}"))
                nc.vector.tensor_reduce(mx[:, u % 2:u % 2 + 1], B[1 + u % 2][:, 0:P if t == 0 else 384], AX.X, ALU.max)
                order()
                ts(mx[:, 2 + u % 2:3 + u % 2], mx[:, u % 2:u % 2 + 1], -SCALE, None, ALU.mult).then_inc(*V.mark(f"mx {u}"))

            def normalise(u):
                h, t = UNITS[u]
                v.wait_ge(*A.at(f"p {u}"))
                nc.vector.reciprocal(ri[:, u % 2:u % 2 + 1], sm[:, u % 2:u % 2 + 1])
                order()
                pr = probs[:, u % 2, 0:P if t == 0 else 384]
                ts(pr, pr, ri[:, u % 2:u % 2 + 1], None, ALU.mult).then_inc(*V.mark(f"pn {u}"))

            def filled(kind, c):
                if kind == "mod":
                    v.wait_ge(*PE.at(f"fill mod {c}"))
                    if c == 2:
                        v.wait_ge(d_mod1, 32)
                    tt(modrow, B[7][:, :], bmod[:, c, :], ALU.add).then_inc(*V.mark(f"modrow {c}"))
                else:
                    v.wait_ge(*A.at(f"ge {c}"))
                    ts(gates[:, c, :], gates[:, c, :], 1.0, None, ALU.add)
                    order()
                    nc.vector.reciprocal(gates[:, c, :], gates[:, c, :])

            def pair_out(pair):
                v.wait_ge(*PE.at(f"PV {6 * pair + 5}"))
                cp(oT[:, pair, :], B[5 + pair % 2][:, 0:NTOK]).then_inc(*V.mark(f"oT {pair}"))

            row_max(0)
            for u in range(len(UNITS)):
                normalise(u)
                if u + 1 < len(UNITS):
                    row_max(u + 1)
                for f in (ends(u - 1) if u else []) + [("g", c) for n, c in enumerate(EARLY_BANK) if u == 4 * n + 3]:
                    filled(*f)
                if u and u % 6 == 0:
                    pair_out(u // 6 - 1)
            pair_out(3)
            for f in ends(len(UNITS) - 1):
                filled(*f)
            for c in range(KC):
                v.wait_ge(*PE.at(f"AF {c}"))
                order()
                tt(uT[:, c, :], B[1 + c % 2][:, 0:NTOK], gates[:, c, :], ALU.mult)
                tt(otmp[:, 0:NTOK], B[3 + c % 2][:, 0:NTOK], gates[:, 8 + c, :], ALU.mult)
                order()
                tt(uT[:, c, :], uT[:, c, :], otmp[:, 0:NTOK], ALU.add).then_inc(*V.mark(f"u {c}"))
            v.wait_ge(d_bc, 9 * 16)
            for r in range(2):
                stt(out=bc[:, 2, r, :], in0=bc[:, 2, r, :], scalar=1.0, in1=g2b, op0=ALU.add, op1=ALU.mult)
            v.wait_ge(d_xre, 32)
            for t in range(NT):
                r = min(t, 1)
                halves = [slice(half * 512, half * 512 + 512) for half in range(2)]
                for half, o in enumerate(halves):
                    v.wait_ge(*PE.at(f"out {t} {half}"))
                    order()
                    tt(otmp[:, o], B[((5, 6), (7, 0), (5, 6))[t][half]][:, :], bc[:, 0, r, o], ALU.mult)
                    order()
                    tt(x_sb[:, t, o], x_sb[:, t, o], otmp[:, o], ALU.add).then_inc(*V.mark(f"x1 {t} {half}"))
                order()
                for o in halves:
                    tt(otmp[:, o], x_sb[:, t, o], bc[:, 2, r, o], ALU.mult)
                v.wait_ge(*A.at(f"rs2 {t}"))
                c = slice(t, t + 1)
                tt(msx[:, c], ssx[:, c], ssy[:, c], ALU.add)
                order()
                ts(msx[:, c], msx[:, c], EPS, None, ALU.add)
                order()
                rsqrt(rsx[:, c], msx[:, c], nwx[:, c])
                order()
                for half, o in enumerate(halves):
                    stt(out=h2[:, t, o], in0=otmp[:, o], scalar=rsx[:, c], in1=bc[:, 1, r, o], op0=ALU.mult,
                        op1=ALU.add).then_inc(*V.mark(f"h2 {t} {half}"))

            def b4(x):
                return x.unsqueeze(2).to_broadcast([P, NT, 4])
            desc = con[:, C_DESC:C_DESC + 4].unsqueeze(1).to_broadcast([P, NT, 4])

            def first_max(out, x, m):
                nc.vector.tensor_reduce(m, x, AX.X, ALU.max)
                order()
                tt(t4, x, b4(m), ALU.is_ge)
                order()
                tt(t4, t4, desc, ALU.mult)
                order()
                nc.vector.tensor_reduce(rr, t4, AX.X, ALU.max)
                order()
                tt(out, t4, b4(rr), ALU.is_equal)
                order()

            nc.vector.memset(MMf[:, 48:64], 0.0)
            v.wait_ge(*PE.at("router"))
            tt(lg, B[7][:, 0:96].rearrange("p (t n) -> p t n", t=NT)[:, :, 0:20], rb.unsqueeze(1).to_broadcast([P, NT, 20]), ALU.add)
            order()
            first_max(ohg, lg[:, :, 0:4], rm)
            tt(prod, lg[:, :, 4:20].rearrange("p t (g e) -> p t g e", g=4), ohg.unsqueeze(3).to_broadcast([P, NT, 4, 4]), ALU.mult)
            order()
            nc.vector.tensor_reduce(esel, prod.rearrange("p t g e -> p t e g"), AX.X, ALU.add)
            order()
            first_max(oh1, esel, rm1)
            stt(out=e2, in0=oh1, scalar=-1e38, in1=esel, op0=ALU.mult, op1=ALU.add)
            order()
            first_max(oh2, e2, rm2)
            for c, oh in enumerate((oh1, oh2)):
                tt(M12[:, c].rearrange("p t (g e) -> p t g e", g=4), ohg.unsqueeze(3).to_broadcast([P, NT, 4, 4]),
                   oh.unsqueeze(2).to_broadcast([P, NT, 4, 4]), ALU.mult)
            order()
            tt(MM, M12[:, 0], M12[:, 1], ALU.add).then_inc(*V.mark("masks"))
            tt(e2, lg[:, :, 0:4], b4(rm), ALU.subtract)
            tt(rd, rm2, rm1, ALU.subtract)
            order()
            v.wait_ge(*PE.at("rank"))
            tt(over, B[0][:, 48:64].unsqueeze(2).to_broadcast([P, NE, 6]), steps6.unsqueeze(1).to_broadcast([P, NE, 6]), ALU.is_gt)
            order()
            nc.vector.tensor_reduce(nt3[:, 0, :], over, AX.X, ALU.add)
            order()
            tt(before, nt3[:, 0, :].unsqueeze(1).to_broadcast([P, NE, NE]), earlier, ALU.mult)
            order()
            nc.vector.tensor_reduce(cum[:, 0, 0:16], before, AX.X, ALU.add)
            order()
            stt(out=slot, in0=cum[:, 0, 0:16].unsqueeze(1).to_broadcast([P, NT, 16]), scalar=float(SLOTS),
                in1=B[0][:, 0:48].rearrange("p (t n) -> p t n", t=NT), op0=ALU.mult, op1=ALU.add)
            order()
            tt(M12, M12, slot.unsqueeze(1).to_broadcast([P, 2, NT, 16]), ALU.mult)
            order()
            nc.vector.tensor_reduce(fsl, M12.rearrange("p c t n -> p t c n"), AX.X, ALU.add)
            order()
            cp(sidx[:, :], fsl.rearrange("p t c -> p (t c)")).then_inc(*V.mark("slots"))
            for t in range(NT):
                ts(tile0[:, t, :], iota, fsl[:, t, 0:1], None, ALU.is_equal)
            order()
            for t in range(NT):
                i = stt(out=tile0[:, t, :], in0=iota, scalar=fsl[:, t, 1:2], in1=tile0[:, t, :], op0=ALU.is_equal, op1=ALU.add)
            i.then_inc(onehot0, 1)
            ts(nt3[:, 1, :], nt3[:, 0, :], -2.0, 0.0, ALU.add, ALU.max)
            ts(nt3[:, 2, :], nt3[:, 0, :], -1.0, None, ALU.add)
            order()
            for w in (1, 2):
                tt(before, nt3[:, w, :].unsqueeze(1).to_broadcast([P, NE, NE]), earlier, ALU.mult)
                order()
                nc.vector.tensor_reduce(cum[:, w, 0:16], before, AX.X, ALU.add)
                order()
            tt(cum[:, :, 16:17], cum[:, :, 15:16], nt3[:, :, 15:16], ALU.add)
            order()
            cp(tab[0:1, 0:16], nt3[0:1, 0, :])
            cp(tab[0:1, 16:67], cum[0:1].rearrange("p v n -> p (v n)")).then_inc(*V.mark("tab"))
            v.wait_ge(*A.at("weights"))
            nc.vector.tensor_reduce(rsum, e2, AX.X, ALU.add)
            ts(rr, rd, 1.0, None, ALU.add)
            order()
            nc.vector.reciprocal(gp, rsum)
            nc.vector.reciprocal(rr, rr)
            order()
            tt(wsl[:, :, 0], rr, gp, ALU.mult)
            order()
            tt(wsl[:, :, 1], wsl[:, :, 0], rd, ALU.mult)

            v.drain().then_inc(t_ye, 1)

            def tile(T1, buf, stored):
                v.wait_ge(t_exp, T1)
                ts(eg, eg, 1.0, None, ALU.add)
                order()
                nc.vector.reciprocal(eg, eg)
                order()
                tt(eg, eg, B[0][:, 0:256], ALU.mult)
                order()
                v.wait_ge(t_u, T1)
                tt(actv, eg, B[4][:, 0:256], ALU.mult).then_inc(t_act, 1)
                v.wait_ge(*stored)
                v.wait_ge(t_y, T1)
                cp(ye[:, buf, :], B[1][:, :]).then_inc(t_ye, 1)

            def expert(e, s, n):
                first, tiles = routed(v, e)
                extra = v.value_load(tab[0:1, bass.ds(50 + e, 1)], min_val=0, max_val=ALL_TILES)
                tile(v.snap(first + 1), s, (d_y0[s], v.snap(n * 32 - 16) if not isinstance(n, int) else n * 32 - 16))
                with v.If(tiles > 1):
                    tile(v.snap(first + 2), ESLOTS, (d_ymore, v.snap(extra * 32 + 16)))
                    with v.If(tiles > 2):
                        with v.Fori(2, tiles) as j:
                            tile(v.snap(first + j + 1), ESLOTS, (d_ymore, v.snap((extra + j) * 32 - 16)))

            with v.Fori(0, NE // ESLOTS) as g:
                for s in range(ESLOTS):
                    expert(g * ESLOTS + s, s, g + 1)
            expert(NE - 1, (NE - 1) % ESLOTS, NE // ESLOTS + 1)
            for s in range(ESLOTS):
                v.wait_ge(d_y0[s], 16 + 32 * len(range(s, NE, ESLOTS)))
            extra = v.value_load(tab[0:1, 66:67], min_val=0, max_val=ALL_TILES)
            stored = v.snap(extra * 32 + 16)
            v.wait_ge(d_ymore, stored)
            cp(nwx, msx).then_inc(all_stored, 1)
            v.wait_ge(d_g5, 32)
            for t in range(NT):
                y0, y1 = ybuf[:, t, 0, :], ybuf[:, t, 1, :]
                v.wait_ge(weighted, 2 * t + 1)
                y0, y1 = y0[:, 0:CUT], y1[:, 0:CUT]
                stt(out=y0, in0=y1, scalar=wsl[:, t, 1:2], in1=y0, op0=ALU.mult, op1=ALU.add)
                order()
                tt(y0, y0, g5[:, min(t, 1), 0:CUT], ALU.mult)
                order()
                tt(x_sb[:, t, 0:CUT], x_sb[:, t, 0:CUT], y0, ALU.add).then_inc(fin, 1)

        @block.scalar
        def _(act):
            av = nc.scalar.activation

            def rsqrt0(out, mean, bias=0.0):
                av(out, mean, ACT.Ln, bias=bias)
                act.drain()
                return av(out, out, ACT.Exp, scale=-0.5)

            nc.scalar.preload_act_table_set("natural_log_exp_and_others")
            act.wait_ge(d_vec, 64)
            av(erow[0:16, :], vrow[0:16, :], ACT.Exp, scale=-1.0).then_inc(*A.mark("exp c"))
            act.wait_ge(zero_done, 3)
            for t in range(NT):
                act.wait_ge(d_x[t], 16)
                av(sqa, x_sb[:, t, :], ACT.Square, scale=D ** -0.5, accum_out=ssx[:, t:t + 1])
                act.drain()
            rsqrt0(rsx, ssx, epsc).then_inc(*A.mark("rsx"))
            act.wait_ge(*V.at("mod cols"))
            for t in range(NT):
                act.wait_ge(*PE.at(f"xT{t}"))
                r = min(t, 1)
                for k in range(KC // 2, KC):
                    i = av(hT[:, k, t * P:(t + 1) * P], B[1 + 2 * t + k // 4][:, (k % 4) * P:(k % 4 + 1) * P], ACT.Identity,
                           scale=a1T[:, r, k:k + 1], bias=shT[:, r, k:k + 1])
                i.then_inc(*A.mark(f"hT {t}"))
            act.wait_ge(zero_done, 4)
            parts = SLOT_ROWS // P
            cuts = [parts * q // 4 for q in range(5)]
            for q, done in enumerate(d_y0 + [d_ymore]):
                act.dma_start(slots[cuts[q] * P:cuts[q + 1] * P, :].rearrange("(c p) n -> p c n", p=P),
                              yTt[:, 0:D].unsqueeze(1).to_broadcast([P, cuts[q + 1] - cuts[q], D])).then_inc(done, 16)

            def tok(t):
                b = 1 if t % 2 == 0 else 4
                act.wait_ge(*PE.at(f"tok {t}"))
                if t:
                    act.wait_ge(*V.at(f"ckv {t - 1}"))
                av(sqa[:, 0:512], B[b][:, :], ACT.Square, scale=Q_LORA ** -0.5, accum_out=ss[:, 8:9])
                av(sqa[:, 512:768], B[b + 1][:, 0:256], ACT.Square, scale=KV_LORA ** -0.5, accum_out=ss[:, 9:10])
                act.drain()
                rsqrt0(rs[:, 8:10], ss[:, 8:10], epsc).then_inc(*A.mark(f"rs {t}"))
                av(kpe[:, t, :], B[b + 1][:, 256:288], ACT.Copy).then_inc(*A.mark(f"kpe {t}"))
                av(fn[:, t, :], B[7 if t == 0 else b + 2][:, :], ACT.Copy).then_inc(*A.mark(f"fn {t}"))
                act.wait_ge(*V.at(f"nr {t}"))
                if t == 2:
                    act.wait_ge(*PE.at("T 0"))
                av(qan[:, t % 2, :], B[b][:, :], ACT.Copy, scale=rs[:, 8:9]).then_inc(*A.mark(f"qan {t}"))

            def values(r):
                act.wait_ge(*PE.at(f"KV {r}"))
                for half in range(2):
                    i = av(vv[:, KSLOT[r], half * 256:(half + 1) * 256].rearrange("p (h n) -> p h n", h=4),
                           B[3 + half][:, :].rearrange("p (h n) -> p h n", h=4)[:, :, NOPE:128], ACT.Copy)
                i.then_inc(*A.mark(f"vv {r}"))

            def rstart(name):
                act.wait_ge(*V.at(name))
                rsqrt0(rs[:, 0:8], ms[:, 0:8]).then_inc(*A.mark(name))

            def q_in(t):
                act.wait_ge(*PE.at(f"QB {t}"))
                if t:
                    act.wait_ge(*PE.at(f"XQ {t - 1}"))
                for half in range(2):
                    i = av(qh[:, 4 * half:4 * half + 4, :], B[1 + half][:, 0:384].rearrange("p (h n) -> p h n", h=4), ACT.Copy)
                i.then_inc(*A.mark(f"qh {t}"))

            def heads_out(dst, lo, pstep, step):
                act.wait_ge(*PE.at(pstep))
                for half in range(2):
                    i = av(dst[0:QKH, 4 * half:4 * half + 4, lo:lo + P], B[5 + half][0:QKH, :].rearrange("p (h n) -> p h n", h=4), ACT.Copy)
                i.then_inc(*A.mark(step))

            def fourier_seq(g):
                bl, bx = (B[5], B[6]) if g < 2 else (B[7], B[0])
                act.wait_ge(*PE.at(f"FA {g}"))
                av(fA[:, g, 0:512], bl[:, :], ACT.Copy)
                av(fA[:, g, 512:768], bx[:, 0:256], ACT.Copy).then_inc(*A.mark(f"fA {g}"))

            def fourier_ch(part):
                act.wait_ge(*PE.at(f"FB {part}"))
                if part == 0:
                    for done in d_y0 + [d_ymore]:
                        act.wait_ge(done, 16)
                    for pair in range(2):
                        i = av(yT[:, 2 * pair:2 * pair + 2, P:NTOK], (B[7], B[0])[pair][:, :].rearrange("p (g n) -> p g n", g=2), ACT.Copy)
                else:
                    i = av(yT[:, :, 0:P], B[7][:, :].rearrange("p (g n) -> p g n", g=4), ACT.Copy)
                i.then_inc(*A.mark(f"yT {part}"))

            def gate_exp(c):
                act.wait_ge(*PE.at(f"fill g {c}"))
                av(gates[:, c, :], B[EARLY_BANK.get(c, 0)][:, 0:NTOK], ACT.Exp,
                   scale=-1.0).then_inc(*A.mark(f"ge {c}"))

            does = {"ge": gate_exp, "tok": tok, "vv": values, "rk": lambda r: rstart(f"rk {r}"), "rq": lambda t: rstart(f"rq {t}"), "qh": q_in,
                    "kT": lambda r: heads_out(kT, KSLOT[r] * P, f"XK {r}", f"kT {r}"),
                    "qT": lambda t: heads_out(qT, t * P, f"XQ {t}", f"qT {t}"), "fA": fourier_seq, "yT": fourier_ch}
            for what, i in ACT_MIDDLE:
                does[what](i)

            def exps(u):
                h, t = UNITS[u]
                act.wait_ge(*V.at(f"mx {u}"))
                if u >= 2:
                    act.wait_ge(*PE.at(f"PT {u - 2}"))
                n = P if t == 0 else 384
                av(probs[:, u % 2, 0:n], B[1 + u % 2][:, 0:n], ACT.Exp, scale=SCALE, bias=mx[:, 2 + u % 2:3 + u % 2],
                   accum_out=sm[:, u % 2:u % 2 + 1])
                act.drain().then_inc(*A.mark(f"p {u}"))

            exps(0)
            for u in range(len(UNITS)):
                if u + 1 < len(UNITS):
                    exps(u + 1)
                for k, c in ends(u):
                    if k == "g":
                        gate_exp(c)
                act.wait_ge(*PE.at(f"PT {u}"))
                if u >= 2:
                    act.wait_ge(*PE.at(f"PV {u - 2}"))
                n = P if UNITS[u][1] == 0 else 384
                av(pT[:, u % 2, 0:n], B[3 + u % 2][:, 0:n], ACT.Copy).then_inc(*A.mark(f"pT {u}"))

            def h2T_out(t):
                act.wait_ge(*PE.at(f"h2T {t}"))
                b = 1 if t % 2 == 0 else 3
                for half in range(2):
                    i = av(h2T[:, 4 * half:4 * half + 4, t * P:(t + 1) * P], B[b + half][:, :].rearrange("p (k n) -> p k n", k=4), ACT.Copy)
                i.then_inc(*A.mark(f"h2T {t}"))

            for t in range(NT):
                for half, sums in enumerate((ssx, ssy)):
                    act.wait_ge(*V.at(f"x1 {t} {half}"))
                    av(junk[:, half * 512:half * 512 + 512], x_sb[:, t, half * 512:half * 512 + 512], ACT.Square, scale=D ** -0.5,
                       accum_out=sums[:, t:t + 1])
                act.drain()
                av(srt[:, t:t + 1], ssx[:, t:t + 1], ACT.Identity, bias=ssy[:, t:t + 1])
                act.drain()
                rsqrt0(rsx[:, t:t + 1], srt[:, t:t + 1], epsc).then_inc(*A.mark(f"rs2 {t}"))
                if t:
                    h2T_out(t - 1)
            h2T_out(2)
            for t in (1, 2):
                act.wait_ge(*PE.at(f"logT {t}"))
                c0, c1 = (0, 2 * P) if t == 1 else (2 * P, 3 * P)
                av(logT[0:20, c0:c1], B[0 if t == 1 else 5][0:20, 0:c1 - c0], ACT.Copy).then_inc(*A.mark(f"logT {t}"))
            act.wait_ge(gathered0, 1)
            av(xg[:, 0, 0, :], B[1][:, :], ACT.Copy).then_inc(rows0, 1)
            act.wait_ge(*V.at("tab"))
            av(e2, e2, ACT.Exp)
            av(rd, rd, ACT.Exp).then_inc(*A.mark("weights"))

            act.wait_ge(*V.at("tab"))

            def rows_T(T1):
                act.wait_ge(t_xeTp, T1)
                av(xeT, B[2][:, :].rearrange("p (i g s) -> p i g s", i=4, g=2), ACT.Copy).then_inc(t_xeTs, 1)

            def tile(T1, between):
                act.wait_ge(t_g, T1)
                av(eg, B[0][:, 0:256], ACT.Exp, scale=-1.0).then_inc(t_exp, 1)
                between()
                act.wait_ge(t_aTp, T1)
                av(actT, B[3][:, 0:256].rearrange("p (j g s) -> p j g s", j=2, g=2), ACT.Copy).then_inc(t_aTs, 1)

            def expert(e, s, n, last=False):
                first, tiles = routed(act, e)

                def after_first():
                    if last:
                        with act.If(tiles > 1):
                            rows_T(act.snap(first + 2))
                    else:
                        rows_T(act.snap(first + 2))

                def after_second():
                    if not last:
                        with act.If(tiles < 3):
                            rows_T(act.snap(first + 3))

                tile(act.snap(first + 1), after_first)
                with act.If(tiles > 1):
                    tile(act.snap(first + 2), after_second)
                    with act.If(tiles > 2):
                        with act.Fori(2, tiles) as j:
                            rows_T(act.snap(first + j + 1))
                            tile(act.snap(first + j + 1), lambda: None)
                        if not last:
                            rows_T(act.snap(first + tiles + 1))

            rows_T(1)
            with act.Fori(0, NE // ESLOTS) as g:
                for s in range(ESLOTS):
                    expert(g * ESLOTS + s, s, g + 1)
            expert(NE - 1, (NE - 1) % ESLOTS, NE // ESLOTS + 1, last=True)
            for t in range(NT):
                act.wait_ge(d_gath[t], 32)
                av(ybuf[:, t, 0, :], ybuf[:, t, 0, :], ACT.Copy, scale=wsl[:, t, 0:1]).then_inc(weighted, 1)
                av(ybuf[:, t, 1, CUT:D], ybuf[:, t, 1, CUT:D], ACT.Copy, scale=wsl[:, t, 1:2]).then_inc(weighted, 1)


INS = ["x_prompt", "x_sample", "cache_ckv", "cache_kpe", "c", "c_ctx", "w_mod", "b_mod", "norm1_g", "w_in", "q_a_norm_g", "w_q_b",
       "kv_a_norm_g", "w_kv_b", "q_norm_g", "k_norm_g", "w_attn_o", "w_fnet", "w_out", "norm2_g", "w_router_group",
       "b_router_group", "w_router_expert", "b_router_expert", "w_exp_gate", "w_exp_up", "w_exp_down"]
OUTS = [("y_prompt", (1, P, D)), ("y_sample", (1, 2 * P, D)), ("new_ckv", (1, 1, P, KV_LORA)), ("new_kpe", (1, 1, P, ROPE))]


def kernel(**inputs):
    import concourse.bacc as bacc
    from concourse.bass_utils import run_bass_kernel_spmd

    nc = bacc.Bacc("TRN2", target_bir_lowering=False, num_devices=1)
    arrays, aps = {}, {}
    for name in INS:
        x = np.ascontiguousarray(inputs[name])
        arrays[f"in_{name}"] = x
        aps[name] = nc.dram_tensor(f"in_{name}", x.shape, mybir.dt.from_np(x.dtype), kind="ExternalInput").ap()
    arrays["in_const_table"] = constants()
    aps["const_table"] = nc.dram_tensor("in_const_table", (P, NCON), F32, kind="ExternalInput").ap()
    for name, shape in OUTS:
        aps[name] = nc.dram_tensor(f"out_{name}", shape, F32, kind="ExternalOutput").ap()
    program(nc, aps)
    r = run_bass_kernel_spmd(nc, [arrays], core_ids=[0])
    return tuple(r.results[0][f"out_{name}"] for name, _ in OUTS)
```
